# Optimizing a Trainium2 kernel written in Bass

```python
import math
import jax, jax.numpy as jnp
from jax import lax
import numpy as np

D_MODEL = 1024
BATCH = 1
SEQ = 256
DEPTH = 1

CHUNK = 64
CONV_CH = D_MODEL // 2
CONV_WIDTH = 31
RET_HEADS = 8
RET_DV = (D_MODEL // 2) // RET_HEADS
RET_DK = RET_DV // 2
D_MIX = CONV_CH + RET_HEADS * RET_DV
N_MEM = 256
XATTN_HEADS = 4
XATTN_HEAD_DIM = D_MODEL // XATTN_HEADS
D_FF = 4 * D_MODEL
ROPE_BASE = 10000.0
EPS = 1e-6

IN_SPLITS = (CONV_CH, CONV_CH, RET_HEADS * RET_DK, RET_HEADS * RET_DK, RET_HEADS * RET_DV, RET_HEADS * RET_DV)
D_IN = sum(IN_SPLITS)


def rmsnorm(x, w):
    xf = x.astype(jnp.float32)
    y = xf * lax.rsqrt(jnp.mean(xf * xf, axis=-1, keepdims=True) + EPS)
    return (y * w.astype(jnp.float32)).astype(x.dtype)

def apply_rotary(t, positions):
    half = t.shape[-1] // 2
    inv_freq = ROPE_BASE ** (-jnp.arange(half, dtype=jnp.float32) / half)
    ang = positions.astype(jnp.float32)[..., None] * inv_freq
    cos = jnp.cos(ang)[:, :, None, :]
    sin = jnp.sin(ang)[:, :, None, :]
    t1, t2 = t[..., :half].astype(jnp.float32), t[..., half:].astype(jnp.float32)
    return jnp.concatenate([t1 * cos - t2 * sin, t1 * sin + t2 * cos], axis=-1)

def conv_module(a, b, conv_w, conv_b, ln_w, ln_b):
    u = a * jax.nn.sigmoid(b)
    y = lax.conv_general_dilated(
        u, conv_w[:, None, :], window_strides=(1,), padding=[(CONV_WIDTH - 1, 0)],
        dimension_numbers=("NWC", "WIO", "NWC"), feature_group_count=CONV_CH) + conv_b
    yf = y.astype(jnp.float32)
    mu = jnp.mean(yf, axis=-1, keepdims=True)
    var = jnp.mean(jnp.square(yf - mu), axis=-1, keepdims=True)
    yn = (yf - mu) * lax.rsqrt(var + EPS) * ln_w + ln_b
    return jax.nn.silu(yn)

def retention(q, k, v, positions):
    B, S = q.shape[:2]
    N = S // CHUNK
    q = apply_rotary(q.reshape(B, S, RET_HEADS, RET_DK), positions) * (RET_DK ** -0.5)
    k = apply_rotary(k.reshape(B, S, RET_HEADS, RET_DK), positions)
    v = v.reshape(B, S, RET_HEADS, RET_DV).astype(jnp.float32)
    qc = q.reshape(B, N, CHUNK, RET_HEADS, RET_DK)
    kc = k.reshape(B, N, CHUNK, RET_HEADS, RET_DK)
    vc = v.reshape(B, N, CHUNK, RET_HEADS, RET_DV)

    log_g = jnp.log1p(-jnp.exp2(-5.0 - jnp.arange(RET_HEADS, dtype=jnp.float32)))
    idx = jnp.arange(CHUNK, dtype=jnp.float32)
    dist = jnp.abs(idx[:, None] - idx[None, :])
    decay_in = jnp.exp(log_g[:, None, None] * dist)
    zeta = jnp.exp(log_g[:, None] * (CHUNK - 1 - idx)[None, :])
    xi = jnp.exp(log_g[:, None] * (idx + 1.0)[None, :])
    g_chunk = jnp.exp(log_g * CHUNK)

    scores = jnp.einsum('bnihd,bnjhd->bnhij', qc, kc) * decay_in
    y_in = jnp.einsum('bnhij,bnjhe->bnihe', scores, vc)

    kv = jnp.einsum('bnjhd,bnjhe,hj->nbhde', kc, vc, zeta)

    def step(state, kv_n):
        return g_chunk[None, :, None, None] * state + kv_n, state

    init = jnp.zeros((B, RET_HEADS, RET_DK, RET_DV), jnp.float32)
    _, state_prev = lax.scan(step, init, kv)
    y_x = jnp.einsum('bnihd,nbhde,hi->bnihe', qc, state_prev, xi)
    return (y_in + y_x).reshape(B, S, RET_HEADS, RET_DV)

def head_group_mixer(h, positions, w_in, conv_w, conv_b, conv_ln_w, conv_ln_b, ret_gn_w, w_out):
    B, S, _ = h.shape
    proj = h @ w_in
    cuts = list(np.cumsum(IN_SPLITS)[:-1])
    ca, cb, rq, rk, rv, rg = jnp.split(proj, cuts, axis=-1)
    y_conv = conv_module(ca, cb, conv_w, conv_b, conv_ln_w, conv_ln_b)
    y = retention(rq, rk, rv, positions)
    mu = jnp.mean(y, axis=-1, keepdims=True)
    var = jnp.mean(jnp.square(y - mu), axis=-1, keepdims=True)
    y = (y - mu) * lax.rsqrt(var + EPS) * ret_gn_w.reshape(RET_HEADS, RET_DV)
    y_ret = jax.nn.silu(rg.astype(jnp.float32)) * y.reshape(B, S, RET_HEADS * RET_DV)
    merged = jnp.concatenate([y_conv, y_ret], axis=-1).astype(h.dtype)
    return merged @ w_out

def memory_cross_attention(h, mem_n, xq_w, xkv_w, xo_w):
    B, S, _ = h.shape
    q = (h @ xq_w).reshape(B, S, XATTN_HEADS, XATTN_HEAD_DIM)
    kv = (mem_n @ xkv_w).reshape(B, N_MEM, 2, XATTN_HEADS, XATTN_HEAD_DIM)
    k, v = kv[:, :, 0], kv[:, :, 1]
    s = jnp.einsum('bshd,bmhd->bhsm', q.astype(jnp.float32), k.astype(jnp.float32)) * (XATTN_HEAD_DIM ** -0.5)
    p = jax.nn.softmax(s, axis=-1)
    o = jnp.einsum('bhsm,bmhd->bshd', p, v.astype(jnp.float32)).reshape(B, S, D_MODEL)
    return o.astype(h.dtype) @ xo_w

def sq_relu_mlp(h, up_w, down_w):
    return jnp.square(jax.nn.relu(h @ up_w)) @ down_w

def first_inputs(seed: int = 0) -> dict:
    key = jax.random.key(seed)
    ks = jax.random.split(key, 24)
    f32 = jnp.float32

    def w(k, shape, fan_in):
        return jax.random.normal(k, shape, f32) * (fan_in ** -0.5)

    def gain(k, n):
        return 1.0 + 0.02 * jax.random.normal(k, (n,), f32)

    x = jax.random.normal(ks[0], (BATCH, SEQ, D_MODEL), f32)
    mem = jax.random.normal(ks[1], (BATCH, N_MEM, D_MODEL), f32)
    start = jax.random.randint(ks[2], (BATCH, 1), 0, 1000, dtype=jnp.int32) * CHUNK
    positions = (start + jnp.arange(SEQ, dtype=jnp.int32)[None, :]).astype(jnp.int32)
    return {
        "x": x,
        "mem": mem,
        "positions": positions,
        "norm_mix_w": gain(ks[3], D_MODEL),
        "w_in": w(ks[4], (D_MODEL, D_IN), D_MODEL),
        "conv_w": w(ks[5], (CONV_WIDTH, CONV_CH), CONV_WIDTH),
        "conv_b": 0.02 * jax.random.normal(ks[6], (CONV_CH,), f32),
        "conv_ln_w": gain(ks[7], CONV_CH),
        "conv_ln_b": 0.02 * jax.random.normal(ks[8], (CONV_CH,), f32),
        "ret_gn_w": gain(ks[9], RET_HEADS * RET_DV),
        "w_out": w(ks[10], (D_MIX, D_MODEL), D_MIX),
        "norm_xattn_w": gain(ks[11], D_MODEL),
        "norm_mem_w": gain(ks[12], D_MODEL),
        "xq_w": w(ks[13], (D_MODEL, D_MODEL), D_MODEL),
        "xkv_w": w(ks[14], (D_MODEL, 2 * D_MODEL), D_MODEL),
        "xo_w": w(ks[15], (D_MODEL, D_MODEL), D_MODEL),
        "norm_mlp_w": gain(ks[16], D_MODEL),
        "mlp_up_w": w(ks[17], (D_MODEL, D_FF), D_MODEL),
        "mlp_down_w": w(ks[18], (D_FF, D_MODEL), D_FF),
        "norm_f_w": gain(ks[19], D_MODEL),
    }

def first_block(x, mem, positions, norm_mix_w, w_in, conv_w, conv_b, conv_ln_w, conv_ln_b, ret_gn_w, w_out,
              norm_xattn_w, norm_mem_w, xq_w, xkv_w, xo_w, norm_mlp_w, mlp_up_w, mlp_down_w, norm_f_w):
    h = x
    mem_n = rmsnorm(mem, norm_mem_w)
    for _ in range(DEPTH):
        h = h + head_group_mixer(rmsnorm(h, norm_mix_w), positions, w_in, conv_w, conv_b,
                                 conv_ln_w, conv_ln_b, ret_gn_w, w_out)
        h = h + memory_cross_attention(rmsnorm(h, norm_xattn_w), mem_n, xq_w, xkv_w, xo_w)
        h = h + sq_relu_mlp(rmsnorm(h, norm_mlp_w), mlp_up_w, mlp_down_w)
    return rmsnorm(h, norm_f_w).astype(x.dtype)


BRANCH_WIDTH = D_MODEL // 2
N_BRANCHES = 3
SB_HEADS = 8
SB_HEAD_DIM = BRANCH_WIDTH // SB_HEADS
SB_BLOCK = 128
SGU_LEN = 128
SGU_GROUPS = 4
SGU_GROUP_DIM = BRANCH_WIDTH // SGU_GROUPS
CONV_WIDTH_2 = 3
MEM_TOKENS = 256
XA_HEADS = 4
XA_HEAD_DIM = D_MODEL // XA_HEADS
FFN_HIDDEN = ((8 * D_MODEL // 3 + 255) // 256) * 256

W_QKV = 3 * BRANCH_WIDTH
W_SGU = 2 * BRANCH_WIDTH
W_CONV = 3 * BRANCH_WIDTH
W_GATES = N_BRANCHES * D_MODEL
IN_COLS = W_QKV + W_SGU + W_CONV + W_GATES
SPLIT_IDX = [BRANCH_WIDTH, 2 * BRANCH_WIDTH, W_QKV,
             W_QKV + W_SGU,
             W_QKV + W_SGU + BRANCH_WIDTH, W_QKV + W_SGU + 2 * BRANCH_WIDTH,
             W_QKV + W_SGU + W_CONV]


def rms_norm(x, g, eps=1e-6):
    xf = x.astype(jnp.float32)
    y = xf * lax.rsqrt(jnp.mean(xf * xf, axis=-1, keepdims=True) + eps)
    return (y * g.astype(jnp.float32)).astype(x.dtype)

def layer_norm(x, g, b, eps=1e-5):
    xf = x.astype(jnp.float32)
    mu = jnp.mean(xf, axis=-1, keepdims=True)
    xc = xf - mu
    y = xc * lax.rsqrt(jnp.mean(xc * xc, axis=-1, keepdims=True) + eps)
    return (y * g.astype(jnp.float32) + b.astype(jnp.float32)).astype(x.dtype)

def stick_breaking_attention(q, k, v):
    seq = q.shape[2]
    scale = SB_HEAD_DIM ** -0.5
    outs = []
    for i in range(seq // SB_BLOCK):
        q0 = i * SB_BLOCK
        kend = q0 + SB_BLOCK
        qb = q[:, :, q0:kend].astype(jnp.float32)
        kb = k[:, :, :kend].astype(jnp.float32)
        z = jnp.einsum("bhqd,bhkd->bhqk", qb, kb) * scale
        t_pos = q0 + jnp.arange(SB_BLOCK)[:, None]
        s_pos = jnp.arange(kend)[None, :]
        valid = s_pos < t_pos
        log_1m = jnp.where(valid, jax.nn.log_sigmoid(-z), 0.0)
        log_a = jax.nn.log_sigmoid(z) + lax.cumsum(log_1m, axis=3, reverse=True) - log_1m
        a = jnp.where(valid, jnp.exp(log_a), 0.0)
        outs.append(jnp.einsum("bhqk,bhkd->bhqd", a.astype(v.dtype), v[:, :, :kend]))
    return jnp.concatenate(outs, axis=2)

def spatial_gating(z, ln_g, ln_b, w_s, b_s):
    bsz, seq, _ = z.shape
    u, v = jnp.split(z, 2, axis=-1)
    v = layer_norm(v, ln_g, ln_b)
    v = v.reshape(bsz, seq // SGU_LEN, SGU_LEN, SGU_GROUPS, SGU_GROUP_DIM)
    pos = jnp.arange(SGU_LEN)
    allowed = (pos[:, None] // CHUNK) >= (pos[None, :] // CHUNK)
    w = jnp.where(allowed[None], w_s, 0.0).astype(v.dtype)
    vm = jnp.einsum("gts,bnsgc->bntgc", w, v) + b_s.T[None, None, :, :, None].astype(v.dtype)
    return u * vm.reshape(bsz, seq, BRANCH_WIDTH)

def gated_short_conv(gate_b, gate_c, xin, conv_w):
    y = gate_c * xin
    ch = y.shape[-1]
    conv = lax.conv_general_dilated(
        y, conv_w[:, None, :].astype(y.dtype), window_strides=(1,),
        padding=((CONV_WIDTH_2 - 1, 0),), dimension_numbers=("NWC", "WIO", "NWC"),
        feature_group_count=ch)
    return gate_b * conv

def hybrid_mixer(h, w_in, sgu_ln_g, sgu_ln_b, w_spatial, b_spatial, conv_w, w_branch, w_out):
    bsz, seq, _ = h.shape
    p = h @ w_in
    q, k, v, z, cb, cc, cx, gates = jnp.split(p, SPLIT_IDX, axis=-1)

    def heads(t):
        return t.reshape(bsz, seq, SB_HEADS, SB_HEAD_DIM).transpose(0, 2, 1, 3)

    ya = stick_breaking_attention(heads(q), heads(k), heads(v))
    ya = ya.transpose(0, 2, 1, 3).reshape(bsz, seq, BRANCH_WIDTH)
    yb = spatial_gating(jax.nn.gelu(z, approximate=False), sgu_ln_g, sgu_ln_b, w_spatial, b_spatial)
    yc = gated_short_conv(cb, cc, cx, conv_w)

    br = jnp.stack([ya, yb, yc], axis=2)
    br_d = jnp.einsum("bsnc,ncd->bsnd", br, w_branch)
    g = jax.nn.sigmoid(gates.reshape(bsz, seq, N_BRANCHES, D_MODEL))
    merged = jnp.sum(g * br_d, axis=2)
    return merged @ w_out

def memory_cross_attention_2(h, mem, mem_g, wq, wk, wv, wo):
    bsz, seq, _ = h.shape
    m = rms_norm(mem, mem_g)
    q = (h @ wq).reshape(bsz, seq, XA_HEADS, XA_HEAD_DIM)
    k = (m @ wk).reshape(bsz, MEM_TOKENS, XA_HEADS, XA_HEAD_DIM)
    v = (m @ wv).reshape(bsz, MEM_TOKENS, XA_HEADS, XA_HEAD_DIM)
    s = jnp.einsum("bqhd,bkhd->bhqk", q.astype(jnp.float32), k.astype(jnp.float32)) * (XA_HEAD_DIM ** -0.5)
    pr = jax.nn.softmax(s, axis=-1)
    o = jnp.einsum("bhqk,bkhd->bqhd", pr.astype(v.dtype), v).reshape(bsz, seq, D_MODEL)
    return o @ wo

def swiglu(h, w_gate, w_up, w_down):
    return (jax.nn.silu(h @ w_gate) * (h @ w_up)) @ w_down

def second_inputs(seed: int = 0) -> dict:
    key = jax.random.key(seed)
    ks = jax.random.split(key, 24)
    f32 = jnp.float32

    def nrm(k, shape, fan_in):
        return jax.random.normal(k, shape, f32) * (fan_in ** -0.5)

    def gain(k, shape):
        return 1.0 + 0.02 * jax.random.normal(k, shape, f32)

    L, D, W = DEPTH, D_MODEL, BRANCH_WIDTH
    return {
        "x": jax.random.normal(ks[0], (BATCH, SEQ, D), f32),
        "mem": jax.random.normal(ks[1], (BATCH, MEM_TOKENS, D), f32),
        "norm_mix_g": gain(ks[2], (L, D)),
        "w_in": nrm(ks[3], (L, D, IN_COLS), D),
        "sgu_ln_g": gain(ks[4], (L, W)),
        "sgu_ln_b": 0.02 * jax.random.normal(ks[5], (L, W), f32),
        "w_spatial": nrm(ks[6], (L, SGU_GROUPS, SGU_LEN, SGU_LEN), SGU_LEN),
        "b_spatial": gain(ks[7], (L, SGU_GROUPS, SGU_LEN)),
        "conv_w": nrm(ks[8], (L, CONV_WIDTH_2, W), CONV_WIDTH_2),
        "w_branch": nrm(ks[9], (L, N_BRANCHES, W, D), W),
        "w_out": nrm(ks[10], (L, D, D), D),
        "norm_xa_g": gain(ks[11], (L, D)),
        "mem_norm_g": gain(ks[12], (L, D)),
        "w_q_xa": nrm(ks[13], (L, D, D), D),
        "w_k_xa": nrm(ks[14], (L, D, D), D),
        "w_v_xa": nrm(ks[15], (L, D, D), D),
        "w_o_xa": nrm(ks[16], (L, D, D), D),
        "norm_ffn_g": gain(ks[17], (L, D)),
        "w_gate_ffn": nrm(ks[18], (L, D, FFN_HIDDEN), D),
        "w_up_ffn": nrm(ks[19], (L, D, FFN_HIDDEN), D),
        "w_down_ffn": nrm(ks[20], (L, FFN_HIDDEN, D), FFN_HIDDEN),
        "final_g": gain(ks[21], (D,)),
    }

def second_block(x, mem, norm_mix_g, w_in, sgu_ln_g, sgu_ln_b, w_spatial, b_spatial, conv_w,
              w_branch, w_out, norm_xa_g, mem_norm_g, w_q_xa, w_k_xa, w_v_xa, w_o_xa,
              norm_ffn_g, w_gate_ffn, w_up_ffn, w_down_ffn, final_g):
    for l in range(DEPTH):
        x = x + hybrid_mixer(rms_norm(x, norm_mix_g[l]), w_in[l], sgu_ln_g[l], sgu_ln_b[l],
                             w_spatial[l], b_spatial[l], conv_w[l], w_branch[l], w_out[l])
        x = x + memory_cross_attention_2(rms_norm(x, norm_xa_g[l]), mem, mem_norm_g[l],
                                       w_q_xa[l], w_k_xa[l], w_v_xa[l], w_o_xa[l])
        x = x + swiglu(rms_norm(x, norm_ffn_g[l]), w_gate_ffn[l], w_up_ffn[l], w_down_ffn[l])
    return rms_norm(x, final_g)


def setup_inputs(seed=0):
    out = dict(first_inputs(seed))
    for name, value in second_inputs(seed + 1).items():
        if name != "x":
            out[name + "_2"] = value
    return out


def reference(
    x, mem, positions, norm_mix_w, w_in, conv_w, conv_b, conv_ln_w, conv_ln_b, ret_gn_w, w_out,
    norm_xattn_w, norm_mem_w, xq_w, xkv_w, xo_w, norm_mlp_w, mlp_up_w, mlp_down_w, norm_f_w,
    mem_2, norm_mix_g_2, w_in_2, sgu_ln_g_2, sgu_ln_b_2, w_spatial_2, b_spatial_2, conv_w_2,
    w_branch_2, w_out_2, norm_xa_g_2, mem_norm_g_2, w_q_xa_2, w_k_xa_2, w_v_xa_2, w_o_xa_2,
    norm_ffn_g_2, w_gate_ffn_2, w_up_ffn_2, w_down_ffn_2, final_g_2,
):
    x = first_block(
        x, mem, positions, norm_mix_w, w_in, conv_w, conv_b, conv_ln_w, conv_ln_b, ret_gn_w,
        w_out, norm_xattn_w, norm_mem_w, xq_w, xkv_w, xo_w, norm_mlp_w, mlp_up_w, mlp_down_w,
        norm_f_w,
    )
    return second_block(
        x, mem_2, norm_mix_g_2, w_in_2, sgu_ln_g_2, sgu_ln_b_2, w_spatial_2, b_spatial_2,
        conv_w_2, w_branch_2, w_out_2, norm_xa_g_2, mem_norm_g_2, w_q_xa_2, w_k_xa_2, w_v_xa_2,
        w_o_xa_2, norm_ffn_g_2, w_gate_ffn_2, w_up_ffn_2, w_down_ffn_2, final_g_2,
    )


_drawn_inputs = setup_inputs


def setup_inputs(seed=0):
    import zlib

    import numpy as np

    out = dict(_drawn_inputs(seed))
    spreads = {}
    factors = {'conv_ln_w': 4.416,
     'conv_ln_b': 5.527,
     'ret_gn_w': 5.472,
     'norm_xattn_w': 8.0,
     'norm_mem_w': 8.0,
     'norm_mix_g_2': 2.737,
     'sgu_ln_g_2': 8.0,
     'sgu_ln_b_2': 8.0,
     'b_spatial_2': 8.0,
     'norm_xa_g_2': 8.0,
     'mem_norm_g_2': 8.0,
     'norm_ffn_g_2': 14.987,
     'final_g_2': 8.046,
     'norm_mlp_w': 3.385}
    for name, (base, spread) in spreads.items():
        noise = np.random.default_rng([zlib.crc32(name.encode()), seed]).standard_normal(out[name].shape)
        drawn = base * np.exp(spread * noise) if base else spread * noise
        out[name] = __import__('jax').numpy.asarray(drawn.astype(out[name].dtype))
    for name, factor in factors.items():
        out[name] = (out[name] * factor).astype(out[name].dtype)
    return out
```

```python
from contextlib import ExitStack

import numpy as np

import concourse.bass as bass
from concourse import mybir

F32 = mybir.dt.float32
F32R = mybir.dt.float32r
I32 = mybir.dt.int32
ACT = mybir.ActivationFunctionType
ALU = mybir.AluOpType
AX_X = mybir.AxisListType.X

P = 128
D = 1024
S = 256
TB = S // P
KD = D // P
HALF = D // 2
NMEM = 256
EPS = 1e-6
LN_EPS = 1e-5
SLAB = 2048
RING = 4

CONV_W = 31
RET_HEADS, RET_DK, RET_DV, CHUNK = 8, 32, 64, 64
ROPE_HALF = RET_DK // 2
XA_HEADS = 4
XA_SCALE = float(D // XA_HEADS) ** -0.5
D_FF = 4 * D
SB_HEADS, SB_DIM = 8, 64
SB_COLS = S + P
SGU_GROUPS = 4
CONV3 = 3
BRANCHES = 3
HID2 = 2816
G1 = D_FF // 512
G2 = HID2 // 256

LOG_G = np.log1p(-np.exp2(-5.0 - np.arange(RET_HEADS)))
INV_FREQ = (10000.0 ** (-np.arange(ROPE_HALF) / ROPE_HALF)).astype(np.float32)
FAR = 1.0e9
PI = float(np.pi)
TWO_PI_A = 6.28125
TWO_PI_B = float(np.float32(np.round((2 * np.pi - TWO_PI_A) * 2 ** 22) / 2 ** 22))
TWO_PI_C = float(2 * np.pi - TWO_PI_A - TWO_PI_B)
SIN_MAX = 3.1415925
ROUND = 12582912.0
RSQRT_MAGIC = 1597463007.0

I_CONV, I_QK, I_RV, I_RG = 0, 4, 6, 8
I_K1, I_V1 = 10, 14
I_OUT1 = 18
I_Q1, I_O1 = 22, 26
I_FF1 = 30
I_SBQK = I_FF1 + 4 * G1
I_SBV, I_ZU, I_ZV, I_C3, I_BR = I_SBQK + 4, I_SBQK + 6, I_SBQK + 8, I_SBQK + 10, I_SBQK + 16
I_OUT2 = I_BR + 6 * BRANCHES
I_K2, I_V2 = I_OUT2 + 4, I_OUT2 + 8
I_Q2, I_O2 = I_OUT2 + 12, I_OUT2 + 16
I_FF2 = I_OUT2 + 20
N_SLABS = I_FF2 + 3 * G2
BRANCH_ORDER = (1, 2, 0)

GAINS = ["norm_mix_w", "norm_mem_w", "norm_xattn_w", "norm_mlp_w", "norm_f_w",
         "norm_mix_g_2", "mem_norm_g_2", "norm_xa_g_2", "norm_ffn_g_2", "final_g_2"]
N_MIX, N_MEM, N_XA, N_MLP, N_MIX2, N_MEM2, N_XA2, N_FF2 = range(8)
GAIN_OF = [0, 1, 2, 3, 5, 6, 7, 8]
GAIN_F, GAIN_FINAL = 4, 9


def slab_places():
    place, uses, before, last, count = [], [], [], {}, {}
    for i in range(N_SLABS):
        s = i % RING
        if i >= I_FF2:
            j = i - I_FF2
            s = j if j < 2 else (0, 1, 2)[(j - 2) % 3]
            if i == N_SLABS - 1:
                s = 2
        place.append(s)
        uses.append(count.get(s, 0))
        before.append(last.get(s))
        count[s] = uses[-1] + 1
        last[s] = i
    return place, uses, before


PLACE, USES, BEFORE = slab_places()


ROW_OF = {"conv_b": 0, "conv_ln_w": 4, "conv_ln_b": 8, "ret_gn_w": 12, "conv_w_2": 16}
ROWS_A = 16 + 4 * CONV3
RET_COLS = S + P
OUT1_ORDER = (2, 3, 0, 1)
C3_COLS = [(5 + w) * HALF + 256 * j for j in range(2) for w in (1, 2)] + [5 * HALF, 5 * HALF + 256]
SB_START = I_ZV + 1
ARENA, ARENA_WORDS = 16512, 53184

INPUTS = ["x", "mem", "positions", "norm_mix_w", "w_in", "conv_w", "conv_b", "conv_ln_w", "conv_ln_b", "ret_gn_w", "w_out",
          "norm_xattn_w", "norm_mem_w", "xq_w", "xkv_w", "xo_w", "norm_mlp_w", "mlp_up_w", "mlp_down_w", "norm_f_w",
          "mem_2", "norm_mix_g_2", "w_in_2", "sgu_ln_g_2", "sgu_ln_b_2", "w_spatial_2", "b_spatial_2", "conv_w_2",
          "w_branch_2", "w_out_2", "norm_xa_g_2", "mem_norm_g_2", "w_q_xa_2", "w_k_xa_2", "w_v_xa_2", "w_o_xa_2",
          "norm_ffn_g_2", "w_gate_ffn_2", "w_up_ffn_2", "w_down_ffn_2", "final_g_2"]


def ff2_gate(g):
    return I_FF2 if g == 0 else I_FF2 + 3 * g - 1


def build(nc, a, out):
    with ExitStack() as ctx:
        arena = ctx.enter_context(nc.sbuf_tensor("arena", [P, ARENA_WORDS], F32))
        cursor = [0]

        def at(name, shape, off, dt=F32):
            assert off + int(np.prod(shape[1:])) <= ARENA_WORDS, (name, off)
            return nc.alloc_sbuf_tensor_at(name, shape, dt, offset=ARENA + 4 * off)

        def new(name, shape, dt=F32):
            t = at(name, shape, cursor[0], dt)
            cursor[0] += -(-int(np.prod(shape[1:])) // 8) * 8
            return t

        w_ring = new("w_ring", [P, RING, SLAB])
        w_hi = new("w_hi", [P, RING, SLAB], F32R)
        w_lo = new("w_lo", [P, RING, SLAB], F32R)
        h = new("h", [P, TB, D])
        xh = new("xh", [P, KD, S], F32R)
        xl = new("xl", [P, KD, S], F32R)
        xn0 = cursor[0]
        xn = new("xn", [P, TB, D])
        gain = new("gain", [P, 2, D])
        ident = new("ident", [P, P])
        ones = new("ones", [P, P])
        later = new("later", [P, P])
        earlier = new("earlier", [P, P])
        cols_a = new("cols_a", [P, ROWS_A])
        cols_b = new("cols_b", [P, CONV_W * 4])
        stat = new("stat", [P, 256])
        ln_g = new("ln_g", [P, HALF])
        ln_b = new("ln_b", [P, HALF])
        b_sp = new("b_sp", [P, SGU_GROUPS, P])
        ws_t = new("ws_t", [P, SGU_GROUPS, P])
        kv0 = cursor[0]
        kT = new("kT", [P, KD, NMEM])
        vm = new("vm", [P, 2, D])
        split0 = cursor[0]
        mem_h = new("mem_h", [P, KD, NMEM], F32R)
        mem_l = new("mem_l", [P, KD, NMEM], F32R)
        t0 = cursor[0]

        u_pad = new("u_pad", [P, 4, CONV_W - 1 + S])
        c_acc = new("c_acc", [P, 4, S])
        rgs = new("rgs", [P, 4, S])
        mt0 = cursor[0]
        qkT = new("qkT", [P, 4, S])
        rv = new("rv", [P, TB, HALF])
        mem_tok = at("mem_tok", [P, 2, D], mt0)
        m1 = cursor[0]
        sig1 = at("sig1", [P, 2, S], m1)
        dist_i = at("dist_i", [P, S], kv0 + 2 * D, I32)
        rope_t = at("rope_t", [P, 4, 256], m1)
        dec = at("dec", [P, 2, S], m1)
        s_dec = at("s_dec", [P, 2, RET_COLS], m1 + 2 * S)
        n_v, n_y, n_t = (at(f"n_{x}", [P, S], m1 + S * i) for i, x in enumerate("vyt"))
        cursor[0] = m1 + 2 * S + 2 * RET_COLS
        dist = new("dist", [P, S])
        ang = new("ang", [P, 2, TB, ROPE_HALF])
        sincos = new("sincos", [P, 2, TB, ROPE_HALF])
        turns = new("turns", [P, TB, ROPE_HALF])
        pos_i = new("pos_i", [P, TB], I32)
        pos_f = new("pos_f", [P, TB])
        freq = new("freq", [P, ROPE_HALF])
        qk = at("qk", [P, TB, HALF], kv0 + 2 * D)
        ry = at("ry", [P, TB, HALF], kv0 + 2 * D)
        qkr = at("qkr", [P, TB, HALF], kv0 + 3 * D)
        ry_sq = at("ry_sq", [P, TB, HALF], kv0 + 3 * D)
        retT = at("retT", [P, 4, S], kv0 + 3 * D)
        c_sq = at("c_sq", [P, 4, S], t0)
        c_out = at("c_out", [P, 4, S], t0)
        rows_a = at("rows_a", [ROWS_A, P], kv0)
        rows_b = at("rows_b", [CONV_W * 4, P], kv0 + P)
        ws_rows = at("ws_rows", [P, SGU_GROUPS, P], kv0 + 2 * P)

        cursor[0] = t0
        qT = new("qT", [P, KD, S])
        prob = new("prob", [P, TB * XA_HEADS, NMEM])
        probT = new("probT", [P, 2, 2, S])

        cursor[0] = t0
        ff_r = new("ff_r", [P, 2, 2 * S])
        ff_u = new("ff_u", [P, 2, 2 * S])
        ff_h = at("ff_h", [P, 4, S], split0, F32R)
        ff_l = at("ff_l", [P, 4, S], split0 + D, F32R)

        cursor[0] = t0
        mem2_tok = at("mem2_tok", [P, 2, D], t0)
        qkT2 = new("qkT2", [P, 8, S])
        sb0 = cursor[0]
        mem2_h = at("mem2_h", [P, KD, NMEM], sb0, F32R)
        mem2_l = at("mem2_l", [P, KD, NMEM], sb0 + 2 * D, F32R)
        mem2_sq = at("mem2_sq", [P, 2, D], sb0)
        sb_e = new("sb_e", [P, 2, SB_COLS])
        sb_l = new("sb_l", [P, 2, SB_COLS])
        sb_m = new("sb_m", [P, 2, SB_COLS])
        sb_a = new("sb_a", [P, 2, SB_COLS])
        ug = new("ug", [P, 4, S])
        v2 = new("v2", [P, TB, HALF])
        y3_pad = at("y3_pad", [P, 4, CONV3 - 1 + S], kv0)
        cc_s = at("cc_s", [P, 2, S], kv0 + 4 * (CONV3 - 1 + S))
        acc3 = at("acc3", [P, 4, S], kv0 + 4 * (CONV3 - 1 + S) + 2 * S)
        merged = at("merged", [P, KD, S], kv0)
        vg = at("vg", [P, TB, HALF], kv0 + 3 * D)
        sig2 = at("sig2", [P, 4, S], kv0 + 3 * D)
        y_h = [at("ya_h", [P, 4, S], xn0, F32R), at("yb_h", [P, 4, S], split0, F32R),
               at("yc_h", [P, 4, S], split0 + 2 * D, F32R)]
        y_l = [at("ya_l", [P, 4, S], xn0 + D, F32R), at("yb_l", [P, 4, S], split0 + D, F32R),
               at("yc_l", [P, 4, S], split0 + 3 * D, F32R)]

        used = [0]

        def cols(n):
            used[0] += n
            assert used[0] <= 256
            return stat[:, used[0] - n:used[0]]

        sq_sum = cols(2 * 10)
        nv, ny, nt = cols(2), cols(2), cols(2)
        xmax, xneg, xsum, xinv = cols(8), cols(8), cols(8), cols(8)
        r_mean, r_var, r_y, r_t = cols(16), cols(16), cols(16), cols(16)
        bn6, bn2 = cols(6 * TB), cols(2 * TB)

        ps = ctx.enter_context(nc.psum_tensor("ps", [P, 8, 512], F32))

        def tok(b):
            return ps[:, b, :]

        def feat(b):
            return ps[:, 4 + b, :]

        def blocks(x):
            return x.rearrange("p (t n) -> p t n", n=S)

        def sem(name):
            return ctx.enter_context(nc.semaphore(name))

        w_loaded = [sem(f"w_loaded{s}") for s in range(RING)]
        hi_done, lo_done, slab_used = sem("hi_done"), sem("lo_done"), sem("slab_used")
        x_loaded, mem_loaded, mem2_loaded = sem("x_loaded"), sem("mem_loaded"), sem("mem2_loaded")
        rows_loaded, pos_loaded, sgu_loaded = sem("rows_loaded"), sem("pos_loaded"), sem("sgu_loaded")
        gain_loaded = [sem("gain_loaded0"), sem("gain_loaded1")]
        gain_used = sem("gain_used")
        fill, const_ready, dist_ready, freq_ready = sem("fill"), sem("const_ready"), sem("dist_ready"), sem("freq_ready")
        pad_ready, ws_masked, pad3_ready = sem("pad_ready"), sem("ws_masked"), sem("pad3_ready")
        act_step, dve_step = sem("act_step"), sem("dve_step")
        norm_sq, norm_xn, norm_t, norm_hi, norm_lo = (sem(f"norm_{x}") for x in ("sq", "xn", "t", "hi", "lo"))
        rows_t, cols_ready = sem("rows_t"), sem("cols_ready")
        ang_ready, sincos_ready = sem("ang_ready"), sem("sincos_ready")
        sig_ready, u_ready, rg_ready, rv_ready, qk_ready = (sem(x) for x in ("sig_ready", "u_ready", "rg_ready", "rv_ready", "qk_ready"))
        rope_ready, qk_t, qkT_ready = sem("rope_ready"), sem("qk_t"), sem("qkT_ready")
        ret_s, dec_ready, s_dec_ready, ret_pv = sem("ret_s"), sem("dec_ready"), sem("s_dec_ready"), sem("ret_pv")
        ry_centred, ry_squared, ry_ready, ry_t = sem("ry_centred"), sem("ry_squared"), sem("ry_ready"), sem("ry_t")
        ret_ready, ret_hi, ret_lo = sem("ret_ready"), sem("ret_hi"), sem("ret_lo")
        conv_step, conv_mean, conv_centred = sem("conv_step"), sem("conv_mean"), sem("conv_centred")
        conv_squared, conv_var, conv_normed = sem("conv_squared"), sem("conv_var"), sem("conv_normed")
        conv_out, conv_hi, conv_lo = sem("conv_out"), sem("conv_hi"), sem("conv_lo")
        k_ready, v_ready = sem("k_ready"), sem("v_ready")
        tb0_done, h_updated, h_normed = sem("tb0_done"), sem("h_updated"), sem("h_normed")
        xq_ready, xs_ready, xmax_ready, xexp_ready = sem("xq_ready"), sem("xs_ready"), sem("xmax_ready"), sem("xexp_ready")
        xp_ready, xp_t, xpT_ready = sem("xp_ready"), sem("xp_t"), sem("xpT_ready")
        xo_ready, xo_hi, xo_lo = sem("xo_ready"), sem("xo_hi"), sem("xo_lo")
        relu_ready, relu_sq, ff_hi, ff_lo = sem("relu_ready"), sem("relu_sq"), sem("ff_hi"), sem("ff_lo")
        silu_ready, glu_ready, glu_hi, glu_lo = sem("silu_ready"), sem("glu_ready"), sem("glu_hi"), sem("glu_lo")
        sbqk_ready, sbv_ready, ug_ready, vg_ready, vn_ready = (sem(x) for x in ("sbqk_ready", "sbv_ready", "ug_ready", "vg_ready", "vn_ready"))
        sb_z, sb_log, sb_pen, sb_cum, sb_arg = sem("sb_z"), sem("sb_log"), sem("sb_pen"), sem("sb_cum"), sem("sb_arg")
        sb_exp, sb_prob, sb_out, sb_hi, sb_lo = sem("sb_exp"), sem("sb_prob"), sem("sb_out"), sem("sb_hi"), sem("sb_lo")
        sgu_mixed, yb_ready, yb_hi, yb_lo = sem("sgu_mixed"), sem("yb_ready"), sem("yb_hi"), sem("yb_lo")
        cc_ready, y3_ready, yc_ready, yc_hi, yc_lo = sem("cc_ready"), sem("y3_ready"), sem("yc_ready"), sem("yc_hi"), sem("yc_lo")
        gate_ready, merge_done, merged_hi, merged_lo = sem("gate_ready"), sem("merge_done"), sem("merged_hi"), sem("merged_lo")
        out_ready, stored = sem("out_ready"), sem("stored")

        block = ctx.enter_context(nc.Block())

        UPD = {I_OUT1: 0, I_O1: 1, I_FF1: 2, I_OUT2: 3, I_O2: 4, I_FF2: 5}

        @block.sync
        def _(sp):
            def load(i, src, step=0, wait_step=0):
                s = PLACE[i]
                if BEFORE[i] is not None:
                    sp.wait_ge(lo_done, BEFORE[i] + 1 + wait_step)
                dst = w_ring[:, s, :].rearrange("p (k n) -> p k n", n=src.shape[2])
                sp.dma_start(dst, src).then_inc(w_loaded[s], 16)

            def panel_a(w, col, n=256):
                return w.rearrange("(k p) n -> p k n", p=P)[:, :, col:col + n]

            def rows_b_form(w, row, col=0, n=D, nk=2):
                return w[row:row + nk * P, col:col + n].rearrange("(k p) n -> p k n", p=P)

            sp.dma_start(h[:, :, :], a["x"].rearrange("a (t p) d -> p (a t) d", p=P)).then_inc(x_loaded, 16)
            w_in = a["w_in"]
            for j in range(2):
                load(I_CONV + 2 * j, panel_a(w_in, 256 * j))
                if j == 0:
                    sp.dma_start(mem_tok[:, :, :], a["mem"].rearrange("a (t p) d -> p (a t) d", p=P)).then_inc(mem_loaded, 16)
                load(I_CONV + 2 * j + 1, panel_a(w_in, HALF + 256 * j))
            for j in range(2):
                load(I_QK + j, rows_b_form(w_in, 512 * j, 2 * HALF, HALF, 4))
            for j in range(2):
                load(I_RV + j, rows_b_form(w_in, 512 * j, 3 * HALF, HALF, 4))
            for j in range(2):
                load(I_RG + j, panel_a(w_in, 4 * HALF + 256 * j))
            for j in range(4):
                load(I_K1 + j, panel_a(a["xkv_w"], 256 * j))
            for j in range(4):
                load(I_V1 + j, rows_b_form(a["xkv_w"], 256 * j, D))
            for j, k in enumerate(OUT1_ORDER):
                load(I_OUT1 + j, rows_b_form(a["w_out"], 256 * k))
            for j in range(4):
                load(I_Q1 + j, panel_a(a["xq_w"], 256 * j))
            for j in range(4):
                load(I_O1 + j, rows_b_form(a["xo_w"], 256 * j))
            up = a["mlp_up_w"].rearrange("(k p) n -> p k n", p=P)
            down = a["mlp_down_w"].rearrange("(k p) n -> p k n", p=P)
            with sp.Fori(0, G1) as g:
                for c in range(2):
                    load(I_FF1 + c, up[:, :, bass.ds(g * 512 + 256 * c, 256)], wait_step=4 * g)
                for c in range(2):
                    load(I_FF1 + 2 + c, down[:, bass.ds(g * 4 + 2 * c, 2), :], wait_step=4 * g)
            w2 = a["w_in_2"].squeeze(0)
            for j in range(4):
                load(I_SBQK + j, panel_a(w2, 256 * j))
            for j in range(2):
                load(I_SBV + j, rows_b_form(w2, 512 * j, 2 * HALF, HALF, 4))
            for j in range(2):
                load(I_ZU + j, panel_a(w2, 3 * HALF + 256 * j))
            for j in range(2):
                load(I_ZV + j, rows_b_form(w2, 512 * j, 4 * HALF, HALF, 4))
            for j, col in enumerate(C3_COLS):
                load(I_C3 + j, panel_a(w2, col))
            wb = a["w_branch_2"].squeeze(0)
            for n, br in enumerate(BRANCH_ORDER):
                for half in range(2):
                    i = I_BR + 6 * n + 3 * half
                    for j in range(2):
                        load(i + j, panel_a(w2, 8 * HALF + D * br + HALF * half + 256 * j))
                    load(i + 2, panel_a(wb[br], HALF * half, HALF))
            for j in range(4):
                load(I_OUT2 + j, rows_b_form(a["w_out_2"].squeeze(0), 256 * j))
            for j in range(4):
                load(I_K2 + j, panel_a(a["w_k_xa_2"].squeeze(0), 256 * j))
            for j in range(4):
                load(I_V2 + j, rows_b_form(a["w_v_xa_2"].squeeze(0), 256 * j))
            for j in range(4):
                load(I_Q2 + j, panel_a(a["w_q_xa_2"].squeeze(0), 256 * j))
            for j in range(4):
                load(I_O2 + j, rows_b_form(a["w_o_xa_2"].squeeze(0), 256 * j))
            wg = a["w_gate_ffn_2"].squeeze(0).rearrange("(k p) n -> p k n", p=P)
            wu = a["w_up_ffn_2"].squeeze(0).rearrange("(k p) n -> p k n", p=P)
            wd = a["w_down_ffn_2"].squeeze(0).rearrange("(k p) n -> p k n", p=P)
            load(I_FF2, wg[:, :, 0:256])
            load(I_FF2 + 1, wu[:, :, 0:256])
            for g in range(1, 2):
                i = ff2_gate(g)
                load(i, wg[:, :, 256 * g:256 * g + 256])
                load(i + 1, wu[:, :, 256 * g:256 * g + 256])
                load(i + 2, wd[:, 2 * g - 2:2 * g, :])
            i = ff2_gate(2)
            with sp.Fori(0, G2 - 2) as t:
                load(i, wg[:, :, bass.ds(t * 256 + 512, 256)], wait_step=3 * t)
                load(i + 1, wu[:, :, bass.ds(t * 256 + 512, 256)], wait_step=3 * t)
                load(i + 2, wd[:, bass.ds(t * 2 + 2, 2), :], wait_step=3 * t)
            load(N_SLABS - 1, wd[:, 2 * G2 - 2:2 * G2, :])
            for tb in range(TB):
                sp.wait_ge(out_ready, tb + 1)
                sp.dma_start(out[0, tb * P:(tb + 1) * P, :], xn[:, tb, :]).then_inc(stored, 16)
            sp.wait_ge(stored, 16 * TB)

        @block.gpsimd
        def _(pool):
            def load_gain(n):
                if n >= 2:
                    pool.wait_ge(gain_used, n - 1)
                w = a[GAINS[n]]
                w = w if len(w.shape) == 1 else w.squeeze(0)
                pool.dma_start(gain[:, n % 2, :], w.partition_broadcast(P)).then_inc(gain_loaded[n % 2], 16)

            load_gain(0)
            pool.dma_start(pos_i[:, :], a["positions"].rearrange("a (t p) -> p (a t)", p=P), allow_slow_non_contiguous=True).then_inc(pos_loaded, 16)
            load_gain(1)
            for name, r in ROW_OF.items():
                w = a[name]
                w = w.squeeze(0).rearrange("k (c p) -> (k c) p", p=P) if name == "conv_w_2" else w.rearrange("(c p) -> c p", p=P)
                pool.dma_start(rows_a[r:r + w.shape[0], :], w).then_inc(rows_loaded, 16)
            pool.dma_start(rows_b[:, :], a["conv_w"].rearrange("k (c p) -> (k c) p", p=P)).then_inc(rows_loaded, 16)
            pool.dma_start(ws_rows[:, :, :], a["w_spatial_2"].squeeze(0).rearrange("g t s -> t g s")).then_inc(rows_loaded, 16)
            pool.dma_start(ln_g[:, :], a["sgu_ln_g_2"].squeeze(0).partition_broadcast(P)).then_inc(sgu_loaded, 16)
            pool.dma_start(ln_b[:, :], a["sgu_ln_b_2"].squeeze(0).partition_broadcast(P)).then_inc(sgu_loaded, 16)
            pool.dma_start(b_sp[:, :, :], a["b_spatial_2"].squeeze(0).rearrange("g t -> (g t)").partition_broadcast(P)
                           .rearrange("p (g t) -> p g t", g=SGU_GROUPS)).then_inc(sgu_loaded, 16)
            pool.memset(ident[:, :], 0.0).then_inc(fill, 1)
            pool.memset(later[:, :], 1.0).then_inc(fill, 1)
            pool.memset(earlier[:, :], 1.0).then_inc(fill, 1)
            pool.wait_ge(fill, 3)
            pool.affine_select(out=ident[:, :], in_=ident[:, :], compare_op=ALU.not_equal, fill=1.0, base=0,
                               pattern=[[-1, P]], channel_multiplier=1).then_inc(const_ready, 1)
            pool.iota(dist_i[:, :], pattern=[[1, S]], base=0, channel_multiplier=-1).then_inc(dist_ready, 1)
            for f in range(ROPE_HALF):
                pool.memset(freq[:, f:f + 1], float(INV_FREQ[f])).then_inc(freq_ready, 1)
            pool.memset(u_pad[:, :, 0:CONV_W - 1], 0.0).then_inc(pad_ready, 1)
            pool.memset(ones[:, :], 1.0).then_inc(const_ready, 1)
            pool.affine_select(out=later[:, :], in_=later[:, :], compare_op=ALU.is_gt, fill=0.0, base=0,
                               pattern=[[-1, P]], channel_multiplier=1).then_inc(const_ready, 1)
            pool.affine_select(out=earlier[:, :], in_=earlier[:, :], compare_op=ALU.is_gt, fill=0.0, base=0,
                               pattern=[[1, P]], channel_multiplier=-1).then_inc(const_ready, 1)
            pool.wait_ge(const_ready, 4)
            pool.wait_ge(cols_ready, 3)
            pool.memset(ws_t[CHUNK:P, :, 0:CHUNK], 0.0).then_inc(ws_masked, 1)
            for n in range(2, 6):
                load_gain(n)
            pool.wait_ge(xo_ready, XA_HEADS)
            pool.wait_ge(ws_masked, 1)
            pool.memset(y3_pad[:, :, 0:CONV3 - 1], 0.0).then_inc(pad3_ready, 1)
            load_gain(6)
            pool.wait_ge(sb_z, 4)
            pool.dma_start(mem2_tok[:, :, :], a["mem_2"].rearrange("a (t p) d -> p (a t) d", p=P)).then_inc(mem2_loaded, 16)
            for n in range(7, 10):
                load_gain(n)

        @block.tensor
        def _(pe):
            def mm3(o, left, right, first, last):
                (lh, ll), (rh, rl) = left, right
                pe.matmul(o, lh, rh, start=first, stop=False)
                pe.matmul(o, lh, rl, start=False, stop=False)
                return pe.matmul(o, ll, rh, start=False, stop=last)

            def slab(i, n):
                s = PLACE[i]
                return tuple(w[:, s, :].rearrange("p (k n) -> p k n", n=n) for w in (w_hi, w_lo))

            def form_a(i, banks, xt, n=256, step=0):
                pe.wait_ge(lo_done, i + 1 + step)
                wh, wl = slab(i, n)
                nk = SLAB // n
                for b in range(n // P):
                    for k in range(nk):
                        c = slice(b * P, (b + 1) * P)
                        mm = mm3(feat(banks[b // 2])[:, (b % 2) * S:(b % 2 + 1) * S], (wh[:, k, c], wl[:, k, c]),
                                 (xt[0][:, k, :], xt[1][:, k, :]), k == 0, k == nk - 1)
                mm.then_inc(slab_used, 1)

            def form_b_rows(i, k0, xt, tbs, first, last, step=0, n=D):
                pe.wait_ge(lo_done, i + 1 + step)
                wh, wl = slab(i, n)
                nk = SLAB // n
                for kk in range(nk):
                    for tb in tbs:
                        t = slice(tb * P, (tb + 1) * P)
                        for half in range(n // HALF):
                            c = slice(half * HALF, (half + 1) * HALF)
                            mm = mm3(tok(2 * tb + half) if n == D else None, (xt[0][:, k0 + kk, t], xt[1][:, k0 + kk, t]),
                                     (wh[:, kk, c], wl[:, kk, c]), first and kk == 0, last and kk == nk - 1)
                return mm

            def form_b(i0, xt, order, ready):
                for j in range(2):
                    ready(order[j])
                    form_b_rows(i0 + j, 2 * order[j], xt, (0, 1), j == 0, False).then_inc(slab_used, 1)
                for j in (2, 3):
                    ready(order[j])
                    mm = form_b_rows(i0 + j, 2 * order[j], xt, (0,), False, j == 3)
                mm.then_inc(tb0_done, 1)
                for j in (2, 3):
                    form_b_rows(i0 + j, 2 * order[j], xt, (1,), False, j == 3).then_inc(slab_used, 1)

            def form_b_half(i0, bank, xt):
                for j in range(2):
                    pe.wait_ge(lo_done, i0 + j + 1)
                    wh, wl = slab(i0 + j, HALF)
                    for kk in range(4):
                        k = 4 * j + kk
                        for tb in range(TB):
                            t = slice(tb * P, (tb + 1) * P)
                            mm = mm3(tok(bank + tb), (xt[0][:, k, t], xt[1][:, k, t]), (wh[:, kk, :], wl[:, kk, :]),
                                     k == 0, k == KD - 1)
                    mm.then_inc(slab_used, 1)

            def norm_transpose(n, src):
                for tb in range(TB):
                    pe.wait_ge(norm_xn, 2 * n + tb + 1)
                    for f in range(KD):
                        mm = pe.transpose(tok(2 * tb + f // 4)[:, (f % 4) * P:(f % 4 + 1) * P],
                                          src[:, tb, f * P:(f + 1) * P], ident[:, :])
                    mm.then_inc(norm_t, 1)

            def normed(n):
                pe.wait_ge(norm_lo, 4 * (n + 1))

            def x_attention(b, i_q, i_o):
                def scores(hd):
                    pe.wait_ge(xq_ready, 4 * b + hd + 1)
                    pe.wait_ge(k_ready, 4 * (b + 1))
                    for tb in range(TB):
                        u = TB * hd + tb
                        if u >= 4:
                            pe.wait_ge(xexp_ready, 8 * b + u - 3)
                        for kk in range(2):
                            f = 2 * hd + kk
                            mm = pe.matmul(tok(u % 4)[:, 0:NMEM], qT[:, f, tb * P:(tb + 1) * P], kT[:, f, :],
                                           start=kk == 0, stop=kk == 1)
                        mm.then_inc(xs_ready, 1)

                def turn(hd):
                    for tb in range(TB):
                        u = TB * hd + tb
                        pe.wait_ge(xp_ready, 8 * b + u + 1)
                        for m in range(2):
                            mm = pe.transpose(feat(hd)[:, m * S + tb * P:m * S + (tb + 1) * P],
                                              prob[:, u, m * P:(m + 1) * P], ident[:, :])
                    mm.then_inc(xp_t, 1)

                def values(hd):
                    pe.wait_ge(xpT_ready, 4 * b + hd + 1)
                    pe.wait_ge(v_ready, 4 * (b + 1))
                    for kk in range(2):
                        f = 2 * hd + kk
                        for m in range(2):
                            mm = pe.matmul(feat(hd)[:, kk * S:(kk + 1) * S], vm[:, m, f * P:(f + 1) * P],
                                           probT[:, hd % 2, m, :], start=m == 0, stop=m == 1)
                    mm.then_inc(xo_ready, 1)

                form_a(i_q, (0,), (xh, xl))
                form_a(i_q + 1, (1,), (xh, xl))
                pe.wait_ge(v_ready, 4 * (b + 1))
                scores(0)
                form_a(i_q + 2, (2,), (xh, xl))
                scores(1)
                form_a(i_q + 3, (3,), (xh, xl))
                turn(0)
                scores(2)
                values(0)
                turn(1)
                scores(3)
                values(1)
                turn(2)
                values(2)
                turn(3)
                values(3)
                pe.wait_ge(xexp_ready, 8 * (b + 1))
                form_b(i_o, (xh, xl), range(4), lambda s: pe.wait_ge(xo_lo, 4 * b + s + 1))

            x_t, m_t = (xh, xl), (mem_h, mem_l)
            pe.wait_ge(const_ready, 1)
            norm_transpose(N_MIX, xn)
            normed(N_MIX)
            form_a(0, (0,), x_t)
            norm_transpose(N_MEM, xn)
            form_a(1, (1,), x_t)
            pe.wait_ge(rows_loaded, 16 * (len(ROW_OF) + 2))
            normed(N_MEM)
            pe.transpose(tok(0)[:, 0:ROWS_A], rows_a[:, :], ident[0:ROWS_A, 0:ROWS_A])
            pe.transpose(tok(0)[:, P:P + 4 * CONV_W], rows_b[:, :], ident[0:4 * CONV_W, 0:4 * CONV_W])
            for g in range(SGU_GROUPS):
                mm = pe.transpose(tok(1)[:, g * P:(g + 1) * P], ws_rows[:, g, :], ident[:, :])
            mm.then_inc(rows_t, 1)
            form_a(2, (2,), x_t)
            form_a(3, (3,), x_t)
            pe.wait_ge(cols_ready, 3)
            form_b_half(I_QK, 0, x_t)
            form_b_half(I_RV, 2, x_t)
            pe.wait_ge(rope_ready, 2)
            for f in range(4):
                for tb in range(TB):
                    mm = pe.transpose(tok(f // 2)[:, (f % 2) * S + tb * P:(f % 2) * S + (tb + 1) * P],
                                      qkr[:, tb, f * P:(f + 1) * P], ident[:, :])
                if f % 2:
                    mm.then_inc(qk_t, 1)
            pe.wait_ge(u_ready, 1)
            form_a(I_RG, (0,), x_t)

            def ret_scores(hd):
                pe.wait_ge(qkT_ready, 2)
                if hd == 2:
                    pe.wait_ge(rv_ready, 2)
                if hd >= 4:
                    pe.wait_ge(s_dec_ready, hd - 3)
                r = slice(RET_DK * (hd % 4), RET_DK * (hd % 4 + 1))
                f = hd // 4
                pe.matmul(tok(hd % 4)[:, 0:S], qkT[r, 2 + f, 0:P], qkT[r, f, 0:S], start=True, stop=True)
                pe.matmul(tok(hd % 4)[:, S:S + P], qkT[r, 2 + f, P:S], qkT[r, f, P:S],
                          start=True, stop=True).then_inc(ret_s, 1)

            def ret_values(hd):
                pe.wait_ge(s_dec_ready, hd + 1)
                pe.wait_ge(rv_ready, 2)
                pe.wait_ge(u_ready, 2)
                c = slice(hd * RET_DV, (hd + 1) * RET_DV)
                sd = s_dec[:, hd % 2, :]
                pe.matmul(feat(2)[:, c], sd[:, 0:P], rv[:, 0, c], start=True, stop=True)
                pe.matmul(feat(3)[:, c], sd[:, P:S], rv[:, 0, c], start=True, stop=False)
                pe.matmul(feat(3)[:, c], sd[:, S:S + P], rv[:, 1, c], start=False, stop=True).then_inc(ret_pv, 1)

            ret_scores(0)
            ret_scores(1)
            form_a(I_RG + 1, (1,), x_t)
            for hd in range(4):
                ret_scores(hd + 2)
                ret_values(hd)
            pe.wait_ge(rg_ready, 1)
            form_a(I_K1, (0,), m_t)
            for hd in range(4, RET_HEADS):
                if hd + 2 < RET_HEADS:
                    ret_scores(hd + 2)
                ret_values(hd)
            pe.wait_ge(rg_ready, 2)
            form_a(I_K1 + 1, (1,), m_t)
            pe.wait_ge(k_ready, 1)
            form_a(I_K1 + 2, (0,), m_t)
            pe.wait_ge(ry_ready, 1)
            for f in range(4):
                for tb in range(TB):
                    mm = pe.transpose(tok(2 + f // 2)[:, (f % 2) * S + tb * P:(f % 2) * S + (tb + 1) * P],
                                      ry[:, tb, f * P:(f + 1) * P], ident[:, :])
            mm.then_inc(ry_t, 1)
            pe.wait_ge(k_ready, 2)
            form_a(I_K1 + 3, (1,), m_t)
            pe.wait_ge(ret_ready, 1)
            for j in range(4):
                form_b_rows(I_V1 + j, 2 * j, m_t, (0, 1), j == 0, j == 3).then_inc(slab_used, 1)
            pe.wait_ge(v_ready, 4)
            pe.wait_ge(ret_lo, 1)
            form_b_rows(I_OUT1, 2 * OUT1_ORDER[0], x_t, (0, 1), True, False).then_inc(slab_used, 1)
            pe.wait_ge(const_ready, 4)
            pe.wait_ge(conv_step, CONV_W * 4)
            for c in range(4):
                mm = pe.matmul(feat(2)[:, 0:S], ones[:, :], c_acc[:, c, :], start=c == 0, stop=c == 3)
            mm.then_inc(conv_mean, 1)
            form_b_rows(I_OUT1 + 1, 2 * OUT1_ORDER[1], x_t, (0, 1), False, False).then_inc(slab_used, 1)
            pe.wait_ge(conv_squared, 1)
            for c in range(4):
                mm = pe.matmul(feat(3)[:, 0:S], ones[:, :], c_sq[:, c, :], start=c == 0, stop=c == 3)
            mm.then_inc(conv_var, 1)
            pe.wait_ge(conv_lo, 1)
            for j in (2, 3):
                mm = form_b_rows(I_OUT1 + j, 2 * OUT1_ORDER[j], x_t, (0,), False, j == 3)
            mm.then_inc(tb0_done, 1)
            for j in (2, 3):
                form_b_rows(I_OUT1 + j, 2 * OUT1_ORDER[j], x_t, (1,), False, j == 3).then_inc(slab_used, 1)
            norm_transpose(N_XA, xn)
            normed(N_XA)
            pe.wait_ge(k_ready, 4)
            x_attention(0, I_Q1, I_O1)
            norm_transpose(N_MLP, xn)
            normed(N_MLP)

            def mlp1(g, first=False, last=False):
                step = 0 if first else 4 * g
                i = I_FF1
                for c in range(2):
                    if first:
                        pe.wait_ge(xo_lo, 4)
                    else:
                        pe.wait_ge(relu_ready, 2 * g - 1 + c)
                    form_a(i + c, (c,), x_t, step=step)
                u_t = (ff_h, ff_l)
                two = 0 if first else 2 * g
                if last:
                    for c in range(2):
                        pe.wait_ge(ff_lo, two + c + 1)
                        mm = form_b_rows(i + 2 + c, 2 * c, u_t, (0,), False, c == 1, step=step)
                    mm.then_inc(tb0_done, 1)
                    for c in range(2):
                        form_b_rows(i + 2 + c, 2 * c, u_t, (1,), False, c == 1, step=step).then_inc(slab_used, 1)
                else:
                    for c in range(2):
                        pe.wait_ge(ff_lo, two + c + 1)
                        form_b_rows(i + 2 + c, 2 * c, u_t, (0, 1), first and c == 0, False, step=step).then_inc(slab_used, 1)

            mlp1(0, first=True)
            with pe.Fori(1, G1 - 1) as g:
                mlp1(g)
            mlp1(G1 - 1, last=True)
            norm_transpose(N_MIX2, xn)
            normed(N_MIX2)
            for j in range(4):
                form_a(I_SBQK + j, (j,), x_t)
            form_b_half(I_SBV, 0, x_t)

            def sb_scores(p):
                if p == 0:
                    pe.wait_ge(sbv_ready, 2)
                    pe.wait_ge(sbqk_ready, 4)
                else:
                    pe.wait_ge(sb_lo, p)
                    pe.wait_ge(sb_arg, p)
                for e in range(2):
                    r = slice(SB_DIM * e, SB_DIM * (e + 1))
                    pe.matmul(tok(e)[:, 0:S], qkT2[r, 4 + p, 0:P], qkT2[r, p, 0:S], start=True, stop=True)
                    mm = pe.matmul(tok(e)[:, S:S + P], qkT2[r, 4 + p, P:S], qkT2[r, p, P:S], start=True, stop=True)
                mm.then_inc(sb_z, 1)

            def sb_sums(p):
                pe.wait_ge(sb_pen, p + 1)
                if p == 0:
                    pe.wait_ge(vg_ready, 2)
                else:
                    pe.wait_ge(sb_arg, p)
                for e in range(2):
                    pe.matmul(tok(2 + e)[:, 0:S], later[:, :], sb_m[:, e, 0:S], start=True, stop=False)
                    pe.matmul(tok(2 + e)[:, P:S], ones[:, :], sb_m[:, e, S:S + P], start=False, stop=True)
                    mm = pe.matmul(tok(2 + e)[:, S:S + P], later[:, :], sb_m[:, e, S:S + P], start=True, stop=True)
                mm.then_inc(sb_cum, 1)

            def sb_values(p):
                pe.wait_ge(sb_prob, p + 1)
                for e in range(2):
                    r = slice(SB_DIM * e, SB_DIM * (e + 1))
                    c = slice((2 * p + e) * SB_DIM, (2 * p + e + 1) * SB_DIM)
                    pe.matmul(tok(0)[r, 0:S], v2[:, 0, c], sb_a[:, e, 0:S], start=True, stop=False)
                    mm = pe.matmul(tok(0)[r, P:S], v2[:, 1, c], sb_a[:, e, S:S + P], start=False, stop=True)
                mm.then_inc(sb_out, 1)

            SB_AT = {}
            for p in range(4):
                SB_AT[SB_START + 5 * p] = lambda p=p: sb_scores(p)
                SB_AT[SB_START + 5 * p + 2] = lambda p=p: sb_sums(p)
                SB_AT[SB_START + 5 * p + 4] = lambda p=p: sb_values(p)

            def beside(i):
                if i in SB_AT:
                    SB_AT[i]()

            pe.wait_ge(sbqk_ready, 2)
            form_a(I_ZU, (0,), x_t)
            form_a(I_ZU + 1, (1,), x_t)
            form_b_half(I_ZV, 2, x_t)
            beside(I_ZV + 1)
            pe.wait_ge(sbqk_ready, 4)
            form_a(I_C3, (2,), x_t)
            beside(I_C3)
            form_a(I_C3 + 1, (3,), x_t)
            beside(I_C3 + 1)
            pe.wait_ge(ug_ready, 2)
            form_a(I_C3 + 2, (0,), x_t)
            beside(I_C3 + 2)
            form_a(I_C3 + 3, (1,), x_t)
            beside(I_C3 + 3)
            pe.wait_ge(y3_ready, 1)
            form_a(I_C3 + 4, (2,), x_t)
            beside(I_C3 + 4)
            form_a(I_C3 + 5, (3,), x_t)
            beside(I_C3 + 5)
            pe.wait_ge(vn_ready, 2)
            pe.wait_ge(ws_masked, 1)
            pe.wait_ge(y3_ready, 2)
            for g in range(SGU_GROUPS):
                for tb in range(TB):
                    o = feat(g // 2)[:, (g % 2) * S + tb * P:(g % 2) * S + (tb + 1) * P]
                    mm = pe.matmul(o, vg[:, tb, g * P:(g + 1) * P], ws_t[:, g, :], start=True, stop=True)
            mm.then_inc(sgu_mixed, 1)
            for n, br in enumerate(BRANCH_ORDER):
                for half in range(2):
                    i = I_BR + 6 * n + 3 * half
                    r = 2 * n + half
                    if r == 0:
                        pe.wait_ge(yb_ready, 2)
                    for j in range(2):
                        if r > 0:
                            pe.wait_ge(gate_ready, 2 * r - 1 + j)
                        form_a(i + j, (j,), x_t)
                        beside(i + j)
                    if r == 0:
                        pe.wait_ge(yc_ready, 2)
                    else:
                        pe.wait_ge(merge_done, r)
                    pe.wait_ge((sb_lo, yb_lo, yc_lo)[br], (4, 1, 1)[br])
                    form_a(i + 2, (2, 3), (y_h[br], y_l[br]), n=HALF)
                    beside(i + 2)
                    if r == 4:
                        norm_transpose(N_MEM2, mem2_tok)
            normed(N_MEM2)
            form_b(I_OUT2, x_t, range(4), lambda s: pe.wait_ge(merged_lo, 1 + s // 2))
            m2_t = (mem2_h, mem2_l)
            pe.wait_ge(gate_ready, 12)
            form_a(I_K2, (0,), m2_t)
            form_a(I_K2 + 1, (1,), m2_t)
            norm_transpose(N_XA2, xn)
            pe.wait_ge(merge_done, 6)
            form_a(I_K2 + 2, (2,), m2_t)
            form_a(I_K2 + 3, (3,), m2_t)
            normed(N_XA2)
            for j in range(4):
                form_b_rows(I_V2 + j, 2 * j, m2_t, (0, 1), j == 0, j == 3).then_inc(slab_used, 1)
            pe.wait_ge(k_ready, 8)
            x_attention(1, I_Q2, I_O2)
            norm_transpose(N_FF2, xn)
            normed(N_FF2)

            def glu_in(g, i, step=0):
                if g is not None:
                    pe.wait_ge(glu_ready, g)
                form_a(i, (0,), x_t, step=step)
                form_a(i + 1, (1,), x_t, step=step)

            def glu_out(i, done, first=False, step=0):
                pe.wait_ge(glu_lo, done)
                form_b_rows(i, 0, (ff_h, ff_l), (0, 1), first, False, step=step).then_inc(slab_used, 1)

            pe.wait_ge(xo_lo, 8)
            glu_in(None, I_FF2)
            glu_in(1, ff2_gate(1))
            glu_out(ff2_gate(1) + 2, 1, first=True)
            with pe.Fori(0, G2 - 2) as t:
                glu_in(t + 2, ff2_gate(2), step=3 * t)
                glu_out(ff2_gate(2) + 2, t + 2, step=3 * t)
            pe.wait_ge(glu_lo, G2)
            form_b_rows(N_SLABS - 1, 0, (ff_h, ff_l), (0,), False, True).then_inc(tb0_done, 1)
            form_b_rows(N_SLABS - 1, 0, (ff_h, ff_l), (1,), False, True).then_inc(slab_used, 1)

        @block.scalar
        def _(act):
            count = [0]

            def after(ins):
                count[0] += 1
                ins.then_inc(act_step, 1)
                act.wait_ge(act_step, count[0])

            def hi(i, step=0, turn=0):
                s = PLACE[i]
                act.wait_ge(w_loaded[s], 16 * (USES[i] + 1) + 16 * turn)
                if BEFORE[i] is not None:
                    act.wait_ge(slab_used, BEFORE[i] + 1 + step)
                act.activation(w_hi[:, s, :], w_ring[:, s, :], ACT.Copy).then_inc(hi_done, 1)

            def norm_square(n, src, tb, use, junk=xn):
                act.activation(junk[:, tb, :], src[:, tb, :], ACT.Square,
                               accum_out=sq_sum[:, 2 * use + tb:2 * use + tb + 1]).then_inc(norm_sq, 1)

            def h_square(n, tb, upd, use):
                act.wait_ge(h_updated, 4 * upd + 2 * tb + 2)
                norm_square(n, h, tb, use)

            def norm_split_hi(n, tb, dst=xh):
                act.wait_ge(norm_t, 2 * n + tb + 1)
                for half in range(2):
                    act.activation(dst[:, 4 * half:4 * half + 4, tb * P:(tb + 1) * P],
                                   tok(2 * tb + half).rearrange("p (f t) -> p f t", t=P), ACT.Copy).then_inc(norm_hi, 1)

            def used_slab(i):
                act.wait_ge(slab_used, i + 1)

            def boundary(n, upd, use, nxt, places=4):
                hi(nxt)
                hi(nxt + 1)
                h_square(n, 0, upd, use)
                if places == 4:
                    hi(nxt + 2)
                h_square(n, 1, upd, use)
                norm_split_hi(n, 0)
                norm_split_hi(n, 1)
                if places == 4:
                    hi(nxt + 3)

            act.wait_ge(x_loaded, 16)
            norm_square(N_MIX, h, 0, 0)
            norm_square(N_MIX, h, 1, 0)
            hi(0)
            norm_split_hi(N_MIX, 0)
            norm_split_hi(N_MIX, 1)
            hi(1)
            act.wait_ge(mem_loaded, 16)
            norm_square(N_MEM, mem_tok, 0, 1)
            norm_square(N_MEM, mem_tok, 1, 1)
            hi(2)
            norm_split_hi(N_MEM, 0, mem_h)
            norm_split_hi(N_MEM, 1, mem_h)
            hi(3)
            act.wait_ge(ang_ready, 1)
            act.activation(sincos[:, :, :, :].rearrange("p a t f -> p (a t f)"),
                           ang[:, :, :, :].rearrange("p a t f -> p (a t f)"), ACT.Sin).then_inc(sincos_ready, 1)
            act.wait_ge(rows_t, 1)
            act.activation(cols_a[:, :], tok(0)[:, 0:ROWS_A], ACT.Copy).then_inc(cols_ready, 1)
            act.activation(cols_b[:, :], tok(0)[:, P:P + 4 * CONV_W], ACT.Copy).then_inc(cols_ready, 1)
            act.activation(ws_t[:, :, :].rearrange("p g t -> p (g t)"), tok(1), ACT.Copy).then_inc(cols_ready, 1)
            used_slab(1)
            act.activation(sig1[:, :, :].rearrange("p a n -> p (a n)"), feat(1), ACT.Sigmoid).then_inc(sig_ready, 1)
            hi(4)
            hi(5)
            used_slab(3)
            act.wait_ge(u_ready, 1)
            act.activation(sig1[:, :, :].rearrange("p a n -> p (a n)"), feat(3), ACT.Sigmoid).then_inc(sig_ready, 1)
            hi(6)
            hi(7)
            used_slab(I_QK + 1)
            for tb in range(TB):
                act.activation(qk[:, tb, :], tok(tb), ACT.Copy).then_inc(qk_ready, 1)
            hi(8)
            hi(9)
            used_slab(I_RV + 1)
            for tb in range(TB):
                act.activation(rv[:, tb, :], tok(2 + tb), ACT.Copy).then_inc(rv_ready, 1)
            hi(10)
            hi(11)
            for b in range(2):
                act.wait_ge(qk_t, b + 1)
                act.activation(qkT[:, 2 * b:2 * b + 2, :], blocks(tok(b)), ACT.Copy).then_inc(qkT_ready, 1)

            def decay(hd):
                if hd >= 2:
                    act.wait_ge(s_dec_ready, hd - 1)
                act.activation(dec[:, hd % 2, :], dist[:, :], ACT.Exp, scale=float(LOG_G[hd])).then_inc(dec_ready, 1)

            decay(0)
            decay(1)
            used_slab(I_RG)
            act.activation(rgs[:, 0:2, :], blocks(feat(0)), ACT.Silu).then_inc(rg_ready, 1)
            hi(12)
            for hd in range(2, 4):
                decay(hd)
            used_slab(I_RG + 1)
            act.activation(rgs[:, 2:4, :], blocks(feat(1)), ACT.Silu).then_inc(rg_ready, 1)
            hi(13)
            for hd in range(4, RET_HEADS):
                decay(hd)

            def keys(i, j, bank):
                used_slab(i + j)
                act.activation(kT[:, 2 * j:2 * j + 2, :], blocks(feat(bank)), ACT.Copy).then_inc(k_ready, 1)

            def values(i):
                used_slab(i + 3)
                for m in range(2):
                    for half in range(2):
                        act.activation(vm[:, m, half * HALF:(half + 1) * HALF], tok(2 * m + half), ACT.Copy).then_inc(v_ready, 1)

            keys(I_K1, 0, 0)
            hi(14)
            keys(I_K1, 1, 1)
            hi(15)
            act.wait_ge(ry_centred, 1)
            act.activation(ry_sq[:, :, :], ry[:, :, :], ACT.Square).then_inc(ry_squared, 1)
            keys(I_K1, 2, 0)
            hi(16)
            keys(I_K1, 3, 1)
            hi(17)
            act.wait_ge(ret_ready, 1)
            used_slab(I_RG + 1)
            act.activation(xh[:, 4:8, :], retT[:, :, :], ACT.Copy).then_inc(ret_hi, 1)
            hi(18)
            hi(19)
            hi(20)
            act.wait_ge(ret_lo, 1)
            values(I_V1)
            hi(21)
            hi(22)
            act.wait_ge(conv_centred, 1)
            act.activation(c_sq[:, :, :], c_acc[:, :, :], ACT.Square).then_inc(conv_squared, 1)
            hi(23)
            act.wait_ge(conv_normed, 1)
            for c in range(4):
                ins = act.activation(c_out[:, c, :], c_acc[:, c, :], ACT.Silu, bias=cols_a[:, ROW_OF["conv_ln_b"] + c:ROW_OF["conv_ln_b"] + c + 1],
                                     scale=cols_a[:, ROW_OF["conv_ln_w"] + c:ROW_OF["conv_ln_w"] + c + 1])
                ins.then_inc(conv_out, 1)
            act.wait_ge(conv_out, 4)
            act.activation(xh[:, 0:4, :], c_out[:, :, :], ACT.Copy).then_inc(conv_hi, 1)
            h_square(N_XA, 0, UPD[I_OUT1], 2)
            hi(24)
            h_square(N_XA, 1, UPD[I_OUT1], 2)
            norm_split_hi(N_XA, 0)
            norm_split_hi(N_XA, 1)
            hi(25)

            def x_attention(b, i_q, i_o, split):
                def q(j):
                    used_slab(i_q + j)
                    act.activation(qT[:, 2 * j:2 * j + 2, :], blocks(feat(j)), ACT.Copy).then_inc(xq_ready, 1)
                    if split:
                        hi(i_o + j)

                def exps(hd):
                    for u in range(TB * hd, TB * hd + TB):
                        act.wait_ge(xmax_ready, 8 * b + u + 1)
                        act.activation(prob[:, u, :], tok(u % 4)[:, 0:NMEM], ACT.Exp, bias=xneg[:, u:u + 1], scale=XA_SCALE,
                                       accum_out=xsum[:, u:u + 1]).then_inc(xexp_ready, 1)

                def p_t(hd):
                    act.wait_ge(xp_t, 4 * b + hd + 1)
                    if hd >= 2:
                        act.wait_ge(xo_ready, 4 * b + hd - 1)
                    act.activation(probT[:, hd % 2, :, :], blocks(feat(hd)), ACT.Copy).then_inc(xpT_ready, 1)

                def out_hi(hd):
                    act.wait_ge(xo_ready, 4 * b + hd + 1)
                    act.activation(xh[:, 2 * hd:2 * hd + 2, :], blocks(feat(hd)), ACT.Copy).then_inc(xo_hi, 1)

                q(0)
                q(1)
                exps(0)
                q(2)
                exps(1)
                q(3)
                p_t(0)
                exps(2)
                out_hi(0)
                p_t(1)
                exps(3)
                out_hi(1)
                p_t(2)
                out_hi(2)
                p_t(3)
                out_hi(3)

            x_attention(0, I_Q1, I_O1, True)
            boundary(N_MLP, UPD[I_O1], 3, I_FF1)

            def mlp1(g, first=False, splits=True):
                step = 0 if first else 4 * g
                two = 0 if first else 2 * g
                for c in range(2):
                    act.wait_ge(slab_used, I_FF1 + c + 1 + step)
                    if not first:
                        act.wait_ge(ff_lo, two - 1 + c)
                    act.activation(ff_r[:, c, :], feat(c), ACT.Relu).then_inc(relu_ready, 1)
                    act.wait_ge(relu_ready, two + c + 1)
                    act.activation(ff_h[:, 2 * c:2 * c + 2, :], blocks(ff_r[:, c, :]), ACT.Square).then_inc(ff_hi, 1)
                    if splits:
                        hi(I_FF1 + 4 + c, step, 0 if first else g)
                if splits:
                    for c in range(2, 4):
                        hi(I_FF1 + 4 + c, step, 0 if first else g)

            mlp1(0, first=True)
            with act.Fori(1, G1 - 1) as g:
                mlp1(g)
            mlp1(G1 - 1, splits=False)
            hi(I_SBQK)
            hi(I_SBQK + 1)
            h_square(None, 0, UPD[I_FF1], 4)
            hi(I_SBQK + 2)
            h_square(None, 1, UPD[I_FF1], 4)
            for tb in range(TB):
                act.wait_ge(h_normed, tb + 1)
                norm_square(N_MIX2, h, tb, 5)
            norm_split_hi(N_MIX2, 0)
            norm_split_hi(N_MIX2, 1)
            hi(I_SBQK + 3)

            def sb_logs(p):
                act.wait_ge(sb_z, p + 1)
                z = ps[:, 0:2, 0:SB_COLS]
                if p > 0:
                    act.wait_ge(sb_arg, p)
                after(act.activation(sb_e[:, :, :], z, ACT.Abs))
                after(act.activation(sb_e[:, :, :], sb_e[:, :, :], ACT.Exp, scale=-1.0))
                act.activation(sb_l[:, :, :], sb_e[:, :, :], ACT.Ln, bias=1.0).then_inc(sb_log, 1)

            def sb_exps(p):
                act.wait_ge(sb_arg, p + 1)
                if p > 0:
                    act.wait_ge(sb_out, p)
                act.activation(sb_a[:, :, :], sb_e[:, :, :], ACT.Exp).then_inc(sb_exp, 1)

            def sb_split(p):
                act.wait_ge(sb_out, p + 1)
                act.activation(y_h[0][:, p, :], tok(0)[:, 0:S], ACT.Copy).then_inc(sb_hi, 1)

            SB_AT = {}
            for p in range(4):
                SB_AT[SB_START + 5 * p + 1] = lambda p=p: sb_logs(p)
                SB_AT[SB_START + 5 * p + 2] = lambda p=p: sb_exps(p)
                SB_AT[SB_START + 5 * p + 4] = lambda p=p: sb_split(p)

            def beside(i):
                if i in SB_AT:
                    SB_AT[i]()

            for j in range(4):
                used_slab(I_SBQK + j)
                act.activation(qkT2[:, 2 * j:2 * j + 2, :], blocks(feat(j)), ACT.Copy,
                               scale=SB_DIM ** -0.5 if j < 2 else 1.0).then_inc(sbqk_ready, 1)
                hi(I_SBQK + 4 + j)
            used_slab(I_SBV + 1)
            for tb in range(TB):
                act.activation(v2[:, tb, :], tok(tb), ACT.Copy).then_inc(sbv_ready, 1)
            hi(I_SBV + 4)
            hi(I_SBV + 5)
            for j in range(2):
                used_slab(I_ZU + j)
                act.activation(ug[:, 2 * j:2 * j + 2, :], blocks(feat(j)), ACT.Gelu).then_inc(ug_ready, 1)
                hi(I_ZU + 4 + j)
            used_slab(I_ZV + 1)
            for tb in range(TB):
                act.activation(vg[:, tb, :], tok(2 + tb), ACT.Gelu).then_inc(vg_ready, 1)
            hi(I_ZV + 4)
            hi(I_ZV + 5)
            for j in range(2):
                used_slab(I_C3 + 2 * j)
                if j:
                    act.wait_ge(y3_ready, 1)
                act.activation(cc_s[:, :, :], blocks(feat(2 - 2 * j)), ACT.Copy).then_inc(cc_ready, 1)
                hi(I_C3 + 2 * j + 4)
                beside(I_C3 + 2 * j)
                hi(I_C3 + 2 * j + 5)
                beside(I_C3 + 2 * j + 1)
            for j in range(2):
                hi(I_C3 + 8 + j)
                beside(I_C3 + 4 + j)
            act.wait_ge(yb_ready, 2)
            act.activation(y_h[1][:, :, :], ug[:, :, :], ACT.Copy).then_inc(yb_hi, 1)
            act.wait_ge(yc_ready, 2)
            act.activation(y_h[2][:, :, :], acc3[:, :, :], ACT.Copy).then_inc(yc_hi, 1)
            for n in range(BRANCHES):
                for half in range(2):
                    i = I_BR + 6 * n + 3 * half
                    r = 2 * n + half
                    for j in range(2):
                        used_slab(i + j)
                        if r > 0:
                            act.wait_ge(merge_done, r)
                        act.activation(sig2[:, 2 * j:2 * j + 2, :], blocks(feat(j)), ACT.Sigmoid).then_inc(gate_ready, 1)
                        hi(i + j + 4)
                        beside(i + j)
                    hi(i + 6)
                    beside(i + 2)
                    if r == 3:
                        act.wait_ge(mem2_loaded, 16)
                        act.wait_ge(sb_out, 4)
                        for tb in range(TB):
                            norm_square(N_MEM2, mem2_tok, tb, 6, mem2_sq)
                    if r == 4:
                        act.wait_ge(yb_lo, 1)
                        norm_split_hi(N_MEM2, 0, mem2_h)
                        norm_split_hi(N_MEM2, 1, mem2_h)
            used_slab(I_BR + 16)
            for half in range(2):
                act.wait_ge(merge_done, 5 + half)
                act.activation(xh[:, 4 * half:4 * half + 4, :], merged[:, 4 * half:4 * half + 4, :], ACT.Copy).then_inc(merged_hi, 1)
            hi(I_K2)
            hi(I_K2 + 1)
            h_square(N_XA2, 0, UPD[I_OUT2], 7)
            hi(I_K2 + 2)
            h_square(N_XA2, 1, UPD[I_OUT2], 7)
            hi(I_K2 + 3)
            keys(I_K2, 0, 0)
            hi(I_K2 + 4)
            keys(I_K2, 1, 1)
            hi(I_K2 + 5)
            norm_split_hi(N_XA2, 0)
            norm_split_hi(N_XA2, 1)
            keys(I_K2, 2, 2)
            hi(I_K2 + 6)
            keys(I_K2, 3, 3)
            hi(I_K2 + 7)
            for j in range(4):
                hi(I_V2 + 4 + j)
                if j == 3:
                    values(I_V2)
            x_attention(1, I_Q2, I_O2, True)
            boundary(N_FF2, UPD[I_O2], 8, I_FF2, places=2)

            def glu(g, i, first=False, last=False, step=0, turn=0):
                act.wait_ge(slab_used, i + 1 + step)
                if not first:
                    act.wait_ge(glu_ready, g)
                act.activation(ff_r[:, 0, :], feat(0), ACT.Silu).then_inc(silu_ready, 1)
                nxt = ff2_gate(1) if first else i + 3
                if not last:
                    hi(nxt, step, turn)
                    hi(nxt + 1, step, turn)
                if not first:
                    act.wait_ge(slab_used, i + 3 + step)
                act.wait_ge(glu_ready, g + 1)
                act.activation(ff_h[:, 0:2, :], blocks(ff_u[:, 0, :]), ACT.Copy).then_inc(glu_hi, 1)
                hi(N_SLABS - 1 if last else nxt + 2, step, turn)

            glu(0, I_FF2, first=True)
            glu(1, ff2_gate(1))
            with act.Fori(0, G2 - 3) as t:
                glu(t + 2, ff2_gate(2), step=3 * t, turn=t)
            glu(G2 - 1, ff2_gate(G2 - 1), last=True)
            for tb in range(TB):
                h_square(None, tb, UPD[I_FF2], 9)

        @block.vector
        def _(dve):
            count = [0]

            def after(ins):
                count[0] += 1
                ins.then_inc(dve_step, 1)
                dve.wait_ge(dve_step, count[0])

            def lo(i, step=0):
                s = PLACE[i]
                dve.wait_ge(hi_done, i + 1 + step)
                dve.tensor_tensor(w_lo[:, s, :], w_ring[:, s, :], w_hi[:, s, :].bitcast(F32), ALU.subtract).then_inc(lo_done, 1)

            def rsqrt(v, y, t):
                after(dve.tensor_scalar(y.bitcast(I32), v.bitcast(I32), -0.5, RSQRT_MAGIC, ALU.mult, ALU.add))
                for _ in range(3):
                    after(dve.tensor_tensor(t, y, y, ALU.mult))
                    after(dve.scalar_tensor_tensor(t, t, -0.5, v, ALU.mult, ALU.mult))
                    after(dve.scalar_tensor_tensor(y, t, 1.5, y, ALU.add, ALU.mult))

            def scale_rows(tb, src, dst, g, use, sq_done):
                dve.wait_ge(norm_sq, sq_done)
                c = slice(2 * use + tb, 2 * use + tb + 1)
                v, y, t = nv[:, tb:tb + 1], ny[:, tb:tb + 1], nt[:, tb:tb + 1]
                after(dve.tensor_scalar(v, sq_sum[:, c], 1.0 / D, EPS, ALU.mult, ALU.add))
                rsqrt(v, y, t)
                dve.wait_ge(gain_loaded[g % 2], 16 * (g // 2 + 1))
                return dve.scalar_tensor_tensor(dst[:, tb, :], src[:, tb, :], y, gain[:, g % 2, :], ALU.mult, ALU.mult)

            def norm_scale(n, tb, src=h, use=None, dst=xn):
                use = n if use is None else use
                ins = scale_rows(tb, src, dst, GAIN_OF[n], use, 2 * use + tb + 1)
                ins.then_inc(norm_xn, 1)
                if tb == TB - 1:
                    dve.wait_ge(norm_xn, 2 * n + 2)
                    dve.sem_inc(gain_used, 1)

            def norm_split_lo(n, tb, hi_t=xh, lo_t=xl):
                for half in range(2):
                    dve.wait_ge(norm_hi, 4 * n + 2 * tb + half + 1)
                    f, t = slice(4 * half, 4 * half + 4), slice(tb * P, (tb + 1) * P)
                    dve.tensor_tensor(lo_t[:, f, t], tok(2 * tb + half).rearrange("p (f t) -> p f t", t=P),
                                      hi_t[:, f, t].bitcast(F32), ALU.subtract).then_inc(norm_lo, 1)

            def update(upd, last_slab):
                def block_of(tb):
                    if tb == 0:
                        dve.wait_ge(tb0_done, upd + 1)
                    else:
                        dve.wait_ge(slab_used, last_slab + 1)
                    for half in range(2):
                        c = slice(half * HALF, (half + 1) * HALF)
                        dve.tensor_tensor(h[:, tb, c], tok(2 * tb + half), h[:, tb, c], ALU.add).then_inc(h_updated, 1)
                return block_of

            def boundary(n, upd, last_slab, use, nxt, places=4):
                add = update(upd, last_slab)
                lo(nxt)
                lo(nxt + 1)
                add(0)
                norm_scale(n, 0, use=use)
                if places == 4:
                    lo(nxt + 2)
                add(1)
                norm_scale(n, 1, use=use)
                norm_split_lo(n, 0)
                norm_split_lo(n, 1)
                if places == 4:
                    lo(nxt + 3)

            norm_scale(N_MIX, 0)
            norm_scale(N_MIX, 1)
            lo(0)
            norm_split_lo(N_MIX, 0)
            norm_split_lo(N_MIX, 1)
            lo(1)
            dve.wait_ge(norm_t, 2)
            norm_scale(N_MEM, 0, mem_tok)
            norm_scale(N_MEM, 1, mem_tok)
            lo(2)
            norm_split_lo(N_MEM, 0, mem_h, mem_l)
            norm_split_lo(N_MEM, 1, mem_h, mem_l)
            lo(3)
            dve.wait_ge(pos_loaded, 16)
            dve.wait_ge(freq_ready, ROPE_HALF)
            after(dve.tensor_copy(pos_f[:, :], pos_i[:, :]))
            sin_a, cos_a = ang[:, 0, :, :], ang[:, 1, :, :]
            shape = [P, TB, ROPE_HALF]
            after(dve.tensor_tensor(sin_a, pos_f[:, :].unsqueeze(2).broadcast_to(shape), freq[:, :].unsqueeze(1).broadcast_to(shape), ALU.mult))
            after(dve.tensor_scalar(turns[:, :, :], sin_a, 1.0 / (2 * PI), ROUND, ALU.mult, ALU.add))
            after(dve.tensor_scalar(turns[:, :, :], turns[:, :, :], ROUND, None, ALU.subtract))
            for part in (TWO_PI_A, TWO_PI_B, TWO_PI_C):
                after(dve.scalar_tensor_tensor(sin_a, turns[:, :, :], -part, sin_a, ALU.mult, ALU.add))
            after(dve.tensor_scalar(sin_a, sin_a, SIN_MAX, -SIN_MAX, ALU.min, ALU.max))
            after(dve.scalar_tensor_tensor(cos_a, sin_a, -1.0, sin_a, ALU.mult, ALU.max))
            dve.tensor_scalar(cos_a, cos_a, -1.0, PI / 2, ALU.mult, ALU.add).then_inc(ang_ready, 1)
            dve.wait_ge(dist_ready, 1)
            after(dve.tensor_copy(dist[:, :], dist_i[:, :]))
            after(dve.scalar_tensor_tensor(dist[:, :], dist[:, :], -1.0, dist[:, :], ALU.mult, ALU.max))
            after(dve.memset(dist[CHUNK:P, 0:CHUNK], FAR))

            def gate_conv(j):
                dve.wait_ge(sig_ready, j + 1)
                dve.wait_ge(pad_ready, 1)
                dve.tensor_tensor(u_pad[:, 2 * j:2 * j + 2, CONV_W - 1:], blocks(feat(2 * j)), sig1[:, :, :], ALU.mult).then_inc(u_ready, 1)

            done = [0]

            def conv(n):
                for m in range(done[0], min(done[0] + n, CONV_W * 4)):
                    k, c = divmod(m, 4)
                    if m == 0:
                        dve.wait_ge(u_ready, 2)
                        dve.wait_ge(cols_ready, 2)
                    tap, win = cols_b[:, m:m + 1], u_pad[:, c, k:k + S]
                    if k == 0:
                        bias = cols_a[:, ROW_OF["conv_b"] + c:ROW_OF["conv_b"] + c + 1]
                        ins = dve.tensor_scalar(c_acc[:, c, :], win, tap, bias, ALU.mult, ALU.add)
                    else:
                        dve.wait_ge(conv_step, m - 3)
                        ins = dve.scalar_tensor_tensor(c_acc[:, c, :], win, tap, c_acc[:, c, :], ALU.mult, ALU.add)
                    ins.then_inc(conv_step, 1)
                    done[0] = m + 1

            gate_conv(0)
            lo(4)
            lo(5)
            gate_conv(1)
            lo(6)
            lo(7)
            conv(12)
            dve.wait_ge(sincos_ready, 1)
            dve.wait_ge(qk_ready, 2)
            for tb in range(TB):
                view = qk[:, tb, :].rearrange("p (g e f) -> p g e f", e=2, f=ROPE_HALF)
                res = qkr[:, tb, :].rearrange("p (g e f) -> p g e f", e=2, f=ROPE_HALF)
                t = [rope_t[:, j, :].rearrange("p (g f) -> p g f", f=ROPE_HALF) for j in range(4)]
                sin, cos = (sincos[:, e, tb, :].unsqueeze(1).broadcast_to([P, 2 * RET_HEADS, ROPE_HALF]) for e in range(2))
                dve.tensor_tensor(t[0], view[:, :, 0, :], cos, ALU.mult)
                dve.tensor_tensor(t[1], view[:, :, 1, :], sin, ALU.mult)
                dve.tensor_tensor(t[2], view[:, :, 0, :], sin, ALU.mult)
                after(dve.tensor_tensor(t[3], view[:, :, 1, :], cos, ALU.mult))
                dve.tensor_tensor(res[:, :, 0, :], t[0], t[1], ALU.subtract)
                after(dve.tensor_tensor(res[:, :, 1, :], t[2], t[3], ALU.add))
                dve.sem_inc(rope_ready, 1)
            lo(8)
            lo(9)
            conv(8)
            lo(10)
            lo(11)
            conv(8)

            def ret_decay(hd):
                dve.wait_ge(ret_s, hd + 1)
                dve.wait_ge(dec_ready, hd + 1)
                if hd >= 2:
                    dve.wait_ge(ret_pv, hd - 1)
                sc = RET_DK ** -0.5
                dve.scalar_tensor_tensor(s_dec[:, hd % 2, 0:S], tok(hd % 4)[:, 0:S], sc, dec[:, hd % 2, :], ALU.mult, ALU.mult)
                after(dve.scalar_tensor_tensor(s_dec[:, hd % 2, S:S + P], tok(hd % 4)[:, S:S + P], sc, dec[:, hd % 2, 0:P], ALU.mult, ALU.mult))
                dve.sem_inc(s_dec_ready, 1)

            ret_decay(0)
            ret_decay(1)
            lo(12)
            conv(6)
            ret_decay(2)
            ret_decay(3)
            lo(13)
            conv(4)
            for hd in range(4, RET_HEADS):
                ret_decay(hd)
            lo(14)
            dve.wait_ge(ret_pv, RET_HEADS)
            heads = [feat(2 + tb).rearrange("p (g e) -> p g e", e=RET_DV) for tb in range(TB)]
            H8 = [slice(RET_HEADS * tb, RET_HEADS * (tb + 1)) for tb in range(TB)]
            dve.tensor_reduce(r_mean[:, H8[0]], heads[0], AX_X, ALU.add)
            after(dve.tensor_reduce(r_mean[:, H8[1]], heads[1], AX_X, ALU.add))
            after(dve.tensor_scalar(r_mean, r_mean, -1.0 / RET_DV, None, ALU.mult))
            for tb in range(TB):
                after(dve.tensor_tensor(ry[:, tb, :].rearrange("p (g e) -> p g e", e=RET_DV), heads[tb],
                                        r_mean[:, H8[tb]].unsqueeze(2).broadcast_to([P, RET_HEADS, RET_DV]), ALU.add))
            dve.sem_inc(ry_centred, 1)
            conv(4)
            lo(15)
            dve.wait_ge(ry_squared, 1)
            all_heads = [x[:, :, :].rearrange("p t (g e) -> p (t g) e", e=RET_DV) for x in (ry, ry_sq)]
            after(dve.tensor_reduce(r_var, all_heads[1], AX_X, ALU.add))
            after(dve.tensor_scalar(r_var, r_var, 1.0 / RET_DV, EPS, ALU.mult, ALU.add))
            rsqrt(r_var, r_y, r_t)
            dve.tensor_tensor(all_heads[0], all_heads[0], r_y.unsqueeze(2).broadcast_to([P, 2 * RET_HEADS, RET_DV]), ALU.mult).then_inc(ry_ready, 1)
            conv(8)
            lo(16)
            dve.wait_ge(ry_t, 1)
            for f in range(4):
                w = cols_a[:, ROW_OF["ret_gn_w"] + f:ROW_OF["ret_gn_w"] + f + 1]
                ins = dve.scalar_tensor_tensor(retT[:, f, :], tok(2 + f // 2)[:, (f % 2) * S:(f % 2 + 1) * S], w, rgs[:, f, :], ALU.mult, ALU.mult)
            ins.then_inc(ret_ready, 1)
            conv(6)
            lo(17)
            dve.wait_ge(ret_hi, 1)
            dve.tensor_tensor(xl[:, 4:8, :], retT[:, :, :], xh[:, 4:8, :].bitcast(F32), ALU.subtract).then_inc(ret_lo, 1)
            for i in range(18, 21):
                lo(i)
                conv(10)
            conv(CONV_W * 4)
            lo(21)
            dve.wait_ge(conv_mean, 1)
            for c in range(4):
                ins = dve.scalar_tensor_tensor(c_acc[:, c, :], feat(2)[:, 0:S], -1.0 / HALF, c_acc[:, c, :], ALU.mult, ALU.add)
                after(ins)
            dve.sem_inc(conv_centred, 1)
            lo(22)
            dve.wait_ge(conv_var, 1)
            after(dve.tensor_scalar(n_v[:, :], feat(3)[:, 0:S], 1.0 / HALF, EPS, ALU.mult, ALU.add))
            rsqrt(n_v[:, :], n_y[:, :], n_t[:, :])
            dve.tensor_tensor(c_acc[:, :, :], c_acc[:, :, :], n_y[:, :].unsqueeze(1).broadcast_to([P, 4, S]), ALU.mult).then_inc(conv_normed, 1)
            lo(23)
            dve.wait_ge(conv_hi, 1)
            dve.tensor_tensor(xl[:, 0:4, :], c_out[:, :, :], xh[:, 0:4, :].bitcast(F32), ALU.subtract).then_inc(conv_lo, 1)
            add = update(UPD[I_OUT1], I_OUT1 + 3)
            add(0)
            norm_scale(N_XA, 0)
            lo(24)
            add(1)
            norm_scale(N_XA, 1)
            norm_split_lo(N_XA, 0)
            norm_split_lo(N_XA, 1)
            lo(25)

            def x_attention(b, i_o):
                def maxima(hd):
                    for u in range(TB * hd, TB * hd + TB):
                        dve.wait_ge(xs_ready, 8 * b + u + 1)
                        after(dve.tensor_reduce(xmax[:, u:u + 1], tok(u % 4)[:, 0:NMEM], AX_X, ALU.max))
                        dve.tensor_scalar(xneg[:, u:u + 1], xmax[:, u:u + 1], -XA_SCALE, None, ALU.mult).then_inc(xmax_ready, 1)

                def normalise(hd):
                    for u in range(TB * hd, TB * hd + TB):
                        dve.wait_ge(xexp_ready, 8 * b + u + 1)
                        after(dve.reciprocal(xinv[:, u:u + 1], xsum[:, u:u + 1]))
                        dve.tensor_scalar(prob[:, u, :], prob[:, u, :], xinv[:, u:u + 1], None, ALU.mult).then_inc(xp_ready, 1)

                def out_lo(hd):
                    dve.wait_ge(xo_hi, 4 * b + hd + 1)
                    f = slice(2 * hd, 2 * hd + 2)
                    dve.tensor_tensor(xl[:, f, :], blocks(feat(hd)), xh[:, f, :].bitcast(F32), ALU.subtract).then_inc(xo_lo, 1)

                lo(i_o)
                lo(i_o + 1)
                maxima(0)
                normalise(0)
                lo(i_o + 2)
                maxima(1)
                normalise(1)
                lo(i_o + 3)
                maxima(2)
                normalise(2)
                out_lo(0)
                maxima(3)
                normalise(3)
                for hd in range(1, XA_HEADS):
                    out_lo(hd)

            x_attention(0, I_O1)
            boundary(N_MLP, UPD[I_O1], I_O1 + 3, 3, I_FF1)

            def mlp1(g, first=False, splits=True):
                step = 0 if first else 4 * g
                two = 0 if first else 2 * g
                for c in range(2):
                    dve.wait_ge(relu_ready, two + c + 1)
                    dve.tensor_tensor(ff_u[:, c, :], ff_r[:, c, :], ff_r[:, c, :], ALU.mult).then_inc(relu_sq, 1)
                    dve.wait_ge(relu_sq, two + c + 1)
                    dve.wait_ge(ff_hi, two + c + 1)
                    f = slice(2 * c, 2 * c + 2)
                    dve.tensor_tensor(ff_l[:, f, :], blocks(ff_u[:, c, :]), ff_h[:, f, :].bitcast(F32), ALU.subtract).then_inc(ff_lo, 1)
                    if splits:
                        lo(I_FF1 + 4 + c, step)
                if splits:
                    for c in range(2, 4):
                        lo(I_FF1 + 4 + c, step)

            mlp1(0, first=True)
            with dve.Fori(1, G1 - 1) as g:
                mlp1(g)
            mlp1(G1 - 1, splits=False)
            add = update(UPD[I_FF1], I_SBQK - 1)
            lo(I_SBQK)
            lo(I_SBQK + 1)

            def last_norm(tb):
                after(scale_rows(tb, h, h, GAIN_F, 4, 8 + tb + 1))
                dve.sem_inc(h_normed, 1)
                if tb == TB - 1:
                    dve.sem_inc(gain_used, 1)

            add(0)
            last_norm(0)
            lo(I_SBQK + 2)
            add(1)
            last_norm(1)
            norm_scale(N_MIX2, 0, use=5)
            norm_scale(N_MIX2, 1, use=5)
            norm_split_lo(N_MIX2, 0)
            norm_split_lo(N_MIX2, 1)
            lo(I_SBQK + 3)
            for i in range(I_SBQK + 4, I_SBQK + 12):
                lo(i)

            def sb_mask(x):
                v = x[:, :, :].rearrange("p e (b t) -> p e b t", t=P)[:, :, 0:3:2, :]
                m = earlier[:, :].unsqueeze(1).unsqueeze(1).broadcast_to([P, 2, 2, P])
                return dve.tensor_tensor(v, v, m, ALU.mult)

            z = ps[:, 0:2, 0:SB_COLS]

            def sb_penalty(p):
                dve.wait_ge(sb_log, p + 1)
                dve.wait_ge(const_ready, 4)
                if p > 0:
                    dve.wait_ge(sb_cum, p)
                after(dve.scalar_tensor_tensor(sb_m[:, :, :], z, 0.0, sb_l[:, :, :], ALU.max, ALU.add))
                after(sb_mask(sb_m))
                dve.sem_inc(sb_pen, 1)
                after(dve.scalar_tensor_tensor(sb_e[:, :, :], z, 0.0, sb_l[:, :, :], ALU.min, ALU.subtract))

            def sb_argument(p):
                dve.wait_ge(sb_cum, p + 1)
                dve.tensor_tensor(sb_e[:, :, :], sb_e[:, :, :], ps[:, 2:4, 0:SB_COLS], ALU.subtract).then_inc(sb_arg, 1)

            def sb_masked(p):
                dve.wait_ge(sb_exp, p + 1)
                sb_mask(sb_a).then_inc(sb_prob, 1)

            def sb_split(p):
                dve.wait_ge(sb_hi, p + 1)
                dve.tensor_tensor(y_l[0][:, p, :], tok(0)[:, 0:S], y_h[0][:, p, :].bitcast(F32), ALU.subtract).then_inc(sb_lo, 1)

            SB_AT = {}
            for p in range(4):
                SB_AT[SB_START + 5 * p + 1] = lambda p=p: sb_penalty(p)
                SB_AT[SB_START + 5 * p + 2] = lambda p=p: sb_argument(p)
                SB_AT[SB_START + 5 * p + 3] = lambda p=p: sb_masked(p)
                SB_AT[SB_START + 5 * p + 4] = lambda p=p: sb_split(p)

            def beside(i):
                if i in SB_AT:
                    SB_AT[i]()

            dve.wait_ge(sgu_loaded, 48)
            for tb in range(TB):
                dve.wait_ge(vg_ready, tb + 1)
                six, two = bn6[:, 6 * tb:6 * tb + 6], bn2[:, 2 * tb:2 * tb + 2]
                v, y, t = nv[:, tb:tb + 1], ny[:, tb:tb + 1], nt[:, tb:tb + 1]
                after(dve.bn_stats(six, vg[:, tb, :]))
                after(dve.bn_aggr(two, six))
                after(dve.tensor_scalar(v, two[:, 1:2], LN_EPS, None, ALU.add))
                rsqrt(v, y, t)
                after(dve.tensor_scalar(vg[:, tb, :], vg[:, tb, :], two[:, 0:1], y, ALU.subtract, ALU.mult))
                after(dve.tensor_tensor(vg[:, tb, :], vg[:, tb, :], ln_g[:, :], ALU.mult))
                dve.tensor_tensor(vg[:, tb, :], vg[:, tb, :], ln_b[:, :], ALU.add).then_inc(vn_ready, 1)
            lo(I_ZV + 4)
            lo(I_ZV + 5)
            beside(I_ZV + 2)
            tap3 = ROW_OF["conv_w_2"]
            for j in range(2):
                lo(I_C3 + 2 * j + 4)
                if j:
                    beside(I_C3 + 2)
                dve.wait_ge(cc_ready, j + 1)
                dve.wait_ge(pad3_ready, 1)
                dve.wait_ge(slab_used, I_C3 + 2 * j + 2)
                dve.tensor_tensor(y3_pad[:, 2 * j:2 * j + 2, CONV3 - 1:], blocks(feat(3 - 2 * j)), cc_s[:, :, :], ALU.mult).then_inc(y3_ready, 1)
                lo(I_C3 + 2 * j + 5)
                beside(I_C3 + 2 * j + 1)
            dve.wait_ge(y3_ready, 2)
            for k in range(CONV3):
                for c in range(4):
                    tap, win = cols_a[:, tap3 + 4 * k + c:tap3 + 4 * k + c + 1], y3_pad[:, c, k:k + S]
                    if k == 0:
                        ins = dve.tensor_scalar(acc3[:, c, :], win, tap, None, ALU.mult)
                    else:
                        ins = dve.scalar_tensor_tensor(acc3[:, c, :], win, tap, acc3[:, c, :], ALU.mult, ALU.add)
                    if c == 3:
                        after(ins)
            for j in range(2):
                lo(I_C3 + 8 + j)
                beside(I_C3 + 4 + j)
                dve.wait_ge(slab_used, I_C3 + 5 + j)
                dve.tensor_tensor(acc3[:, 2 * j:2 * j + 2, :], blocks(feat(2 + j)), acc3[:, 2 * j:2 * j + 2, :], ALU.mult).then_inc(yc_ready, 1)
            dve.wait_ge(sgu_mixed, 1)
            dve.wait_ge(ug_ready, 2)
            for j in range(2):
                g = slice(2 * j, 2 * j + 2)
                mixed = feat(j).rearrange("p (g b t) -> p g b t", g=2, t=P)
                after(dve.tensor_tensor(vg[:, j, :].rearrange("p (g b t) -> p g b t", g=2, t=P), mixed,
                                        b_sp[:, g, :].unsqueeze(2).broadcast_to([P, 2, TB, P]), ALU.add))
                dve.tensor_tensor(ug[:, g, :], blocks(vg[:, j, :]), ug[:, g, :], ALU.mult).then_inc(yb_ready, 1)
            dve.wait_ge(yb_hi, 1)
            dve.tensor_tensor(y_l[1][:, :, :], ug[:, :, :], y_h[1][:, :, :].bitcast(F32), ALU.subtract).then_inc(yb_lo, 1)
            dve.wait_ge(yc_hi, 1)
            dve.tensor_tensor(y_l[2][:, :, :], acc3[:, :, :], y_h[2][:, :, :].bitcast(F32), ALU.subtract).then_inc(yc_lo, 1)
            for n in range(BRANCHES):
                for half in range(2):
                    i = I_BR + 6 * n + 3 * half
                    r = 2 * n + half
                    for j in range(2):
                        lo(i + j + 4)
                        beside(i + j)
                    lo(i + 6)
                    dve.wait_ge(gate_ready, 2 * r + 2)
                    dve.wait_ge(slab_used, i + 3)
                    m = merged[:, 4 * half:4 * half + 4, :]
                    if n == 0:
                        for j in range(2):
                            ins = dve.tensor_tensor(m[:, 2 * j:2 * j + 2, :], blocks(feat(2 + j)), sig2[:, 2 * j:2 * j + 2, :], ALU.mult)
                            after(ins)
                    else:
                        for j in range(2):
                            s2 = sig2[:, 2 * j:2 * j + 2, :]
                            after(dve.tensor_tensor(s2, blocks(feat(2 + j)), s2, ALU.mult))
                        after(dve.tensor_tensor(m, m, sig2[:, :, :], ALU.add))
                    dve.sem_inc(merge_done, 1)
                    beside(i + 2)
                    if r == 3:
                        norm_scale(N_MEM2, 0, mem2_tok, 6, mem2_tok)
                        norm_scale(N_MEM2, 1, mem2_tok, 6, mem2_tok)
                    if r == 4:
                        norm_split_lo(N_MEM2, 0, mem2_h, mem2_l)
                        norm_split_lo(N_MEM2, 1, mem2_h, mem2_l)
            for half in range(2):
                dve.wait_ge(merged_hi, half + 1)
                f = slice(4 * half, 4 * half + 4)
                dve.tensor_tensor(xl[:, f, :], merged[:, f, :], xh[:, f, :].bitcast(F32), ALU.subtract).then_inc(merged_lo, 1)
            add = update(UPD[I_OUT2], I_OUT2 + 3)
            lo(I_K2)
            lo(I_K2 + 1)
            add(0)
            norm_scale(N_XA2, 0, use=7)
            lo(I_K2 + 2)
            add(1)
            norm_scale(N_XA2, 1, use=7)
            for i in range(I_K2 + 3, I_K2 + 6):
                lo(i)
            norm_split_lo(N_XA2, 0)
            norm_split_lo(N_XA2, 1)
            for i in range(I_K2 + 6, I_Q2 + 4):
                lo(i)
            x_attention(1, I_O2)
            boundary(N_FF2, UPD[I_O2], I_O2 + 3, 8, I_FF2, places=2)

            def glu(g, i, first=False, last=False, step=0):
                dve.wait_ge(silu_ready, g + 1)
                dve.wait_ge(slab_used, i + 2 + step)
                if not first:
                    dve.wait_ge(glu_lo, g)
                dve.tensor_tensor(ff_u[:, 0, :], feat(1), ff_r[:, 0, :], ALU.mult).then_inc(glu_ready, 1)
                nxt = ff2_gate(1) if first else i + 3
                if not last:
                    lo(nxt, step)
                    lo(nxt + 1, step)
                dve.wait_ge(glu_hi, g + 1)
                dve.tensor_tensor(ff_l[:, 0:2, :], blocks(ff_u[:, 0, :]), ff_h[:, 0:2, :].bitcast(F32), ALU.subtract).then_inc(glu_lo, 1)
                lo(N_SLABS - 1 if last else nxt + 2, step)

            glu(0, I_FF2, first=True)
            glu(1, ff2_gate(1))
            with dve.Fori(0, G2 - 3) as t:
                glu(t + 2, ff2_gate(2), step=3 * t)
            glu(G2 - 1, ff2_gate(G2 - 1), last=True)
            add = update(UPD[I_FF2], N_SLABS - 1)
            for tb in range(TB):
                add(tb)
            for tb in range(TB):
                scale_rows(tb, h, xn, GAIN_FINAL, 9, 18 + tb + 1).then_inc(out_ready, 1)


def kernel(**inputs):
    import concourse.bacc as bacc
    from concourse.bass_utils import run_bass_kernel_spmd

    nc = bacc.Bacc("TRN2", target_bir_lowering=False, num_devices=1)
    arrays, aps = {}, {}
    for name in INPUTS:
        x = np.ascontiguousarray(inputs[name])
        arrays[f"in_{name}"] = x
        aps[name] = nc.dram_tensor(f"in_{name}", x.shape, mybir.dt.from_np(x.dtype), kind="ExternalInput").ap()
    out = nc.dram_tensor("out", (1, S, D), F32, kind="ExternalOutput").ap()
    build(nc, aps, out)
    r = run_bass_kernel_spmd(nc, [arrays], core_ids=[0])
    return r.results[0]["out"]
```

```python
from contextlib import ExitStack

import numpy as np

import concourse.bass as bass
from concourse import mybir

F32 = mybir.dt.float32
F32R = mybir.dt.float32r
I32 = mybir.dt.int32
ACT = mybir.ActivationFunctionType
ALU = mybir.AluOpType
AX_X = mybir.AxisListType.X

P = 128
D = 1024
S = 256
TB = S // P
KD = D // P
HALF = D // 2
NMEM = 256
EPS = 1e-6
LN_EPS = 1e-5
SLAB = 2048
RING = 4

CONV_W = 31
RET_HEADS, RET_DK, RET_DV, CHUNK = 8, 32, 64, 64
ROPE_HALF = RET_DK // 2
XA_HEADS = 4
XA_SCALE = float(D // XA_HEADS) ** -0.5
D_FF = 4 * D
SB_HEADS, SB_DIM = 8, 64
SB_COLS = S + P
SGU_GROUPS = 4
CONV3 = 3
BRANCHES = 3
HID2 = 2816
G1 = D_FF // 512
G2 = HID2 // 256

LOG_G = np.log1p(-np.exp2(-5.0 - np.arange(RET_HEADS)))
INV_FREQ = (10000.0 ** (-np.arange(ROPE_HALF) / ROPE_HALF)).astype(np.float32)
FAR = 1.0e9
PI = float(np.pi)
TWO_PI_A = 6.28125
TWO_PI_B = float(np.float32(np.round((2 * np.pi - TWO_PI_A) * 2 ** 22) / 2 ** 22))
TWO_PI_C = float(2 * np.pi - TWO_PI_A - TWO_PI_B)
SIN_MAX = 3.1415925
ROUND = 12582912.0
RSQRT_MAGIC = 1597463007.0

I_CONV, I_QK, I_RV, I_RG = 0, 4, 6, 8
I_K1, I_V1 = 10, 14
I_OUT1 = 18
I_Q1, I_O1 = 22, 26
I_FF1 = 30
I_SBQK = I_FF1 + 4 * G1
I_SBV, I_ZU, I_ZV, I_C3, I_BR = I_SBQK + 4, I_SBQK + 6, I_SBQK + 8, I_SBQK + 10, I_SBQK + 16
I_OUT2 = I_BR + 6 * BRANCHES
I_K2, I_V2 = I_OUT2 + 4, I_OUT2 + 8
I_Q2, I_O2 = I_OUT2 + 12, I_OUT2 + 16
I_FF2 = I_OUT2 + 20
N_SLABS = I_FF2 + 3 * G2
BRANCH_ORDER = (1, 2, 0)

R_MIX, R_XA, R_MLP, R_MIX2, R_XA2, R_FF2 = range(6)
GAIN_COLS = ["norm_mix_w", "norm_xattn_w", "norm_mlp_w", "norm_mix_g_2", "norm_xa_g_2", "norm_ffn_g_2"]
G_MEM, G_F, G_MEM2, G_FINAL = range(4)
GAIN_ROWS = ["norm_mem_w", "norm_f_w", "mem_norm_g_2", "final_g_2"]
N_MEM, N_MEM2 = range(2)
Q_MIX, Q_MEM, Q_XA, Q_MLP, Q_F, Q_MIX2, Q_MEM2, Q_XA2, Q_FF2, Q_FINAL = range(10)


def slab_places():
    place, uses, before, last, count = [], [], [], {}, {}
    for i in range(N_SLABS):
        s = i % RING
        if i >= I_FF2:
            j = i - I_FF2
            s = j % RING if j < 5 else (1, 2, 3)[(j - 5) % 3]
            if i == N_SLABS - 1:
                s = 0
        place.append(s)
        uses.append(count.get(s, 0))
        before.append(last.get(s))
        count[s] = uses[-1] + 1
        last[s] = i
    return place, uses, before


PLACE, USES, BEFORE = slab_places()


ROW_OF = {"conv_b": 0, "conv_ln_w": 4, "conv_ln_b": 8, "ret_gn_w": 12, "conv_w_2": 16}
ROWS_A = 16 + 4 * CONV3
RET_COLS = S + P
TAPS_DVE = 16
OUT1_ORDER = (2, 3, 0, 1)
C3_COLS = [(5 + w) * HALF + 256 * j for j in range(2) for w in (1, 2)] + [5 * HALF, 5 * HALF + 256]
SB_START = I_ZV + 1
ARENA, ARENA_WORDS = 16512, 53184

INPUTS = ["x", "mem", "positions", "norm_mix_w", "w_in", "conv_w", "conv_b", "conv_ln_w", "conv_ln_b", "ret_gn_w", "w_out",
          "norm_xattn_w", "norm_mem_w", "xq_w", "xkv_w", "xo_w", "norm_mlp_w", "mlp_up_w", "mlp_down_w", "norm_f_w",
          "mem_2", "norm_mix_g_2", "w_in_2", "sgu_ln_g_2", "sgu_ln_b_2", "w_spatial_2", "b_spatial_2", "conv_w_2",
          "w_branch_2", "w_out_2", "norm_xa_g_2", "mem_norm_g_2", "w_q_xa_2", "w_k_xa_2", "w_v_xa_2", "w_o_xa_2",
          "norm_ffn_g_2", "w_gate_ffn_2", "w_up_ffn_2", "w_down_ffn_2", "final_g_2"]


def ff2_gate(g):
    return I_FF2 if g == 0 else I_FF2 + 3 * g - 1


def build(nc, a, out):
    with ExitStack() as ctx:
        arena = ctx.enter_context(nc.sbuf_tensor("arena", [P, ARENA_WORDS], F32))
        cursor = [0]

        def at(name, shape, off, dt=F32):
            assert off + int(np.prod(shape[1:])) <= ARENA_WORDS, (name, off)
            return nc.alloc_sbuf_tensor_at(name, shape, dt, offset=ARENA + 4 * off)

        def new(name, shape, dt=F32):
            t = at(name, shape, cursor[0], dt)
            cursor[0] += -(-int(np.prod(shape[1:])) // 8) * 8
            return t

        w_ring = new("w_ring", [P, RING, SLAB])
        w_hi = new("w_hi", [P, RING, SLAB], F32R)
        w_lo = new("w_lo", [P, RING, SLAB], F32R)
        h = new("h", [P, TB, D])
        xh = new("xh", [P, KD, S], F32R)
        xl = new("xl", [P, KD, S], F32R)
        xn0 = cursor[0]
        xn = new("xn", [P, TB, D])
        gain = new("gain", [P, D])
        r_row = new("r_row", [P, 2, S])
        diag = new("diag", [P, TB, P])
        cols_g = new("cols_g", [P, KD * len(GAIN_COLS)])
        ident = new("ident", [P, P])
        ones = new("ones", [P, P])
        later = new("later", [P, P])
        earlier = new("earlier", [P, P])
        cols_a = new("cols_a", [P, ROWS_A])
        cols_b = new("cols_b", [P, CONV_W * 4])
        stat = new("stat", [P, 256])
        ln_g = new("ln_g", [P, HALF])
        ln_b = new("ln_b", [P, HALF])
        b_sp = new("b_sp", [P, SGU_GROUPS, P])
        ws_t = new("ws_t", [P, SGU_GROUPS, P])
        kv0 = cursor[0]
        kT = new("kT", [P, KD, NMEM])
        vm = new("vm", [P, 2, D])
        split0 = cursor[0]
        mem_h = new("mem_h", [P, KD, NMEM], F32R)
        mem_l = new("mem_l", [P, KD, NMEM], F32R)
        t0 = cursor[0]

        u_pad = new("u_pad", [P, 4, CONV_W - 1 + S])
        c_acc = new("c_acc", [P, 4, S])
        c_tap = at("c_tap", [P, 2, S], xn0)
        c_rest = at("c_rest", [P, S], xn0 + 2 * S)
        rgs = new("rgs", [P, 4, S])
        mt0 = cursor[0]
        qkT = new("qkT", [P, 4, S])
        rv = new("rv", [P, TB, HALF])
        mem_tok = at("mem_tok", [P, 2, D], mt0)
        m1 = cursor[0]
        sig1 = at("sig1", [P, 2, S], m1)
        dist_i = at("dist_i", [P, S], kv0 + 2 * D, I32)
        rope_t = at("rope_t", [P, 4, 256], m1)
        dec = at("dec", [P, 2, S], m1)
        s_dec = at("s_dec", [P, 2, RET_COLS], m1 + 2 * S)
        n_v, n_y, n_t = (at(f"n_{x}", [P, S], m1 + S * i) for i, x in enumerate("vyt"))
        cursor[0] = m1 + 2 * S + 2 * RET_COLS
        dist = new("dist", [P, S])
        ang = new("ang", [P, 2, TB, ROPE_HALF])
        sincos = new("sincos", [P, 2, TB, ROPE_HALF])
        turns = new("turns", [P, TB, ROPE_HALF])
        pos_i = new("pos_i", [P, TB], I32)
        pos_f = new("pos_f", [P, TB])
        freq = new("freq", [P, ROPE_HALF])
        qk = at("qk", [P, TB, HALF], kv0 + 2 * D)
        ry = at("ry", [P, TB, HALF], kv0 + 2 * D)
        qkr = at("qkr", [P, TB, HALF], kv0 + 3 * D)
        ry_sq = at("ry_sq", [P, TB, HALF], kv0 + 3 * D)
        retT = at("retT", [P, 4, S], kv0 + 3 * D)
        c_sq = at("c_sq", [P, 4, S], t0)
        c_out = at("c_out", [P, 4, S], t0)
        rows_a = at("rows_a", [ROWS_A, P], kv0)
        rows_b = at("rows_b", [CONV_W * 4, P], kv0 + P)
        ws_rows = at("ws_rows", [P, SGU_GROUPS, P], kv0 + 2 * P)
        rows_g = at("rows_g", [KD * len(GAIN_COLS), P], kv0 + 6 * P)

        cursor[0] = t0
        qT = new("qT", [P, KD, S])
        prob = new("prob", [P, TB * XA_HEADS, NMEM])
        probT = new("probT", [P, 2, 2, S])

        cursor[0] = t0
        ff_r = new("ff_r", [P, 2, 2 * S])
        ff_u = new("ff_u", [P, 2, 2 * S])
        hg_sq = at("hg_sq", [P, TB, D], t0)
        ff_h = at("ff_h", [P, 4, S], split0, F32R)
        ff_l = at("ff_l", [P, 4, S], split0 + D, F32R)

        cursor[0] = t0
        mem2_tok = at("mem2_tok", [P, 2, D], t0)
        qkT2 = new("qkT2", [P, 8, S])
        sb0 = cursor[0]
        mem2_h = at("mem2_h", [P, KD, NMEM], sb0, F32R)
        mem2_l = at("mem2_l", [P, KD, NMEM], sb0 + 2 * D, F32R)
        mem2_sq = at("mem2_sq", [P, 2, D], sb0)
        sb_e = new("sb_e", [P, 2, SB_COLS])
        sb_l = new("sb_l", [P, 2, SB_COLS])
        sb_m = new("sb_m", [P, 2, SB_COLS])
        sb_a = new("sb_a", [P, 2, SB_COLS])
        ug = new("ug", [P, 4, S])
        v2 = new("v2", [P, TB, HALF])
        y3_pad = at("y3_pad", [P, 4, CONV3 - 1 + S], kv0)
        cc_s = at("cc_s", [P, 2, S], kv0 + 4 * (CONV3 - 1 + S))
        acc3 = at("acc3", [P, 4, S], kv0 + 4 * (CONV3 - 1 + S) + 2 * S)
        merged = at("merged", [P, KD, S], kv0)
        vg = at("vg", [P, TB, HALF], kv0 + 3 * D)
        sig2 = at("sig2", [P, 4, S], kv0 + 3 * D)
        y_h = [at("ya_h", [P, 4, S], xn0, F32R), at("yb_h", [P, 4, S], split0, F32R),
               at("yc_h", [P, 4, S], split0 + 2 * D, F32R)]
        y_l = [at("ya_l", [P, 4, S], xn0 + D, F32R), at("yb_l", [P, 4, S], split0 + D, F32R),
               at("yc_l", [P, 4, S], split0 + 3 * D, F32R)]

        used = [0]

        def cols(n):
            used[0] += n
            assert used[0] <= 256
            return stat[:, used[0] - n:used[0]]

        sq_sum = cols(2 * 10)
        nv, ny, nt = cols(2), cols(2), cols(2)
        r_mix, r_xa, r_mlp, r_f, r_mix2, r_ff2 = (cols(2) for _ in range(6))
        xmax, xneg, xsum, xinv = cols(8), cols(8), cols(8), cols(8)
        r_mean, r_var, r_y, r_t = cols(16), cols(16), cols(16), cols(16)
        bn6, bn2 = cols(6 * TB), cols(2 * TB)

        ps = ctx.enter_context(nc.psum_tensor("ps", [P, 8, 512], F32))

        def tok(b):
            return ps[:, b, :]

        def feat(b):
            return ps[:, 4 + b, :]

        def blocks(x):
            return x.rearrange("p (t n) -> p t n", n=S)

        def sem(name):
            return ctx.enter_context(nc.semaphore(name))

        w_loaded = [sem(f"w_loaded{s}") for s in range(RING)]
        hi_done, lo_done, slab_used = sem("hi_done"), sem("lo_done"), sem("slab_used")
        x_loaded = [sem("x_loaded0"), sem("x_loaded1")]
        mem_loaded, mem2_loaded = sem("mem_loaded"), sem("mem2_loaded")
        rows_loaded, pos_loaded, sgu_loaded = sem("rows_loaded"), sem("pos_loaded"), sem("sgu_loaded")
        gain_loaded, gain_used = sem("gain_loaded"), sem("gain_used")
        gain_mix_loaded, gains_t, gains_ready = sem("gain_mix_loaded"), sem("gains_t"), sem("gains_ready")
        raw_t, raw_hi, raw_lo, hg_ready, h_scaled = sem("raw_t"), sem("raw_hi"), sem("raw_lo"), sem("hg_ready"), sem("h_scaled")
        diag_ready, row_t, row_ready = sem("diag_ready"), sem("row_t"), sem("row_ready")
        sig_in, rg_in, ug_in, gate_in, glu_in_ready = (sem(x) for x in ("sig_in", "rg_in", "ug_in", "gate_in", "glu_in_ready"))
        fill, const_ready, dist_ready, freq_ready = sem("fill"), sem("const_ready"), sem("dist_ready"), sem("freq_ready")
        pad_ready, ws_masked, pad3_ready = sem("pad_ready"), sem("ws_masked"), sem("pad3_ready")
        act_step, dve_step = sem("act_step"), sem("dve_step")
        norm_sq, norm_xn, norm_t, norm_hi, norm_lo = (sem(f"norm_{x}") for x in ("sq", "xn", "t", "hi", "lo"))
        rows_t, cols_ready = sem("rows_t"), sem("cols_ready")
        ang_ready, sincos_ready = sem("ang_ready"), sem("sincos_ready")
        sig_ready, u_ready, rg_ready, rv_ready, qk_ready = (sem(x) for x in ("sig_ready", "u_ready", "rg_ready", "rv_ready", "qk_ready"))
        rope_ready, qk_t, qkT_ready = sem("rope_ready"), sem("qk_t"), sem("qkT_ready")
        ret_s, dec_ready, s_dec_ready, ret_pv = sem("ret_s"), sem("dec_ready"), sem("s_dec_ready"), sem("ret_pv")
        ry_centred, ry_squared, ry_ready, ry_t = sem("ry_centred"), sem("ry_squared"), sem("ry_ready"), sem("ry_t")
        ret_ready, ret_hi, ret_lo = sem("ret_ready"), sem("ret_hi"), sem("ret_lo")
        conv_step, conv_tap, conv_last = sem("conv_step"), sem("conv_tap"), sem("conv_last")
        conv_mean, conv_centred = sem("conv_mean"), sem("conv_centred")
        conv_squared, conv_var, conv_normed = sem("conv_squared"), sem("conv_var"), sem("conv_normed")
        conv_out, conv_hi, conv_lo = sem("conv_out"), sem("conv_hi"), sem("conv_lo")
        k_ready, v_ready = sem("k_ready"), sem("v_ready")
        tb0_done, h_updated = sem("tb0_done"), sem("h_updated")
        xq_ready, xs_ready, xmax_ready, xexp_ready = sem("xq_ready"), sem("xs_ready"), sem("xmax_ready"), sem("xexp_ready")
        xp_ready, xp_t, xpT_ready = sem("xp_ready"), sem("xp_t"), sem("xpT_ready")
        xo_ready, xo_hi, xo_lo = sem("xo_ready"), sem("xo_hi"), sem("xo_lo")
        relu_ready, relu_sq, ff_hi, ff_lo = sem("relu_ready"), sem("relu_sq"), sem("ff_hi"), sem("ff_lo")
        silu_ready, glu_ready, glu_hi, glu_lo = sem("silu_ready"), sem("glu_ready"), sem("glu_hi"), sem("glu_lo")
        sbqk_ready, sbv_ready, ug_ready, vg_ready, vn_ready = (sem(x) for x in ("sbqk_ready", "sbv_ready", "ug_ready", "vg_ready", "vn_ready"))
        sb_z, sb_z_read, sb_log, sb_pen, sb_cum, sb_arg = sem("sb_z"), sem("sb_z_read"), sem("sb_log"), sem("sb_pen"), sem("sb_cum"), sem("sb_arg")
        sb_exp, sb_prob, sb_out, sb_hi, sb_lo = sem("sb_exp"), sem("sb_prob"), sem("sb_out"), sem("sb_hi"), sem("sb_lo")
        sgu_mixed, yb_ready, yb_hi, yb_lo = sem("sgu_mixed"), sem("yb_ready"), sem("yb_hi"), sem("yb_lo")
        y3_ready, yc_ready, yc_hi, yc_lo = sem("y3_ready"), sem("yc_ready"), sem("yc_hi"), sem("yc_lo")
        gate_ready, merge_done, merged_hi, merged_lo = sem("gate_ready"), sem("merge_done"), sem("merged_hi"), sem("merged_lo")
        out_ready, stored = sem("out_ready"), sem("stored")

        block = ctx.enter_context(nc.Block())

        UPD = {I_OUT1: 0, I_O1: 1, I_FF1: 2, I_OUT2: 3, I_O2: 4, I_FF2: 5}

        @block.sync
        def _(sp):
            def load(i, src, step=0, wait_step=0):
                s = PLACE[i]
                if BEFORE[i] is not None:
                    sp.wait_ge(lo_done, BEFORE[i] + 1 + wait_step)
                dst = w_ring[:, s, :].rearrange("p (k n) -> p k n", n=src.shape[2])
                sp.dma_start(dst, src).then_inc(w_loaded[s], 16)

            def panel_a(w, col, n=256):
                return w.rearrange("(k p) n -> p k n", p=P)[:, :, col:col + n]

            def rows_b_form(w, row, col=0, n=D, nk=2):
                return w[row:row + nk * P, col:col + n].rearrange("(k p) n -> p k n", p=P)

            sp.dma_start(rows_g[0:KD, :], a[GAIN_COLS[0]].rearrange("(f p) -> f p", p=P)).then_inc(gain_mix_loaded, 16)
            for tb in range(TB):
                sp.dma_start(h[:, tb, :], a["x"][0, tb * P:(tb + 1) * P, :]).then_inc(x_loaded[tb], 16)
            w_in = a["w_in"]
            for j in range(2):
                load(I_CONV + 2 * j, panel_a(w_in, 256 * j))
                if j == 0:
                    sp.dma_start(mem_tok[:, :, :], a["mem"].rearrange("a (t p) d -> p (a t) d", p=P)).then_inc(mem_loaded, 16)
                load(I_CONV + 2 * j + 1, panel_a(w_in, HALF + 256 * j))
            for j in range(2):
                load(I_QK + j, rows_b_form(w_in, 512 * j, 2 * HALF, HALF, 4))
            for j in range(2):
                load(I_RV + j, rows_b_form(w_in, 512 * j, 3 * HALF, HALF, 4))
            for j in range(2):
                load(I_RG + j, panel_a(w_in, 4 * HALF + 256 * j))
            for j in range(4):
                load(I_K1 + j, panel_a(a["xkv_w"], 256 * j))
            for j in range(4):
                load(I_V1 + j, rows_b_form(a["xkv_w"], 256 * j, D))
            for j, k in enumerate(OUT1_ORDER):
                load(I_OUT1 + j, rows_b_form(a["w_out"], 256 * k))
            for j in range(4):
                load(I_Q1 + j, panel_a(a["xq_w"], 256 * j))
            for j in range(4):
                load(I_O1 + j, rows_b_form(a["xo_w"], 256 * j))
            up = a["mlp_up_w"].rearrange("(k p) n -> p k n", p=P)
            down = a["mlp_down_w"].rearrange("(k p) n -> p k n", p=P)
            with sp.Fori(0, G1) as g:
                for c in range(2):
                    load(I_FF1 + c, up[:, :, bass.ds(g * 512 + 256 * c, 256)], wait_step=4 * g)
                for c in range(2):
                    load(I_FF1 + 2 + c, down[:, bass.ds(g * 4 + 2 * c, 2), :], wait_step=4 * g)
            w2 = a["w_in_2"].squeeze(0)
            for j in range(4):
                load(I_SBQK + j, panel_a(w2, 256 * j))
            for j in range(2):
                load(I_SBV + j, rows_b_form(w2, 512 * j, 2 * HALF, HALF, 4))
            for j in range(2):
                load(I_ZU + j, panel_a(w2, 3 * HALF + 256 * j))
            for j in range(2):
                load(I_ZV + j, rows_b_form(w2, 512 * j, 4 * HALF, HALF, 4))
            for j, col in enumerate(C3_COLS):
                load(I_C3 + j, panel_a(w2, col))
            wb = a["w_branch_2"].squeeze(0)
            for n, br in enumerate(BRANCH_ORDER):
                for half in range(2):
                    i = I_BR + 6 * n + 3 * half
                    for j in range(2):
                        load(i + j, panel_a(w2, 8 * HALF + D * br + HALF * half + 256 * j))
                    load(i + 2, panel_a(wb[br], HALF * half, HALF))
            for j in range(4):
                load(I_OUT2 + j, rows_b_form(a["w_out_2"].squeeze(0), 256 * j))
            for j in range(4):
                load(I_K2 + j, panel_a(a["w_k_xa_2"].squeeze(0), 256 * j))
            for j in range(4):
                load(I_V2 + j, rows_b_form(a["w_v_xa_2"].squeeze(0), 256 * j))
            for j in range(4):
                load(I_Q2 + j, panel_a(a["w_q_xa_2"].squeeze(0), 256 * j))
            for j in range(4):
                load(I_O2 + j, rows_b_form(a["w_o_xa_2"].squeeze(0), 256 * j))
            wg = a["w_gate_ffn_2"].squeeze(0).rearrange("(k p) n -> p k n", p=P)
            wu = a["w_up_ffn_2"].squeeze(0).rearrange("(k p) n -> p k n", p=P)
            wd = a["w_down_ffn_2"].squeeze(0).rearrange("(k p) n -> p k n", p=P)
            load(I_FF2, wg[:, :, 0:256])
            load(I_FF2 + 1, wu[:, :, 0:256])
            for g in range(1, 3):
                i = ff2_gate(g)
                load(i, wg[:, :, 256 * g:256 * g + 256])
                load(i + 1, wu[:, :, 256 * g:256 * g + 256])
                load(i + 2, wd[:, 2 * g - 2:2 * g, :])
            i = ff2_gate(3)
            with sp.Fori(0, G2 - 3) as t:
                load(i, wg[:, :, bass.ds(t * 256 + 768, 256)], wait_step=3 * t)
                load(i + 1, wu[:, :, bass.ds(t * 256 + 768, 256)], wait_step=3 * t)
                load(i + 2, wd[:, bass.ds(t * 2 + 4, 2), :], wait_step=3 * t)
            load(N_SLABS - 1, wd[:, 2 * G2 - 2:2 * G2, :])
            for tb in range(TB):
                sp.wait_ge(out_ready, tb + 1)
                sp.dma_start(out[0, tb * P:(tb + 1) * P, :], xn[:, tb, :]).then_inc(stored, 16)
            sp.wait_ge(stored, 16 * TB)

        @block.gpsimd
        def _(pool):
            def load_gain(n):
                if n > 0:
                    pool.wait_ge(gain_used, n)
                w = a[GAIN_ROWS[n]]
                w = w if len(w.shape) == 1 else w.squeeze(0)
                pool.dma_start(gain[:, :], w.partition_broadcast(P)).then_inc(gain_loaded, 16)

            pool.memset(ident[:, :], 0.0).then_inc(fill, 1)
            pool.memset(later[:, :], 1.0).then_inc(fill, 1)
            pool.memset(earlier[:, :], 1.0).then_inc(fill, 1)
            pool.wait_ge(fill, 3)
            pool.affine_select(out=ident[:, :], in_=ident[:, :], compare_op=ALU.not_equal, fill=1.0, base=0,
                               pattern=[[-1, P]], channel_multiplier=1).then_inc(const_ready, 1)
            pool.iota(dist_i[:, :], pattern=[[1, S]], base=0, channel_multiplier=-1).then_inc(dist_ready, 1)
            for f in range(ROPE_HALF):
                pool.memset(freq[:, f:f + 1], float(INV_FREQ[f])).then_inc(freq_ready, 1)
            pool.memset(u_pad[:, :, 0:CONV_W - 1], 0.0).then_inc(pad_ready, 1)
            pool.memset(ones[:, :], 1.0).then_inc(const_ready, 1)
            load_gain(G_MEM)
            pool.dma_start(pos_i[:, :], a["positions"].rearrange("a (t p) -> p (a t)", p=P), allow_slow_non_contiguous=True).then_inc(pos_loaded, 16)
            pool.dma_start(ln_g[:, :], a["sgu_ln_g_2"].squeeze(0).partition_broadcast(P)).then_inc(sgu_loaded, 16)
            pool.dma_start(ln_b[:, :], a["sgu_ln_b_2"].squeeze(0).partition_broadcast(P)).then_inc(sgu_loaded, 16)
            pool.dma_start(b_sp[:, :, :], a["b_spatial_2"].squeeze(0).rearrange("g t -> (g t)").partition_broadcast(P)
                           .rearrange("p (g t) -> p g t", g=SGU_GROUPS)).then_inc(sgu_loaded, 16)
            pool.affine_select(out=later[:, :], in_=later[:, :], compare_op=ALU.is_gt, fill=0.0, base=0,
                               pattern=[[-1, P]], channel_multiplier=1).then_inc(const_ready, 1)
            pool.affine_select(out=earlier[:, :], in_=earlier[:, :], compare_op=ALU.is_gt, fill=0.0, base=0,
                               pattern=[[1, P]], channel_multiplier=-1).then_inc(const_ready, 1)
            pool.wait_ge(const_ready, 4)
            pool.wait_ge(cols_ready, 4)
            pool.memset(ws_t[CHUNK:P, :, 0:CHUNK], 0.0).then_inc(ws_masked, 1)
            pool.wait_ge(ws_masked, 1)
            pool.wait_ge(u_ready, 2)
            for n, (c, k) in enumerate([(3, k) for k in range(CONV_W)] + [(2, k) for k in range(TAPS_DVE, CONV_W)]):
                tap, win = cols_b[:, 4 * k + c:4 * k + c + 1], u_pad[:, c, k:k + S]
                acc = c_acc[:, 3, :] if c == 3 else c_rest[:, :]
                if k == 0:
                    pool.tensor_scalar(acc, win, tap, cols_a[:, ROW_OF["conv_b"] + 3:ROW_OF["conv_b"] + 4], ALU.mult, ALU.add).then_inc(conv_last, 1)
                elif n == CONV_W:
                    pool.tensor_scalar(acc, win, tap, None, ALU.mult).then_inc(conv_last, 1)
                else:
                    if n >= 2:
                        pool.wait_ge(conv_last, n - 1)
                    pool.tensor_scalar(c_tap[:, n % 2, :], win, tap, None, ALU.mult).then_inc(conv_tap, 1)
                    pool.wait_ge(conv_tap, n if c == 3 else n - 1)
                    pool.wait_ge(conv_last, n)
                    pool.tensor_tensor(acc, acc, c_tap[:, n % 2, :], ALU.add).then_inc(conv_last, 1)
            load_gain(G_F)
            pool.wait_ge(xo_ready, XA_HEADS)
            pool.memset(y3_pad[:, :, 0:CONV3 - 1], 0.0).then_inc(pad3_ready, 1)
            load_gain(G_MEM2)
            pool.wait_ge(sb_z, 4)
            pool.dma_start(mem2_tok[:, :, :], a["mem_2"].rearrange("a (t p) d -> p (a t) d", p=P)).then_inc(mem2_loaded, 16)
            load_gain(G_FINAL)

        @block.tensor
        def _(pe):
            def mm3(o, left, right, first, last):
                (lh, ll), (rh, rl) = left, right
                pe.matmul(o, lh, rh, start=first, stop=False)
                pe.matmul(o, lh, rl, start=False, stop=False)
                return pe.matmul(o, ll, rh, start=False, stop=last)

            def slab(i, n):
                s = PLACE[i]
                return tuple(w[:, s, :].rearrange("p (k n) -> p k n", n=n) for w in (w_hi, w_lo))

            def form_a(i, banks, xt, n=256, step=0, ready=None):
                pe.wait_ge(lo_done, i + 1 + step)
                wh, wl = slab(i, n)
                nk = SLAB // n
                for b in range(n // P):
                    for k in range(nk):
                        if ready and b == 0:
                            ready(k)
                        c = slice(b * P, (b + 1) * P)
                        mm = mm3(feat(banks[b // 2])[:, (b % 2) * S:(b % 2 + 1) * S], (wh[:, k, c], wl[:, k, c]),
                                 (xt[0][:, k, :], xt[1][:, k, :]), k == 0, k == nk - 1)
                mm.then_inc(slab_used, 1)

            def form_b_rows(i, k0, xt, tbs, first, last, step=0, n=D):
                pe.wait_ge(lo_done, i + 1 + step)
                wh, wl = slab(i, n)
                nk = SLAB // n
                for kk in range(nk):
                    for tb in tbs:
                        t = slice(tb * P, (tb + 1) * P)
                        for half in range(n // HALF):
                            c = slice(half * HALF, (half + 1) * HALF)
                            mm = mm3(tok(2 * tb + half) if n == D else None, (xt[0][:, k0 + kk, t], xt[1][:, k0 + kk, t]),
                                     (wh[:, kk, c], wl[:, kk, c]), first and kk == 0, last and kk == nk - 1)
                return mm

            def form_b(i0, xt, order, ready, between, midway=None):
                for j in range(2):
                    ready(order[j])
                    form_b_rows(i0 + j, 2 * order[j], xt, (0, 1), j == 0, False).then_inc(slab_used, 1)
                if midway:
                    midway()
                for j in (2, 3):
                    ready(order[j])
                    mm = form_b_rows(i0 + j, 2 * order[j], xt, (0,), False, j == 3)
                mm.then_inc(tb0_done, 1)
                for j in (2, 3):
                    form_b_rows(i0 + j, 2 * order[j], xt, (1,), False, j == 3).then_inc(slab_used, 1)
                    if j == 2:
                        between()

            def form_b_half(i0, bank, xt):
                for j in range(2):
                    pe.wait_ge(lo_done, i0 + j + 1)
                    wh, wl = slab(i0 + j, HALF)
                    for kk in range(4):
                        k = 4 * j + kk
                        for tb in range(TB):
                            t = slice(tb * P, (tb + 1) * P)
                            mm = mm3(tok(bank + tb), (xt[0][:, k, t], xt[1][:, k, t]), (wh[:, kk, :], wl[:, kk, :]),
                                     k == 0, k == KD - 1)
                    mm.then_inc(slab_used, 1)

            def norm_transpose(n, src, bank=tok):
                for tb in range(TB):
                    pe.wait_ge(norm_xn, 2 * n + tb + 1)
                    for f in range(KD):
                        mm = pe.transpose(bank(2 * tb + f // 4)[:, (f % 4) * P:(f % 4 + 1) * P],
                                          src[:, tb, f * P:(f + 1) * P], ident[:, :])
                    mm.then_inc(norm_t, 1)

            def normed(n):
                pe.wait_ge(norm_lo, 4 * (n + 1))

            def raw_transpose(src, tb, done, base):
                for half in range(2):
                    if done is not None:
                        pe.wait_ge(done, base + 2 * tb + half + 1)
                    for f in range(4):
                        mm = pe.transpose(tok(2 * tb + half)[:, f * P:(f + 1) * P],
                                          src[:, tb, (4 * half + f) * P:(4 * half + f + 1) * P], ident[:, :])
                    mm.then_inc(raw_t, 1)

            def raw_ready(n):
                return lambda k: pe.wait_ge(raw_lo, 16 * n + 9 + k)

            def spread(m, bank):
                pe.wait_ge(const_ready, 2)
                for tb in range(TB):
                    pe.wait_ge(diag_ready, 2 * m + tb + 1)
                    mm = pe.matmul(bank[:, tb * P:(tb + 1) * P], ones[:, :], diag[:, tb, :], start=True, stop=True)
                mm.then_inc(row_t, 1)

            def x_attention(b, i_q, i_o, ready, between):
                def scores(hd):
                    pe.wait_ge(xq_ready, 4 * b + hd + 1)
                    pe.wait_ge(k_ready, 4 * (b + 1))
                    for tb in range(TB):
                        u = TB * hd + tb
                        if u >= 4:
                            pe.wait_ge(xexp_ready, 8 * b + u - 3)
                        for kk in range(2):
                            f = 2 * hd + kk
                            mm = pe.matmul(tok(u % 4)[:, 0:NMEM], qT[:, f, tb * P:(tb + 1) * P], kT[:, f, :],
                                           start=kk == 0, stop=kk == 1)
                        mm.then_inc(xs_ready, 1)

                def turn(hd):
                    for tb in range(TB):
                        u = TB * hd + tb
                        pe.wait_ge(xp_ready, 8 * b + u + 1)
                        for m in range(2):
                            mm = pe.transpose(feat(hd)[:, m * S + tb * P:m * S + (tb + 1) * P],
                                              prob[:, u, m * P:(m + 1) * P], ident[:, :])
                    mm.then_inc(xp_t, 1)

                def values(hd):
                    pe.wait_ge(xpT_ready, 4 * b + hd + 1)
                    pe.wait_ge(v_ready, 4 * (b + 1))
                    for kk in range(2):
                        f = 2 * hd + kk
                        for m in range(2):
                            mm = pe.matmul(feat(hd)[:, kk * S:(kk + 1) * S], vm[:, m, f * P:(f + 1) * P],
                                           probT[:, hd % 2, m, :], start=m == 0, stop=m == 1)
                    mm.then_inc(xo_ready, 1)

                form_a(i_q, (0,), (xh, xl), ready=ready)
                form_a(i_q + 1, (1,), (xh, xl))
                pe.wait_ge(v_ready, 4 * (b + 1))
                scores(0)
                form_a(i_q + 2, (2,), (xh, xl))
                scores(1)
                form_a(i_q + 3, (3,), (xh, xl))
                turn(0)
                scores(2)
                values(0)
                turn(1)
                scores(3)
                values(1)
                turn(2)
                values(2)
                turn(3)
                values(3)
                pe.wait_ge(xexp_ready, 8 * (b + 1))
                form_b(i_o, (xh, xl), range(4), lambda s: pe.wait_ge(xo_lo, 4 * b + s + 1), between)

            x_t, m_t = (xh, xl), (mem_h, mem_l)
            pe.wait_ge(const_ready, 1)
            pe.wait_ge(gain_mix_loaded, 16)
            pe.transpose(feat(3)[:, 0:KD], rows_g[0:KD, :], ident[0:KD, 0:KD]).then_inc(gains_t, 1)
            for tb in range(TB):
                pe.wait_ge(x_loaded[tb], 16)
                raw_transpose(h, tb, None, 0)
            form_a(0, (0,), x_t, ready=raw_ready(R_MIX))
            form_a(1, (1,), x_t)
            spread(0, tok(0))
            form_a(2, (2,), x_t)
            pe.wait_ge(row_ready, 1)
            norm_transpose(N_MEM, mem_tok)
            pe.wait_ge(gains_ready, 1)
            form_a(3, (3,), x_t)
            pe.wait_ge(rows_loaded, 16 * (len(ROW_OF) + 2 + len(GAIN_COLS) - 1))
            normed(N_MEM)
            pe.transpose(tok(2)[:, 0:ROWS_A], rows_a[:, :], ident[0:ROWS_A, 0:ROWS_A])
            pe.transpose(tok(2)[:, P:P + 4 * CONV_W], rows_b[:, :], ident[0:4 * CONV_W, 0:4 * CONV_W])
            n = KD * len(GAIN_COLS)
            pe.transpose(tok(2)[:, 2 * P:2 * P + n], rows_g[:, :], ident[0:n, 0:n])
            for g in range(SGU_GROUPS):
                mm = pe.transpose(tok(3)[:, g * P:(g + 1) * P], ws_rows[:, g, :], ident[:, :])
            mm.then_inc(rows_t, 1)
            form_b_half(I_QK, 0, x_t)
            pe.wait_ge(cols_ready, 4)
            form_b_half(I_RV, 2, x_t)
            pe.wait_ge(rope_ready, 2)
            for f in range(4):
                for tb in range(TB):
                    mm = pe.transpose(tok(f // 2)[:, (f % 2) * S + tb * P:(f % 2) * S + (tb + 1) * P],
                                      qkr[:, tb, f * P:(f + 1) * P], ident[:, :])
                if f % 2:
                    mm.then_inc(qk_t, 1)
            pe.wait_ge(u_ready, 1)
            form_a(I_RG, (0,), x_t)

            def ret_scores(hd):
                pe.wait_ge(qkT_ready, 2)
                if hd == 2:
                    pe.wait_ge(rv_ready, 2)
                if hd >= 4:
                    pe.wait_ge(s_dec_ready, hd - 3)
                r = slice(RET_DK * (hd % 4), RET_DK * (hd % 4 + 1))
                f = hd // 4
                pe.matmul(tok(hd % 4)[:, 0:S], qkT[r, 2 + f, 0:P], qkT[r, f, 0:S], start=True, stop=True)
                pe.matmul(tok(hd % 4)[:, S:S + P], qkT[r, 2 + f, P:S], qkT[r, f, P:S],
                          start=True, stop=True).then_inc(ret_s, 1)

            def ret_values(hd):
                pe.wait_ge(s_dec_ready, hd + 1)
                pe.wait_ge(rv_ready, 2)
                pe.wait_ge(u_ready, 2)
                c = slice(hd * RET_DV, (hd + 1) * RET_DV)
                sd = s_dec[:, hd % 2, :]
                pe.matmul(feat(2)[:, c], sd[:, 0:P], rv[:, 0, c], start=True, stop=True)
                pe.matmul(feat(3)[:, c], sd[:, P:S], rv[:, 0, c], start=True, stop=False)
                pe.matmul(feat(3)[:, c], sd[:, S:S + P], rv[:, 1, c], start=False, stop=True).then_inc(ret_pv, 1)

            ret_scores(0)
            ret_scores(1)
            form_a(I_RG + 1, (1,), x_t)
            for hd in range(4):
                ret_scores(hd + 2)
                ret_values(hd)
            pe.wait_ge(rg_in, 1)
            form_a(I_K1, (0,), m_t)
            for hd in range(4, RET_HEADS):
                if hd + 2 < RET_HEADS:
                    ret_scores(hd + 2)
                ret_values(hd)
            pe.wait_ge(rg_in, 2)
            form_a(I_K1 + 1, (1,), m_t)
            pe.wait_ge(k_ready, 1)
            form_a(I_K1 + 2, (0,), m_t)
            pe.wait_ge(k_ready, 2)
            form_a(I_K1 + 3, (1,), m_t)
            pe.wait_ge(k_ready, 3)
            pe.wait_ge(ry_ready, 1)
            for f in range(4):
                for tb in range(TB):
                    mm = pe.transpose(feat(2 * (f // 2))[:, (f % 2) * S + tb * P:(f % 2) * S + (tb + 1) * P],
                                      ry[:, tb, f * P:(f + 1) * P], ident[:, :])
            mm.then_inc(ry_t, 1)
            for j in range(4):
                form_b_rows(I_V1 + j, 2 * j, m_t, (0, 1), j == 0, j == 3).then_inc(slab_used, 1)
                if j == 2:
                    pe.wait_ge(const_ready, 4)
                    pe.wait_ge(ret_ready, 1)
                    pe.wait_ge(conv_last, 2 * CONV_W - TAPS_DVE)
                    pe.wait_ge(conv_step, 2 * CONV_W + TAPS_DVE + 1)
                    for c in range(4):
                        mm = pe.matmul(feat(2)[:, 0:S], ones[:, :], c_acc[:, c, :], start=c == 0, stop=c == 3)
                    mm.then_inc(conv_mean, 1)
            pe.wait_ge(conv_squared, 1)
            for c in range(4):
                mm = pe.matmul(feat(3)[:, 0:S], ones[:, :], c_sq[:, c, :], start=c == 0, stop=c == 3)
            mm.then_inc(conv_var, 1)
            pe.wait_ge(v_ready, 4)
            pe.wait_ge(ret_lo, 1)
            form_b_rows(I_OUT1, 2 * OUT1_ORDER[0], x_t, (0, 1), True, False).then_inc(slab_used, 1)
            form_b_rows(I_OUT1 + 1, 2 * OUT1_ORDER[1], x_t, (0, 1), False, False).then_inc(slab_used, 1)
            pe.wait_ge(conv_lo, 1)
            for j in (2, 3):
                mm = form_b_rows(I_OUT1 + j, 2 * OUT1_ORDER[j], x_t, (0,), False, j == 3)
            mm.then_inc(tb0_done, 1)
            for j in (2, 3):
                form_b_rows(I_OUT1 + j, 2 * OUT1_ORDER[j], x_t, (1,), False, j == 3).then_inc(slab_used, 1)
                if j == 2:
                    raw_transpose(h, 0, h_updated, 4 * UPD[I_OUT1])
            raw_transpose(h, 1, h_updated, 4 * UPD[I_OUT1])
            pe.wait_ge(k_ready, 4)
            x_attention(0, I_Q1, I_O1, raw_ready(R_XA), lambda: raw_transpose(h, 0, h_updated, 4 * UPD[I_O1]))
            raw_transpose(h, 1, h_updated, 4 * UPD[I_O1])

            def mlp1(g, first=False, last=False):
                step = 0 if first else 4 * g
                i = I_FF1
                for c in range(2):
                    if first:
                        pe.wait_ge(xo_lo, 4)
                    else:
                        pe.wait_ge(relu_ready, 2 * g - 1 + c)
                    form_a(i + c, (c,), x_t, step=step, ready=raw_ready(R_MLP) if first and c == 0 else None)
                u_t = (ff_h, ff_l)
                two = 0 if first else 2 * g
                if last:
                    for c in range(2):
                        pe.wait_ge(ff_lo, two + c + 1)
                        mm = form_b_rows(i + 2 + c, 2 * c, u_t, (0,), False, c == 1, step=step)
                    mm.then_inc(tb0_done, 1)
                    for c in range(2):
                        form_b_rows(i + 2 + c, 2 * c, u_t, (1,), False, c == 1, step=step).then_inc(slab_used, 1)
                        if c == 0:
                            raw_transpose(xn, 0, hg_ready, 0)
                else:
                    for c in range(2):
                        pe.wait_ge(ff_lo, two + c + 1)
                        form_b_rows(i + 2 + c, 2 * c, u_t, (0, 1), first and c == 0, False, step=step).then_inc(slab_used, 1)

            mlp1(0, first=True)
            with pe.Fori(1, G1 - 1) as g:
                mlp1(g)
            mlp1(G1 - 1, last=True)
            raw_transpose(xn, 1, hg_ready, 0)
            for j in range(4):
                form_a(I_SBQK + j, (j,), x_t, ready=raw_ready(R_MIX2) if j == 0 else None)
                if j == 2:
                    spread(1, tok(3))
            form_b_half(I_SBV, 0, x_t)

            def sb_scores(p):
                if p == 0:
                    pe.wait_ge(sbv_ready, 2)
                    pe.wait_ge(sbqk_ready, 4)
                else:
                    pe.wait_ge(sb_z_read, p)
                for e in range(2):
                    r = slice(SB_DIM * e, SB_DIM * (e + 1))
                    pe.matmul(tok(e)[:, 0:S], qkT2[r, 4 + p, 0:P], qkT2[r, p, 0:S], start=True, stop=True)
                    mm = pe.matmul(tok(e)[:, S:S + P], qkT2[r, 4 + p, P:S], qkT2[r, p, P:S], start=True, stop=True)
                mm.then_inc(sb_z, 1)

            def sb_sums(p):
                pe.wait_ge(sb_pen, p + 1)
                if p == 0:
                    pe.wait_ge(vg_ready, 2)
                else:
                    pe.wait_ge(sb_lo, p)
                for e in range(2):
                    pe.matmul(tok(2 + e)[:, 0:S], later[:, :], sb_m[:, e, 0:S], start=True, stop=False)
                    pe.matmul(tok(2 + e)[:, P:S], ones[:, :], sb_m[:, e, S:S + P], start=False, stop=True)
                    mm = pe.matmul(tok(2 + e)[:, S:S + P], later[:, :], sb_m[:, e, S:S + P], start=True, stop=True)
                mm.then_inc(sb_cum, 1)

            def sb_values(p):
                pe.wait_ge(sb_prob, p + 1)
                for e in range(2):
                    r = slice(SB_DIM * e, SB_DIM * (e + 1))
                    c = slice((2 * p + e) * SB_DIM, (2 * p + e + 1) * SB_DIM)
                    pe.matmul(tok(2)[r, 0:S], v2[:, 0, c], sb_a[:, e, 0:S], start=True, stop=False)
                    mm = pe.matmul(tok(2)[r, P:S], v2[:, 1, c], sb_a[:, e, S:S + P], start=False, stop=True)
                mm.then_inc(sb_out, 1)

            SB_AT = {}

            def at_slab(i, step, p):
                SB_AT.setdefault(i, []).append((step, p))

            for p in range(4):
                at_slab(SB_START + 4 * p, sb_scores, p)
                at_slab(SB_START + 4 * p + 3, sb_sums, p)
                at_slab(SB_START + 4 * p + 6, sb_values, p)

            def beside(i):
                for step, p in SB_AT.get(i, ()):
                    step(p)

            pe.wait_ge(sbqk_ready, 2)
            form_a(I_ZU, (0,), x_t)
            form_a(I_ZU + 1, (1,), x_t)
            pe.wait_ge(row_ready, 2)
            form_b_half(I_ZV, 2, x_t)
            beside(I_ZV + 1)
            pe.wait_ge(sbqk_ready, 4)
            form_a(I_C3, (2,), x_t)
            beside(I_C3)
            form_a(I_C3 + 1, (3,), x_t)
            beside(I_C3 + 1)
            pe.wait_ge(ug_in, 2)
            form_a(I_C3 + 2, (0,), x_t)
            beside(I_C3 + 2)
            form_a(I_C3 + 3, (1,), x_t)
            beside(I_C3 + 3)
            pe.wait_ge(y3_ready, 1)
            form_a(I_C3 + 4, (2,), x_t)
            beside(I_C3 + 4)
            pe.wait_ge(vn_ready, 2)
            pe.wait_ge(ws_masked, 1)
            pe.wait_ge(y3_ready, 2)
            for g in range(SGU_GROUPS):
                for tb in range(TB):
                    o = feat(g // 2)[:, (g % 2) * S + tb * P:(g % 2) * S + (tb + 1) * P]
                    mm = pe.matmul(o, vg[:, tb, g * P:(g + 1) * P], ws_t[:, g, :], start=True, stop=True)
            mm.then_inc(sgu_mixed, 1)
            form_a(I_C3 + 5, (3,), x_t)
            beside(I_C3 + 5)
            for n, br in enumerate(BRANCH_ORDER):
                for half in range(2):
                    i = I_BR + 6 * n + 3 * half
                    r = 2 * n + half
                    if r == 0:
                        pe.wait_ge(yb_ready, 2)
                    for j in range(2):
                        if r > 0:
                            pe.wait_ge(gate_in, 2 * r - 1 + j)
                        form_a(i + j, (j,), x_t)
                        beside(i + j)
                    if r == 0:
                        pe.wait_ge(yc_ready, 2)
                    else:
                        pe.wait_ge(merge_done, r)
                    pe.wait_ge((sb_lo, yb_lo, yc_lo)[br], (4, 1, 1)[br])
                    form_a(i + 2, (2, 3), (y_h[br], y_l[br]), n=HALF)
                    beside(i + 2)

            def second_memory():
                pe.wait_ge(merge_done, 6)
                norm_transpose(N_MEM2, mem2_tok, feat)

            pe.wait_ge(sb_lo, 4)
            form_b(I_OUT2, x_t, range(4), lambda s: pe.wait_ge(merged_lo, 1 + s // 2),
                   lambda: raw_transpose(h, 0, h_updated, 4 * UPD[I_OUT2]), second_memory)
            m2_t = (mem2_h, mem2_l)
            normed(N_MEM2)
            form_a(I_K2, (0,), m2_t)
            raw_transpose(h, 1, h_updated, 4 * UPD[I_OUT2])
            form_a(I_K2 + 1, (1,), m2_t)
            form_a(I_K2 + 2, (2,), m2_t)
            form_a(I_K2 + 3, (3,), m2_t)
            raw_ready(R_XA2)(KD - 1)
            for j in range(4):
                form_b_rows(I_V2 + j, 2 * j, m2_t, (0, 1), j == 0, j == 3).then_inc(slab_used, 1)
            pe.wait_ge(k_ready, 8)
            x_attention(1, I_Q2, I_O2, None, lambda: raw_transpose(h, 0, h_updated, 4 * UPD[I_O2]))
            raw_transpose(h, 1, h_updated, 4 * UPD[I_O2])

            def glu_in(i, banks=(0, 1), gate_done=None, up_done=None, step=0, ready=None):
                if gate_done is not None:
                    pe.wait_ge(glu_in_ready, gate_done)
                form_a(i, banks[:1], x_t, step=step, ready=ready)
                if up_done is not None:
                    pe.wait_ge(glu_ready, up_done)
                form_a(i + 1, banks[1:], x_t, step=step)

            def glu_out(i, done, first=False, step=0):
                pe.wait_ge(glu_lo, done)
                form_b_rows(i, 0, (ff_h, ff_l), (0, 1), first, False, step=step).then_inc(slab_used, 1)

            pe.wait_ge(xo_lo, 8)
            glu_in(I_FF2, (2, 3), ready=raw_ready(R_FF2))
            spread(2, tok(0))
            glu_in(ff2_gate(1))
            pe.wait_ge(row_ready, 3)
            glu_out(ff2_gate(1) + 2, 1, first=True)
            glu_in(ff2_gate(2), gate_done=2, up_done=2)
            glu_out(ff2_gate(2) + 2, 2)
            with pe.Fori(0, G2 - 3) as t:
                glu_in(ff2_gate(3), gate_done=t + 3, up_done=t + 3, step=3 * t)
                glu_out(ff2_gate(3) + 2, t + 3, step=3 * t)
            pe.wait_ge(glu_lo, G2)
            form_b_rows(N_SLABS - 1, 2, (ff_h, ff_l), (0,), False, True).then_inc(tb0_done, 1)
            form_b_rows(N_SLABS - 1, 2, (ff_h, ff_l), (1,), False, True).then_inc(slab_used, 1)

        @block.scalar
        def _(act):
            count = [0]

            def after(ins):
                count[0] += 1
                ins.then_inc(act_step, 1)
                act.wait_ge(act_step, count[0])

            def hi(i, step=0, turn=0):
                s = PLACE[i]
                act.wait_ge(w_loaded[s], 16 * (USES[i] + 1) + 16 * turn)
                if BEFORE[i] is not None:
                    act.wait_ge(slab_used, BEFORE[i] + 1 + step)
                act.activation(w_hi[:, s, :], w_ring[:, s, :], ACT.Copy).then_inc(hi_done, 1)

            def norm_square(src, tb, use, junk=None):
                if use + tb > 0:
                    act.wait_ge(norm_sq, 2 * use + tb)
                act.activation(xn[:, tb, :] if junk is None else junk, src[:, tb, :], ACT.Square,
                               accum_out=sq_sum[:, 2 * use + tb:2 * use + tb + 1]).then_inc(norm_sq, 1)

            def norm_split_hi(n, tb, dst, bank=tok):
                act.wait_ge(norm_t, 2 * n + tb + 1)
                for half in range(2):
                    act.activation(dst[:, 4 * half:4 * half + 4, tb * P:(tb + 1) * P],
                                   bank(2 * tb + half).rearrange("p (f t) -> p f t", t=P), ACT.Copy).then_inc(norm_hi, 1)

            def raw_split_hi(n, tb):
                for half in range(2):
                    act.wait_ge(raw_t, 4 * n + 2 * tb + half + 1)
                    for f in range(4):
                        k = 4 * half + f
                        act.activation(xh[:, k, tb * P:(tb + 1) * P], tok(2 * tb + half)[:, f * P:(f + 1) * P], ACT.Copy,
                                       scale=cols_g[:, KD * n + k:KD * n + k + 1]).then_inc(raw_hi, 1)

            def row_copy(m, bank):
                act.wait_ge(row_t, m + 1)
                act.activation(r_row[:, 0, :], bank[:, 0:S], ACT.Copy).then_inc(row_ready, 1)

            def used_slab(i):
                act.wait_ge(slab_used, i + 1)

            def boundary(n, use, nxt):
                hi(nxt)
                hi(nxt + 1)
                raw_split_hi(n, 0)
                raw_split_hi(n, 1)
                hi(nxt + 2)
                for tb in range(TB):
                    norm_square(h, tb, use)
                hi(nxt + 3)

            for name, r in ROW_OF.items():
                w = a[name]
                w = w.squeeze(0).rearrange("k (c p) -> (k c) p", p=P) if name == "conv_w_2" else w.rearrange("(c p) -> c p", p=P)
                act.dma_start(rows_a[r:r + w.shape[0], :], w).then_inc(rows_loaded, 16)
            act.dma_start(rows_b[:, :], a["conv_w"].rearrange("k (c p) -> (k c) p", p=P)).then_inc(rows_loaded, 16)
            act.dma_start(ws_rows[:, :, :], a["w_spatial_2"].squeeze(0).rearrange("g t s -> t g s")).then_inc(rows_loaded, 16)
            for n, name in enumerate(GAIN_COLS[1:], 1):
                w = a[name]
                w = w if len(w.shape) == 1 else w.squeeze(0)
                act.dma_start(rows_g[KD * n:KD * (n + 1), :], w.rearrange("(f p) -> f p", p=P)).then_inc(rows_loaded, 16)
            act.wait_ge(gains_t, 1)
            act.activation(cols_g[:, 0:KD], feat(3)[:, 0:KD], ACT.Copy).then_inc(gains_ready, 1)
            act.wait_ge(gains_ready, 1)
            raw_split_hi(R_MIX, 0)
            hi(0)
            raw_split_hi(R_MIX, 1)
            hi(1)
            norm_square(h, 0, Q_MIX)
            norm_square(h, 1, Q_MIX)
            act.wait_ge(mem_loaded, 16)
            norm_square(mem_tok, 0, Q_MEM)
            hi(2)
            norm_square(mem_tok, 1, Q_MEM)
            row_copy(0, tok(0))
            hi(3)
            norm_split_hi(N_MEM, 0, mem_h)
            norm_split_hi(N_MEM, 1, mem_h)
            act.wait_ge(ang_ready, 1)
            act.activation(sincos[:, :, :, :].rearrange("p a t f -> p (a t f)"),
                           ang[:, :, :, :].rearrange("p a t f -> p (a t f)"), ACT.Sin).then_inc(sincos_ready, 1)
            act.wait_ge(rows_t, 1)
            act.activation(cols_a[:, :], tok(2)[:, 0:ROWS_A], ACT.Copy).then_inc(cols_ready, 1)
            act.activation(cols_b[:, :], tok(2)[:, P:P + 4 * CONV_W], ACT.Copy).then_inc(cols_ready, 1)
            act.activation(cols_g[:, KD:], tok(2)[:, 2 * P + KD:2 * P + KD * len(GAIN_COLS)], ACT.Copy).then_inc(cols_ready, 1)
            act.activation(ws_t[:, :, :].rearrange("p g t -> p (g t)"), tok(3), ACT.Copy).then_inc(cols_ready, 1)
            act.wait_ge(sig_in, 1)
            act.activation(sig1[:, :, :], sig1[:, :, :], ACT.Sigmoid).then_inc(sig_ready, 1)
            hi(4)
            hi(5)
            act.wait_ge(sig_in, 2)
            act.activation(sig1[:, :, :], sig1[:, :, :], ACT.Sigmoid).then_inc(sig_ready, 1)
            hi(6)
            hi(7)
            used_slab(I_QK + 1)
            for tb in range(TB):
                act.activation(qk[:, tb, :], tok(tb), ACT.Copy, scale=r_mix[:, tb:tb + 1]).then_inc(qk_ready, 1)
            hi(8)
            hi(9)
            used_slab(I_RV + 1)
            for tb in range(TB):
                act.activation(rv[:, tb, :], tok(2 + tb), ACT.Copy, scale=r_mix[:, tb:tb + 1]).then_inc(rv_ready, 1)
            hi(10)
            hi(11)
            for b in range(2):
                act.wait_ge(qk_t, b + 1)
                act.activation(qkT[:, 2 * b:2 * b + 2, :], blocks(tok(b)), ACT.Copy).then_inc(qkT_ready, 1)

            def decay(hd):
                if hd >= 2:
                    act.wait_ge(s_dec_ready, hd - 1)
                act.activation(dec[:, hd % 2, :], dist[:, :], ACT.Exp, scale=float(LOG_G[hd])).then_inc(dec_ready, 1)

            decay(0)
            decay(1)
            act.wait_ge(rg_in, 1)
            act.activation(rgs[:, 0:2, :], rgs[:, 0:2, :], ACT.Silu).then_inc(rg_ready, 1)
            hi(12)
            for hd in range(2, 4):
                decay(hd)
            act.wait_ge(rg_in, 2)
            act.activation(rgs[:, 2:4, :], rgs[:, 2:4, :], ACT.Silu).then_inc(rg_ready, 1)
            hi(13)
            for hd in range(4, RET_HEADS):
                decay(hd)

            def keys(i, j, bank):
                used_slab(i + j)
                act.activation(kT[:, 2 * j:2 * j + 2, :], blocks(feat(bank)), ACT.Copy).then_inc(k_ready, 1)

            def values(i):
                used_slab(i + 3)
                for m in range(2):
                    for half in range(2):
                        act.activation(vm[:, m, half * HALF:(half + 1) * HALF], tok(2 * m + half), ACT.Copy).then_inc(v_ready, 1)

            keys(I_K1, 0, 0)
            hi(14)
            keys(I_K1, 1, 1)
            hi(15)
            act.wait_ge(ry_centred, 1)
            act.activation(ry_sq[:, :, :], ry[:, :, :], ACT.Square).then_inc(ry_squared, 1)
            keys(I_K1, 2, 0)
            hi(16)
            keys(I_K1, 3, 1)
            hi(17)
            act.wait_ge(ret_ready, 1)
            used_slab(I_RG + 1)
            act.activation(xh[:, 4:8, :], retT[:, :, :], ACT.Copy).then_inc(ret_hi, 1)
            hi(18)
            hi(19)
            hi(20)
            act.wait_ge(conv_centred, 1)
            act.activation(c_sq[:, :, :], c_acc[:, :, :], ACT.Square).then_inc(conv_squared, 1)
            act.wait_ge(ret_lo, 1)
            values(I_V1)
            hi(21)
            act.wait_ge(conv_normed, 1)
            for c in range(4):
                ins = act.activation(c_out[:, c, :], c_acc[:, c, :], ACT.Silu, bias=cols_a[:, ROW_OF["conv_ln_b"] + c:ROW_OF["conv_ln_b"] + c + 1],
                                     scale=cols_a[:, ROW_OF["conv_ln_w"] + c:ROW_OF["conv_ln_w"] + c + 1])
                ins.then_inc(conv_out, 1)
            act.wait_ge(conv_out, 4)
            act.activation(xh[:, 0:4, :], c_out[:, :, :], ACT.Copy).then_inc(conv_hi, 1)
            boundary(R_XA, Q_XA, I_Q1)

            def x_attention(b, i_q, i_o, split):
                def q(j):
                    used_slab(i_q + j)
                    act.activation(qT[:, 2 * j:2 * j + 2, :], blocks(feat(j)), ACT.Copy).then_inc(xq_ready, 1)
                    if split:
                        hi(i_o + j)

                def exps(hd):
                    for u in range(TB * hd, TB * hd + TB):
                        act.wait_ge(xmax_ready, 8 * b + u + 1)
                        act.activation(prob[:, u, :], tok(u % 4)[:, 0:NMEM], ACT.Exp, bias=xneg[:, u:u + 1], scale=r_xa[:, u % TB:u % TB + 1],
                                       accum_out=xsum[:, u:u + 1]).then_inc(xexp_ready, 1)

                def p_t(hd):
                    act.wait_ge(xp_t, 4 * b + hd + 1)
                    if hd >= 2:
                        act.wait_ge(xo_ready, 4 * b + hd - 1)
                    act.activation(probT[:, hd % 2, :, :], blocks(feat(hd)), ACT.Copy).then_inc(xpT_ready, 1)

                def out_hi(hd):
                    act.wait_ge(xo_ready, 4 * b + hd + 1)
                    act.activation(xh[:, 2 * hd:2 * hd + 2, :], blocks(feat(hd)), ACT.Copy).then_inc(xo_hi, 1)

                q(0)
                q(1)
                exps(0)
                q(2)
                exps(1)
                q(3)
                p_t(0)
                exps(2)
                out_hi(0)
                p_t(1)
                exps(3)
                out_hi(1)
                p_t(2)
                out_hi(2)
                p_t(3)
                out_hi(3)

            x_attention(0, I_Q1, I_O1, True)
            boundary(R_MLP, Q_MLP, I_FF1)

            def mlp1(g, first=False, splits=True):
                step = 0 if first else 4 * g
                two = 0 if first else 2 * g
                for c in range(2):
                    act.wait_ge(slab_used, I_FF1 + c + 1 + step)
                    if not first:
                        act.wait_ge(ff_lo, two - 1 + c)
                    act.activation(ff_r[:, c, :], feat(c), ACT.Relu).then_inc(relu_ready, 1)
                    act.wait_ge(relu_ready, two + c + 1)
                    act.activation(ff_h[:, 2 * c:2 * c + 2, :], blocks(ff_r[:, c, :]), ACT.Square).then_inc(ff_hi, 1)
                    if splits:
                        hi(I_FF1 + 4 + c, step, 0 if first else g)
                if splits:
                    for c in range(2, 4):
                        hi(I_FF1 + 4 + c, step, 0 if first else g)

            mlp1(0, first=True)
            with act.Fori(1, G1 - 1) as g:
                mlp1(g)
            mlp1(G1 - 1, splits=False)
            hi(I_SBQK)
            hi(I_SBQK + 1)
            raw_split_hi(R_MIX2, 0)
            raw_split_hi(R_MIX2, 1)
            for tb in range(TB):
                norm_square(h, tb, Q_F, hg_sq[:, tb, :])
            for tb in range(TB):
                norm_square(xn, tb, Q_MIX2, hg_sq[:, tb, :])
            hi(I_SBQK + 2)
            hi(I_SBQK + 3)

            def sb_logs(p):
                act.wait_ge(sb_z, p + 1)
                z = ps[:, 0:2, 0:SB_COLS]
                if p > 0:
                    act.wait_ge(sb_z_read, p)
                    act.wait_ge(sb_exp, p)
                after(act.activation(sb_e[:, :, :], z, ACT.Abs))
                after(act.activation(sb_e[:, :, :], sb_e[:, :, :], ACT.Exp, scale=-1.0))
                act.activation(sb_l[:, :, :], sb_e[:, :, :], ACT.Ln, bias=1.0).then_inc(sb_log, 1)

            def sb_exps(p):
                act.wait_ge(sb_arg, p + 1)
                if p > 0:
                    act.wait_ge(sb_out, p)
                act.activation(sb_a[:, :, :], sb_e[:, :, :], ACT.Exp).then_inc(sb_exp, 1)

            def sb_split(p):
                act.wait_ge(sb_out, p + 1)
                act.activation(y_h[0][:, p, :], tok(2)[:, 0:S], ACT.Copy).then_inc(sb_hi, 1)

            SB_AT = {}

            def at_slab(i, step, p):
                SB_AT.setdefault(i, []).append((step, p))

            for p in range(4):
                at_slab(SB_START + 4 * p, sb_logs, p)
                at_slab(SB_START + 4 * p + 4, sb_exps, p)
                at_slab(SB_START + 4 * p + 6, sb_split, p)

            def beside(i):
                for step, p in SB_AT.get(i, ()):
                    step(p)

            for j in range(4):
                hi(I_SBQK + 4 + j)
                if j == 2:
                    row_copy(1, tok(3))
            used_slab(I_SBV + 1)
            for tb in range(TB):
                act.activation(v2[:, tb, :], tok(tb), ACT.Copy, scale=r_mix2[:, tb:tb + 1]).then_inc(sbv_ready, 1)
            hi(I_SBV + 4)
            hi(I_SBV + 5)
            for j in range(2):
                act.wait_ge(ug_in, j + 1)
                act.activation(ug[:, 2 * j:2 * j + 2, :], ug[:, 2 * j:2 * j + 2, :], ACT.Gelu).then_inc(ug_ready, 1)
                hi(I_ZU + 4 + j)
            used_slab(I_ZV + 1)
            for tb in range(TB):
                act.activation(vg[:, tb, :], tok(2 + tb), ACT.Gelu, scale=r_mix2[:, tb:tb + 1]).then_inc(vg_ready, 1)
            hi(I_ZV + 4)
            hi(I_ZV + 5)
            beside(I_ZV + 1)
            for j in range(2):
                hi(I_C3 + 2 * j + 4)
                beside(I_C3 + 2 * j)
                hi(I_C3 + 2 * j + 5)
                beside(I_C3 + 2 * j + 1)
            for j in range(2):
                hi(I_C3 + 8 + j)
                beside(I_C3 + 4 + j)
            act.wait_ge(yb_ready, 2)
            act.activation(y_h[1][:, :, :], ug[:, :, :], ACT.Copy).then_inc(yb_hi, 1)
            act.wait_ge(yc_ready, 2)
            act.activation(y_h[2][:, :, :], acc3[:, :, :], ACT.Copy).then_inc(yc_hi, 1)

            def merged_split(half):
                act.wait_ge(merge_done, 5 + half)
                act.activation(xh[:, 4 * half:4 * half + 4, :], merged[:, 4 * half:4 * half + 4, :], ACT.Copy).then_inc(merged_hi, 1)

            for n in range(BRANCHES):
                for half in range(2):
                    i = I_BR + 6 * n + 3 * half
                    r = 2 * n + half
                    for j in range(2):
                        act.wait_ge(gate_in, 2 * r + j + 1)
                        act.activation(sig2[:, 2 * j:2 * j + 2, :], sig2[:, 2 * j:2 * j + 2, :], ACT.Sigmoid).then_inc(gate_ready, 1)
                        if r == 5 and j == 1:
                            merged_split(0)
                        hi(i + j + 4)
                        beside(i + j)
                    if r < 5:
                        hi(i + 6)
                    beside(i + 2)
                    if r == 3:
                        act.wait_ge(mem2_loaded, 16)
                        act.wait_ge(sb_out, 4)
                        for tb in range(TB):
                            norm_square(mem2_tok, tb, Q_MEM2, mem2_sq[:, tb, :])
            merged_split(1)
            hi(I_OUT2 + 3)
            act.wait_ge(norm_sq, 2 * Q_MEM2 + 2)
            norm_split_hi(N_MEM2, 0, mem2_h, feat)
            norm_split_hi(N_MEM2, 1, mem2_h, feat)
            hi(I_K2)
            hi(I_K2 + 1)
            raw_split_hi(R_XA2, 0)
            hi(I_K2 + 2)
            hi(I_K2 + 3)
            keys(I_K2, 0, 0)
            raw_split_hi(R_XA2, 1)
            hi(I_K2 + 4)
            for tb in range(TB):
                norm_square(h, tb, Q_XA2)
            keys(I_K2, 1, 1)
            hi(I_K2 + 5)
            keys(I_K2, 2, 2)
            hi(I_K2 + 6)
            keys(I_K2, 3, 3)
            hi(I_K2 + 7)
            for j in range(4):
                hi(I_V2 + 4 + j)
                if j == 3:
                    values(I_V2)
            x_attention(1, I_Q2, I_O2, True)
            boundary(R_FF2, Q_FF2, I_FF2)
            row_copy(2, tok(0))

            def glu(g, i, first=False, last=False, step=0, turn=0):
                nxt = ff2_gate(1) if first else i + 3
                if last:
                    hi(N_SLABS - 1)
                elif not first:
                    hi(nxt, step, turn)
                act.wait_ge(glu_in_ready, g + 1)
                if not first:
                    act.wait_ge(glu_ready, g)
                act.activation(ff_r[:, 0, :], ff_u[:, 1, :], ACT.Silu).then_inc(silu_ready, 1)
                if not first and not last:
                    hi(nxt + 1, step, turn)
                    act.wait_ge(slab_used, i + 3 + step)
                act.wait_ge(glu_ready, g + 1)
                act.activation(ff_h[:, 2:4, :] if last else ff_h[:, 0:2, :], blocks(ff_u[:, 0, :]), ACT.Copy).then_inc(glu_hi, 1)
                if not last:
                    hi(nxt + 2, step, turn)

            glu(0, I_FF2, first=True)
            glu(1, ff2_gate(1))
            glu(2, ff2_gate(2))
            with act.Fori(0, G2 - 4) as t:
                glu(t + 3, ff2_gate(3), step=3 * t, turn=t)
            glu(G2 - 1, ff2_gate(G2 - 1), last=True)
            for tb in range(TB):
                act.wait_ge(h_updated, 4 * UPD[I_FF2] + 2 * tb + 2)
                norm_square(h, tb, Q_FINAL)

        @block.vector
        def _(dve):
            count = [0]

            def after(ins):
                count[0] += 1
                ins.then_inc(dve_step, 1)
                dve.wait_ge(dve_step, count[0])

            def lo(i, step=0):
                s = PLACE[i]
                dve.wait_ge(hi_done, i + 1 + step)
                dve.tensor_tensor(w_lo[:, s, :], w_ring[:, s, :], w_hi[:, s, :].bitcast(F32), ALU.subtract).then_inc(lo_done, 1)

            def rsqrt(v, y, t):
                after(dve.tensor_scalar(y.bitcast(I32), v.bitcast(I32), -0.5, RSQRT_MAGIC, ALU.mult, ALU.add))
                for _ in range(3):
                    after(dve.tensor_tensor(t, y, y, ALU.mult))
                    after(dve.scalar_tensor_tensor(t, t, -0.5, v, ALU.mult, ALU.mult))
                    after(dve.scalar_tensor_tensor(y, t, 1.5, y, ALU.add, ALU.mult))

            def scale_rows(tb, src, dst, g, use):
                dve.wait_ge(norm_sq, 2 * use + tb + 1)
                c = slice(2 * use + tb, 2 * use + tb + 1)
                v, y, t = nv[:, tb:tb + 1], ny[:, tb:tb + 1], nt[:, tb:tb + 1]
                after(dve.tensor_scalar(v, sq_sum[:, c], 1.0 / D, EPS, ALU.mult, ALU.add))
                rsqrt(v, y, t)
                dve.wait_ge(gain_loaded, 16 * (g + 1))
                return dve.scalar_tensor_tensor(dst[:, tb, :], src[:, tb, :], y, gain[:, :], ALU.mult, ALU.mult)

            def norm_split_lo(n, tb, hi_t, lo_t, bank=tok):
                for half in range(2):
                    dve.wait_ge(norm_hi, 4 * n + 2 * tb + half + 1)
                    f, t = slice(4 * half, 4 * half + 4), slice(tb * P, (tb + 1) * P)
                    dve.tensor_tensor(lo_t[:, f, t], bank(2 * tb + half).rearrange("p (f t) -> p f t", t=P),
                                      hi_t[:, f, t].bitcast(F32), ALU.subtract).then_inc(norm_lo, 1)

            def raw_split_lo(n, tb):
                for k in range(KD):
                    if k % 4 == 0:
                        dve.wait_ge(raw_hi, 16 * n + 8 * tb + k + 4)
                    t = slice(tb * P, (tb + 1) * P)
                    dve.scalar_tensor_tensor(xl[:, k, t], tok(2 * tb + k // 4)[:, (k % 4) * P:(k % 4 + 1) * P], cols_g[:, KD * n + k:KD * n + k + 1],
                                             xh[:, k, t].bitcast(F32), ALU.mult, ALU.subtract).then_inc(raw_lo, 1)

            def token_scales(use, r):
                dve.wait_ge(norm_sq, 2 * use + 2)
                after(dve.tensor_scalar(nv, sq_sum[:, 2 * use:2 * use + 2], 1.0 / D, EPS, ALU.mult, ALU.add))
                rsqrt(nv, r, nt)

            def memory_rows(n, src, g, use):
                token_scales(use, ny)
                dve.wait_ge(gain_loaded, 16 * (g + 1))
                for tb in range(TB):
                    dve.scalar_tensor_tensor(src[:, tb, :], src[:, tb, :], ny[:, tb:tb + 1], gain[:, :], ALU.mult, ALU.mult).then_inc(norm_xn, 1)
                dve.wait_ge(norm_xn, 2 * n + 2)
                dve.sem_inc(gain_used, 1)

            def scales_on_diagonal(r):
                for tb in range(TB):
                    dve.tensor_scalar(diag[:, tb, :], ident[:, :], r[:, tb:tb + 1], None, ALU.mult).then_inc(diag_ready, 1)

            def row_of_scales(n):
                return r_row[:, n, :].unsqueeze(1).broadcast_to([P, 2, S])

            def update(upd, last_slab, scale=None):
                def block_of(tb):
                    if tb == 0:
                        dve.wait_ge(tb0_done, upd + 1)
                    else:
                        dve.wait_ge(slab_used, last_slab + 1)
                    for half in range(2):
                        c = slice(half * HALF, (half + 1) * HALF)
                        if scale is None:
                            ins = dve.tensor_tensor(h[:, tb, c], tok(2 * tb + half), h[:, tb, c], ALU.add)
                        else:
                            ins = dve.scalar_tensor_tensor(h[:, tb, c], tok(2 * tb + half), scale[:, tb:tb + 1], h[:, tb, c], ALU.mult, ALU.add)
                        ins.then_inc(h_updated, 1)
                return block_of

            def boundary(n, upd, last_slab, use, r, nxt):
                add = update(upd, last_slab)
                lo(nxt)
                lo(nxt + 1)
                for tb in range(TB):
                    add(tb)
                    raw_split_lo(n, tb)
                lo(nxt + 2)
                token_scales(use, r)
                lo(nxt + 3)

            dve.wait_ge(gains_ready, 1)
            raw_split_lo(R_MIX, 0)
            lo(0)
            raw_split_lo(R_MIX, 1)
            lo(1)
            token_scales(Q_MIX, r_mix)
            dve.wait_ge(const_ready, 1)
            scales_on_diagonal(r_mix)
            lo(2)
            memory_rows(N_MEM, mem_tok, G_MEM, Q_MEM)
            lo(3)
            norm_split_lo(N_MEM, 0, mem_h, mem_l)
            norm_split_lo(N_MEM, 1, mem_h, mem_l)
            dve.wait_ge(pos_loaded, 16)
            dve.wait_ge(freq_ready, ROPE_HALF)
            after(dve.tensor_copy(pos_f[:, :], pos_i[:, :]))
            sin_a, cos_a = ang[:, 0, :, :], ang[:, 1, :, :]
            shape = [P, TB, ROPE_HALF]
            after(dve.tensor_tensor(sin_a, pos_f[:, :].unsqueeze(2).broadcast_to(shape), freq[:, :].unsqueeze(1).broadcast_to(shape), ALU.mult))
            after(dve.tensor_scalar(turns[:, :, :], sin_a, 1.0 / (2 * PI), ROUND, ALU.mult, ALU.add))
            after(dve.tensor_scalar(turns[:, :, :], turns[:, :, :], ROUND, None, ALU.subtract))
            for part in (TWO_PI_A, TWO_PI_B, TWO_PI_C):
                after(dve.scalar_tensor_tensor(sin_a, turns[:, :, :], -part, sin_a, ALU.mult, ALU.add))
            after(dve.tensor_scalar(sin_a, sin_a, SIN_MAX, -SIN_MAX, ALU.min, ALU.max))
            after(dve.scalar_tensor_tensor(cos_a, sin_a, -1.0, sin_a, ALU.mult, ALU.max))
            dve.tensor_scalar(cos_a, cos_a, -1.0, PI / 2, ALU.mult, ALU.add).then_inc(ang_ready, 1)
            dve.wait_ge(dist_ready, 1)
            after(dve.tensor_copy(dist[:, :], dist_i[:, :]))
            after(dve.scalar_tensor_tensor(dist[:, :], dist[:, :], -1.0, dist[:, :], ALU.mult, ALU.max))
            after(dve.memset(dist[CHUNK:P, 0:CHUNK], FAR))

            def scaled_gate(j):
                dve.wait_ge(slab_used, 2 * j + 2)
                dve.wait_ge(row_ready, 1)
                dve.tensor_tensor(sig1[:, :, :], blocks(feat(2 * j + 1)), row_of_scales(0), ALU.mult).then_inc(sig_in, 1)

            def gate_conv(j):
                dve.wait_ge(sig_ready, j + 1)
                dve.wait_ge(pad_ready, 1)
                after(dve.tensor_tensor(sig1[:, :, :], sig1[:, :, :], row_of_scales(0), ALU.mult))
                after(dve.tensor_tensor(u_pad[:, 2 * j:2 * j + 2, CONV_W - 1:], blocks(feat(2 * j)), sig1[:, :, :], ALU.mult))
                dve.sem_inc(u_ready, 1)

            done = [0]
            order = [(k, c) for k in range(CONV_W) for c in range(3) if c < 2 or k < TAPS_DVE]
            order = [(k, c, order.index((k - 1, c)) if k else None) for k, c in order]

            def conv(n):
                for m in range(done[0], min(done[0] + n, len(order))):
                    k, c, prev = order[m]
                    if m == 0:
                        dve.wait_ge(u_ready, 2)
                        dve.wait_ge(cols_ready, 2)
                    tap, win = cols_b[:, 4 * k + c:4 * k + c + 1], u_pad[:, c, k:k + S]
                    if k == 0:
                        bias = cols_a[:, ROW_OF["conv_b"] + c:ROW_OF["conv_b"] + c + 1]
                        ins = dve.tensor_scalar(c_acc[:, c, :], win, tap, bias, ALU.mult, ALU.add)
                    else:
                        dve.wait_ge(conv_step, prev + 1)
                        ins = dve.scalar_tensor_tensor(c_acc[:, c, :], win, tap, c_acc[:, c, :], ALU.mult, ALU.add)
                    ins.then_inc(conv_step, 1)
                    done[0] = m + 1

            scaled_gate(0)
            lo(4)
            gate_conv(0)
            lo(5)
            scaled_gate(1)
            lo(6)
            gate_conv(1)
            lo(7)
            conv(12)
            dve.wait_ge(sincos_ready, 1)
            dve.wait_ge(qk_ready, 2)
            for tb in range(TB):
                view = qk[:, tb, :].rearrange("p (g e f) -> p g e f", e=2, f=ROPE_HALF)
                res = qkr[:, tb, :].rearrange("p (g e f) -> p g e f", e=2, f=ROPE_HALF)
                t = [rope_t[:, j, :].rearrange("p (g f) -> p g f", f=ROPE_HALF) for j in range(4)]
                sin, cos = (sincos[:, e, tb, :].unsqueeze(1).broadcast_to([P, 2 * RET_HEADS, ROPE_HALF]) for e in range(2))
                dve.tensor_tensor(t[0], view[:, :, 0, :], cos, ALU.mult)
                dve.tensor_tensor(t[1], view[:, :, 1, :], sin, ALU.mult)
                dve.tensor_tensor(t[2], view[:, :, 0, :], sin, ALU.mult)
                after(dve.tensor_tensor(t[3], view[:, :, 1, :], cos, ALU.mult))
                dve.tensor_tensor(res[:, :, 0, :], t[0], t[1], ALU.subtract)
                after(dve.tensor_tensor(res[:, :, 1, :], t[2], t[3], ALU.add))
                dve.sem_inc(rope_ready, 1)
            lo(8)
            lo(9)
            conv(8)
            lo(10)
            lo(11)
            conv(8)

            def ret_decay(hd):
                dve.wait_ge(ret_s, hd + 1)
                dve.wait_ge(dec_ready, hd + 1)
                if hd >= 2:
                    dve.wait_ge(ret_pv, hd - 1)
                sc = RET_DK ** -0.5
                dve.scalar_tensor_tensor(s_dec[:, hd % 2, 0:S], tok(hd % 4)[:, 0:S], sc, dec[:, hd % 2, :], ALU.mult, ALU.mult)
                after(dve.scalar_tensor_tensor(s_dec[:, hd % 2, S:S + P], tok(hd % 4)[:, S:S + P], sc, dec[:, hd % 2, 0:P], ALU.mult, ALU.mult))
                dve.sem_inc(s_dec_ready, 1)

            def scaled_gate_ret(j):
                dve.wait_ge(slab_used, I_RG + j + 1)
                dve.tensor_tensor(rgs[:, 2 * j:2 * j + 2, :], blocks(feat(j)), row_of_scales(0), ALU.mult).then_inc(rg_in, 1)

            scaled_gate_ret(0)
            ret_decay(0)
            ret_decay(1)
            lo(12)
            scaled_gate_ret(1)
            conv(6)
            ret_decay(2)
            ret_decay(3)
            lo(13)
            conv(4)
            for hd in range(4, RET_HEADS):
                if hd == 6:
                    conv(16)
                ret_decay(hd)
            lo(14)
            dve.wait_ge(ret_pv, RET_HEADS)
            heads = [feat(2 + tb).rearrange("p (g e) -> p g e", e=RET_DV) for tb in range(TB)]
            H8 = [slice(RET_HEADS * tb, RET_HEADS * (tb + 1)) for tb in range(TB)]
            dve.tensor_reduce(r_mean[:, H8[0]], heads[0], AX_X, ALU.add)
            after(dve.tensor_reduce(r_mean[:, H8[1]], heads[1], AX_X, ALU.add))
            after(dve.tensor_scalar(r_mean, r_mean, -1.0 / RET_DV, None, ALU.mult))
            for tb in range(TB):
                after(dve.tensor_tensor(ry[:, tb, :].rearrange("p (g e) -> p g e", e=RET_DV), heads[tb],
                                        r_mean[:, H8[tb]].unsqueeze(2).broadcast_to([P, RET_HEADS, RET_DV]), ALU.add))
            dve.sem_inc(ry_centred, 1)
            conv(4)
            lo(15)
            dve.wait_ge(ry_squared, 1)
            all_heads = [x[:, :, :].rearrange("p t (g e) -> p (t g) e", e=RET_DV) for x in (ry, ry_sq)]
            after(dve.tensor_reduce(r_var, all_heads[1], AX_X, ALU.add))
            after(dve.tensor_scalar(r_var, r_var, 1.0 / RET_DV, EPS, ALU.mult, ALU.add))
            rsqrt(r_var, r_y, r_t)
            dve.tensor_tensor(all_heads[0], all_heads[0], r_y.unsqueeze(2).broadcast_to([P, 2 * RET_HEADS, RET_DV]), ALU.mult).then_inc(ry_ready, 1)
            conv(8)
            lo(16)
            dve.wait_ge(ry_t, 1)
            for f in range(4):
                w = cols_a[:, ROW_OF["ret_gn_w"] + f:ROW_OF["ret_gn_w"] + f + 1]
                ins = dve.scalar_tensor_tensor(retT[:, f, :], feat(2 * (f // 2))[:, (f % 2) * S:(f % 2 + 1) * S], w, rgs[:, f, :], ALU.mult, ALU.mult)
            ins.then_inc(ret_ready, 1)
            conv(6)
            lo(17)
            dve.wait_ge(ret_hi, 1)
            dve.tensor_tensor(xl[:, 4:8, :], retT[:, :, :], xh[:, 4:8, :].bitcast(F32), ALU.subtract).then_inc(ret_lo, 1)
            for i in range(18, 20):
                conv(6)
                lo(i)
                conv(6)
            conv(len(order))
            dve.wait_ge(conv_last, 2 * CONV_W - TAPS_DVE)
            dve.wait_ge(conv_step, len(order))
            dve.tensor_tensor(c_acc[:, 2, :], c_acc[:, 2, :], c_rest[:, :], ALU.add).then_inc(conv_step, 1)
            lo(20)
            dve.wait_ge(conv_mean, 1)
            after(dve.scalar_tensor_tensor(c_acc[:, :, :], feat(2)[:, 0:S].unsqueeze(1).broadcast_to([P, 4, S]), -1.0 / HALF,
                                           c_acc[:, :, :], ALU.mult, ALU.add))
            dve.sem_inc(conv_centred, 1)
            dve.wait_ge(conv_var, 1)
            after(dve.tensor_scalar(n_v[:, :], feat(3)[:, 0:S], 1.0 / HALF, EPS, ALU.mult, ALU.add))
            rsqrt(n_v[:, :], n_y[:, :], n_t[:, :])
            dve.tensor_tensor(c_acc[:, :, :], c_acc[:, :, :], n_y[:, :].unsqueeze(1).broadcast_to([P, 4, S]), ALU.mult).then_inc(conv_normed, 1)
            lo(21)
            dve.wait_ge(conv_hi, 1)
            dve.tensor_tensor(xl[:, 0:4, :], c_out[:, :, :], xh[:, 0:4, :].bitcast(F32), ALU.subtract).then_inc(conv_lo, 1)
            boundary(R_XA, UPD[I_OUT1], I_OUT1 + 3, Q_XA, r_xa, I_Q1)
            after(dve.tensor_scalar(r_xa, r_xa, XA_SCALE, None, ALU.mult))

            def x_attention(b, i_o):
                def maxima(hd):
                    for u in range(TB * hd, TB * hd + TB):
                        dve.wait_ge(xs_ready, 8 * b + u + 1)
                        after(dve.tensor_reduce(xmax[:, u:u + 1], tok(u % 4)[:, 0:NMEM], AX_X, ALU.max))
                        dve.tensor_scalar(xneg[:, u:u + 1], xmax[:, u:u + 1], r_xa[:, u % TB:u % TB + 1], -1.0, ALU.mult, ALU.mult).then_inc(xmax_ready, 1)

                def normalise(hd):
                    for u in range(TB * hd, TB * hd + TB):
                        dve.wait_ge(xexp_ready, 8 * b + u + 1)
                        after(dve.reciprocal(xinv[:, u:u + 1], xsum[:, u:u + 1]))
                        dve.tensor_scalar(prob[:, u, :], prob[:, u, :], xinv[:, u:u + 1], None, ALU.mult).then_inc(xp_ready, 1)

                def out_lo(hd):
                    dve.wait_ge(xo_hi, 4 * b + hd + 1)
                    f = slice(2 * hd, 2 * hd + 2)
                    dve.tensor_tensor(xl[:, f, :], blocks(feat(hd)), xh[:, f, :].bitcast(F32), ALU.subtract).then_inc(xo_lo, 1)

                lo(i_o)
                lo(i_o + 1)
                maxima(0)
                normalise(0)
                lo(i_o + 2)
                maxima(1)
                normalise(1)
                lo(i_o + 3)
                maxima(2)
                normalise(2)
                out_lo(0)
                maxima(3)
                normalise(3)
                for hd in range(1, XA_HEADS):
                    out_lo(hd)

            x_attention(0, I_O1)
            boundary(R_MLP, UPD[I_O1], I_O1 + 3, Q_MLP, r_mlp, I_FF1)
            after(dve.tensor_tensor(r_mlp, r_mlp, r_mlp, ALU.mult))

            def mlp1(g, first=False, splits=True):
                step = 0 if first else 4 * g
                two = 0 if first else 2 * g
                for c in range(2):
                    dve.wait_ge(relu_ready, two + c + 1)
                    dve.tensor_tensor(ff_u[:, c, :], ff_r[:, c, :], ff_r[:, c, :], ALU.mult).then_inc(relu_sq, 1)
                    dve.wait_ge(relu_sq, two + c + 1)
                    dve.wait_ge(ff_hi, two + c + 1)
                    f = slice(2 * c, 2 * c + 2)
                    dve.tensor_tensor(ff_l[:, f, :], blocks(ff_u[:, c, :]), ff_h[:, f, :].bitcast(F32), ALU.subtract).then_inc(ff_lo, 1)
                    if splits:
                        lo(I_FF1 + 4 + c, step)
                if splits:
                    for c in range(2, 4):
                        lo(I_FF1 + 4 + c, step)

            mlp1(0, first=True)
            with dve.Fori(1, G1 - 1) as g:
                mlp1(g)
            mlp1(G1 - 1, splits=False)
            add = update(UPD[I_FF1], I_SBQK - 1, r_mlp)
            lo(I_SBQK)
            lo(I_SBQK + 1)
            dve.wait_ge(gain_loaded, 16 * (G_F + 1))
            for tb in range(TB):
                add(tb)
                for half in range(2):
                    c = slice(half * HALF, (half + 1) * HALF)
                    dve.wait_ge(h_updated, 4 * UPD[I_FF1] + 2 * tb + half + 1)
                    dve.tensor_tensor(xn[:, tb, c], h[:, tb, c], gain[:, c], ALU.mult).then_inc(hg_ready, 1)
                raw_split_lo(R_MIX2, tb)
            dve.sem_inc(gain_used, 1)
            lo(I_SBQK + 2)
            token_scales(Q_F, r_f)
            dve.wait_ge(norm_sq, 2 * Q_MIX2 + 2)
            after(dve.tensor_tensor(nv, r_f, r_f, ALU.mult))
            after(dve.tensor_tensor(nv, nv, sq_sum[:, 2 * Q_MIX2:2 * Q_MIX2 + 2], ALU.mult))
            after(dve.tensor_scalar(nv, nv, 1.0 / D, EPS, ALU.mult, ALU.add))
            rsqrt(nv, r_mix2, nt)
            after(dve.tensor_tensor(r_mix2, r_mix2, r_f, ALU.mult))
            scales_on_diagonal(r_mix2)
            lo(I_SBQK + 3)
            for j in range(4):
                lo(I_SBQK + 4 + j)
                if j == 0:
                    dve.wait_ge(row_ready, 2)
                dve.wait_ge(slab_used, I_SBQK + j + 1)
                dve.scalar_tensor_tensor(qkT2[:, 2 * j:2 * j + 2, :], blocks(feat(j)), SB_DIM ** -0.5 if j < 2 else 1.0, row_of_scales(0),
                                         ALU.mult, ALU.mult).then_inc(sbqk_ready, 1)
            for tb in range(TB):
                dve.tensor_scalar(h[:, tb, :], xn[:, tb, :], r_f[:, tb:tb + 1], None, ALU.mult).then_inc(h_scaled, 1)
            dve.tensor_tensor(r_row[:, 1, :], r_row[:, 0, :], r_row[:, 0, :], ALU.mult).then_inc(h_scaled, 1)
            lo(I_ZV)
            lo(I_ZV + 1)
            for j in range(2):
                dve.wait_ge(slab_used, I_ZU + j + 1)
                dve.tensor_tensor(ug[:, 2 * j:2 * j + 2, :], blocks(feat(j)), row_of_scales(0), ALU.mult).then_inc(ug_in, 1)
                lo(I_ZV + 2 + j)

            def sb_mask(x):
                v = x[:, :, :].rearrange("p e (b t) -> p e b t", t=P)[:, :, 0:3:2, :]
                m = earlier[:, :].unsqueeze(1).unsqueeze(1).broadcast_to([P, 2, 2, P])
                return dve.tensor_tensor(v, v, m, ALU.mult)

            z = ps[:, 0:2, 0:SB_COLS]

            def sb_penalty(p):
                dve.wait_ge(sb_log, p + 1)
                dve.wait_ge(const_ready, 4)
                if p > 0:
                    dve.wait_ge(sb_cum, p)
                after(dve.scalar_tensor_tensor(sb_m[:, :, :], z, 0.0, sb_l[:, :, :], ALU.max, ALU.add))
                after(sb_mask(sb_m))
                dve.sem_inc(sb_pen, 1)
                dve.scalar_tensor_tensor(sb_e[:, :, :], z, 0.0, sb_l[:, :, :], ALU.min, ALU.subtract).then_inc(sb_z_read, 1)

            def sb_argument(p):
                dve.wait_ge(sb_cum, p + 1)
                dve.wait_ge(sb_z_read, p + 1)
                dve.tensor_tensor(sb_e[:, :, :], sb_e[:, :, :], ps[:, 2:4, 0:SB_COLS], ALU.subtract).then_inc(sb_arg, 1)

            def sb_masked(p):
                dve.wait_ge(sb_exp, p + 1)
                sb_mask(sb_a).then_inc(sb_prob, 1)

            def sb_split(p):
                dve.wait_ge(sb_hi, p + 1)
                dve.tensor_tensor(y_l[0][:, p, :], tok(2)[:, 0:S], y_h[0][:, p, :].bitcast(F32), ALU.subtract).then_inc(sb_lo, 1)

            SB_AT, SB_EARLY = {}, {}

            def at_slab(i, step, p, table=SB_AT):
                table.setdefault(i, []).append((step, p))

            for p in range(4):
                at_slab(SB_START + 4 * p + 1, sb_penalty, p, SB_EARLY)
                at_slab(SB_START + 4 * p + 3, sb_argument, p)
                at_slab(SB_START + 4 * p + 5, sb_masked, p, SB_EARLY)
                at_slab(SB_START + 4 * p + 6, sb_split, p)

            def early(i):
                for step, p in SB_EARLY.get(i, ()):
                    step(p)

            def beside(i):
                for step, p in SB_AT.get(i, ()):
                    step(p)

            dve.wait_ge(sgu_loaded, 48)
            for tb in range(TB):
                dve.wait_ge(vg_ready, tb + 1)
                six, two = bn6[:, 6 * tb:6 * tb + 6], bn2[:, 2 * tb:2 * tb + 2]
                v, y, t = nv[:, tb:tb + 1], ny[:, tb:tb + 1], nt[:, tb:tb + 1]
                after(dve.bn_stats(six, vg[:, tb, :]))
                after(dve.bn_aggr(two, six))
                after(dve.tensor_scalar(v, two[:, 1:2], LN_EPS, None, ALU.add))
                rsqrt(v, y, t)
                after(dve.tensor_scalar(vg[:, tb, :], vg[:, tb, :], two[:, 0:1], y, ALU.subtract, ALU.mult))
                after(dve.tensor_tensor(vg[:, tb, :], vg[:, tb, :], ln_g[:, :], ALU.mult))
                dve.tensor_tensor(vg[:, tb, :], vg[:, tb, :], ln_b[:, :], ALU.add).then_inc(vn_ready, 1)
                lo(I_ZV + 4 + tb)
            tap3 = ROW_OF["conv_w_2"]
            for j in range(2):
                early(I_C3 + 2 * j)
                lo(I_C3 + 2 * j + 4)
                beside(I_C3 + 2 * j)
                dve.wait_ge(slab_used, I_C3 + 2 * j + 1)
                dve.wait_ge(h_scaled, TB + 1)
                if j:
                    dve.wait_ge(y3_ready, 1)
                after(dve.tensor_tensor(cc_s[:, :, :], blocks(feat(2 - 2 * j)), row_of_scales(1), ALU.mult))
                dve.wait_ge(pad3_ready, 1)
                dve.wait_ge(slab_used, I_C3 + 2 * j + 2)
                dve.tensor_tensor(y3_pad[:, 2 * j:2 * j + 2, CONV3 - 1:], blocks(feat(3 - 2 * j)), cc_s[:, :, :], ALU.mult).then_inc(y3_ready, 1)
                early(I_C3 + 2 * j + 1)
                lo(I_C3 + 2 * j + 5)
                beside(I_C3 + 2 * j + 1)
            dve.wait_ge(y3_ready, 2)
            for k in range(CONV3):
                for c in range(4):
                    tap, win = cols_a[:, tap3 + 4 * k + c:tap3 + 4 * k + c + 1], y3_pad[:, c, k:k + S]
                    if k == 0:
                        ins = dve.tensor_scalar(acc3[:, c, :], win, tap, None, ALU.mult)
                    else:
                        ins = dve.scalar_tensor_tensor(acc3[:, c, :], win, tap, acc3[:, c, :], ALU.mult, ALU.add)
                    if c == 3:
                        after(ins)
            after(dve.tensor_tensor(acc3[:, :, :], acc3[:, :, :], r_row[:, 0, :].unsqueeze(1).broadcast_to([P, 4, S]), ALU.mult))
            dve.wait_ge(sgu_mixed, 1)
            dve.wait_ge(ug_ready, 2)
            for j in range(2):
                g = slice(2 * j, 2 * j + 2)
                mixed = feat(j).rearrange("p (g b t) -> p g b t", g=2, t=P)
                after(dve.tensor_tensor(vg[:, j, :].rearrange("p (g b t) -> p g b t", g=2, t=P), mixed,
                                        b_sp[:, g, :].unsqueeze(2).broadcast_to([P, 2, TB, P]), ALU.add))
                dve.tensor_tensor(ug[:, g, :], blocks(vg[:, j, :]), ug[:, g, :], ALU.mult).then_inc(yb_ready, 1)
            for j in range(2):
                early(I_C3 + 4 + j)
                lo(I_C3 + 8 + j)
                beside(I_C3 + 4 + j)
                dve.wait_ge(slab_used, I_C3 + 5 + j)
                dve.tensor_tensor(acc3[:, 2 * j:2 * j + 2, :], blocks(feat(2 + j)), acc3[:, 2 * j:2 * j + 2, :], ALU.mult).then_inc(yc_ready, 1)
            dve.wait_ge(yb_hi, 1)
            dve.tensor_tensor(y_l[1][:, :, :], ug[:, :, :], y_h[1][:, :, :].bitcast(F32), ALU.subtract).then_inc(yb_lo, 1)
            dve.wait_ge(yc_hi, 1)
            dve.tensor_tensor(y_l[2][:, :, :], acc3[:, :, :], y_h[2][:, :, :].bitcast(F32), ALU.subtract).then_inc(yc_lo, 1)

            def merged_split(half):
                dve.wait_ge(merged_hi, half + 1)
                f = slice(4 * half, 4 * half + 4)
                dve.tensor_tensor(xl[:, f, :], merged[:, f, :], xh[:, f, :].bitcast(F32), ALU.subtract).then_inc(merged_lo, 1)

            for n in range(BRANCHES):
                for half in range(2):
                    i = I_BR + 6 * n + 3 * half
                    r = 2 * n + half
                    for j in range(2):
                        dve.wait_ge(slab_used, i + j + 1)
                        dve.tensor_tensor(sig2[:, 2 * j:2 * j + 2, :], blocks(feat(j)), row_of_scales(0), ALU.mult).then_inc(gate_in, 1)
                        if r == 5 and j == 1:
                            merged_split(0)
                        early(i + j)
                        lo(i + j + 4)
                        beside(i + j)
                    dve.wait_ge(gate_ready, 2 * r + 2)
                    dve.wait_ge(slab_used, i + 3)
                    m = merged[:, 4 * half:4 * half + 4, :]
                    if n == 0:
                        for j in range(2):
                            ins = dve.tensor_tensor(m[:, 2 * j:2 * j + 2, :], blocks(feat(2 + j)), sig2[:, 2 * j:2 * j + 2, :], ALU.mult)
                            after(ins)
                    else:
                        for j in range(2):
                            s2 = sig2[:, 2 * j:2 * j + 2, :]
                            after(dve.tensor_tensor(s2, blocks(feat(2 + j)), s2, ALU.mult))
                        after(dve.tensor_tensor(m, m, sig2[:, :, :], ALU.add))
                    dve.sem_inc(merge_done, 1)
                    early(i + 2)
                    if r < 5:
                        lo(i + 6)
                    beside(i + 2)
            merged_split(1)
            lo(I_OUT2 + 3)
            memory_rows(N_MEM2, mem2_tok, G_MEM2, Q_MEM2)
            norm_split_lo(N_MEM2, 0, mem2_h, mem2_l, feat)
            norm_split_lo(N_MEM2, 1, mem2_h, mem2_l, feat)
            add = update(UPD[I_OUT2], I_OUT2 + 3)
            lo(I_K2)
            lo(I_K2 + 1)
            add(0)
            raw_split_lo(R_XA2, 0)
            add(1)
            lo(I_K2 + 2)
            lo(I_K2 + 3)
            raw_split_lo(R_XA2, 1)
            lo(I_K2 + 4)
            token_scales(Q_XA2, r_xa)
            after(dve.tensor_scalar(r_xa, r_xa, XA_SCALE, None, ALU.mult))
            for i in range(I_K2 + 5, I_Q2 + 4):
                lo(i)
            x_attention(1, I_O2)
            boundary(R_FF2, UPD[I_O2], I_O2 + 3, Q_FF2, r_ff2, I_FF2)
            scales_on_diagonal(r_ff2)

            def glu(g, i, first=False, last=False, step=0):
                nxt = ff2_gate(1) if first else i + 3
                dve.wait_ge(slab_used, i + 1 + step)
                if first:
                    dve.wait_ge(row_ready, 3)
                dve.tensor_tensor(blocks(ff_u[:, 1, :]), blocks(feat(2 if first else 0)), row_of_scales(0), ALU.mult).then_inc(glu_in_ready, 1)
                if last:
                    lo(N_SLABS - 1)
                elif not first:
                    lo(nxt, step)
                dve.wait_ge(silu_ready, g + 1)
                dve.wait_ge(slab_used, i + 2 + step)
                if not first:
                    dve.wait_ge(glu_lo, g)
                dve.tensor_tensor(ff_u[:, 0, :], feat(3 if first else 1), ff_r[:, 0, :], ALU.mult).then_inc(glu_ready, 1)
                if not first and not last:
                    lo(nxt + 1, step)
                dve.wait_ge(glu_hi, g + 1)
                f = slice(2, 4) if last else slice(0, 2)
                dve.tensor_tensor(ff_l[:, f, :], blocks(ff_u[:, 0, :]), ff_h[:, f, :].bitcast(F32), ALU.subtract).then_inc(glu_lo, 1)
                if not last:
                    lo(nxt + 2, step)

            glu(0, I_FF2, first=True)
            glu(1, ff2_gate(1))
            glu(2, ff2_gate(2))
            with dve.Fori(0, G2 - 4) as t:
                glu(t + 3, ff2_gate(3), step=3 * t)
            glu(G2 - 1, ff2_gate(G2 - 1), last=True)
            add = update(UPD[I_FF2], N_SLABS - 1, r_ff2)
            for tb in range(TB):
                add(tb)
            for tb in range(TB):
                scale_rows(tb, h, xn, G_FINAL, Q_FINAL).then_inc(out_ready, 1)


def kernel(**inputs):
    import concourse.bacc as bacc
    from concourse.bass_utils import run_bass_kernel_spmd

    nc = bacc.Bacc("TRN2", target_bir_lowering=False, num_devices=1)
    arrays, aps = {}, {}
    for name in INPUTS:
        x = np.ascontiguousarray(inputs[name])
        arrays[f"in_{name}"] = x
        aps[name] = nc.dram_tensor(f"in_{name}", x.shape, mybir.dt.from_np(x.dtype), kind="ExternalInput").ap()
    out = nc.dram_tensor("out", (1, S, D), F32, kind="ExternalOutput").ap()
    build(nc, aps, out)
    r = run_bass_kernel_spmd(nc, [arrays], core_ids=[0])
    return r.results[0]["out"]
```

```python
from contextlib import ExitStack

import numpy as np

import concourse.bass as bass
from concourse import mybir

F32 = mybir.dt.float32
F32R = mybir.dt.float32r
I32 = mybir.dt.int32
ACT = mybir.ActivationFunctionType
ALU = mybir.AluOpType
AX_X = mybir.AxisListType.X

P = 128
D = 1024
S = 256
TB = S // P
KD = D // P
HALF = D // 2
NMEM = 256
EPS = 1e-6
LN_EPS = 1e-5
SLAB = 2048
RING = 4

CONV_W = 31
RET_HEADS, RET_DK, RET_DV, CHUNK = 8, 32, 64, 64
ROPE_HALF = RET_DK // 2
XA_HEADS = 4
XA_SCALE = float(D // XA_HEADS) ** -0.5
D_FF = 4 * D
SB_DIM = 64
SB_COLS = S + P
SGU_GROUPS = 4
CONV3 = 3
BRANCHES = 3
HID2 = 2816
G1 = D_FF // 512
G2 = HID2 // 256

LOG_G = np.log1p(-np.exp2(-5.0 - np.arange(RET_HEADS)))
INV_FREQ = (10000.0 ** (-np.arange(ROPE_HALF) / ROPE_HALF)).astype(np.float32)
FAR = 1.0e9
PI = float(np.pi)
TWO_PI_A = 6.28125
TWO_PI_B = float(np.float32(np.round((2 * np.pi - TWO_PI_A) * 2 ** 22) / 2 ** 22))
TWO_PI_C = float(2 * np.pi - TWO_PI_A - TWO_PI_B)
SIN_MAX = 3.1415925
ROUND = 12582912.0
RSQRT_MAGIC = 1597463007.0

I_CONV, I_QK, I_RV, I_RG = 0, 4, 6, 8
I_K1, I_V1 = 10, 14
I_OUT1 = 18
I_Q1, I_O1 = 22, 26
I_FF1 = 30
I_SBQK = I_FF1 + 4 * G1
I_SBV, I_ZU, I_ZV, I_C3, I_BR = I_SBQK + 4, I_SBQK + 6, I_SBQK + 8, I_SBQK + 10, I_SBQK + 16
I_OUT2 = I_BR + 6 * BRANCHES
I_K2, I_V2 = I_OUT2 + 4, I_OUT2 + 8
I_Q2, I_O2 = I_OUT2 + 12, I_OUT2 + 16
I_FF2 = I_OUT2 + 20
N_SLABS = I_FF2 + 3 * G2
BRANCH_ORDER = (1, 2, 0)

R_MIX, R_XA, R_MLP, R_MIX2, R_XA2, R_FF2 = range(6)
GAIN_COLS = ["norm_mix_w", "norm_xattn_w", "norm_mlp_w", "norm_mix_g_2", "norm_xa_g_2", "norm_ffn_g_2", "norm_f_w"]
C_F = 6
G_MEM, G_F, G_MEM2, G_FINAL = range(4)
GAIN_ROWS = ["norm_mem_w", "norm_f_w", "mem_norm_g_2", "final_g_2"]
N_MEM, N_MEM2 = range(2)
Q_MIX, Q_MEM, Q_XA, Q_MLP, Q_F, Q_MIX2, Q_MEM2, Q_XA2, Q_FF2 = range(9)


def slab_places():
    place, uses, before, last, count = [], [], [], {}, {}
    for i in range(N_SLABS):
        s = i % RING
        if i >= I_FF2:
            j = i - I_FF2
            s = j % RING if j < 5 else (1, 2, 3)[(j - 5) % 3]
            if i == N_SLABS - 1:
                s = 0
        place.append(s)
        uses.append(count.get(s, 0))
        before.append(last.get(s))
        count[s] = uses[-1] + 1
        last[s] = i
    return place, uses, before


PLACE, USES, BEFORE = slab_places()


ROW_OF = {"conv_b": 0, "conv_ln_w": 4, "conv_ln_b": 8, "ret_gn_w": 12, "conv_w_2": 16}
ROWS_A = 16 + 4 * CONV3
RET_COLS = S + P
TAPS_DVE = 23
TAP_BATCH = 6
POOL_TAPS = [(c, k) for c in (3, 2) for k in range(CONV_W)] + [(1, k) for k in range(TAPS_DVE, CONV_W)]
FIRST_TAPS = [n for n, ck in enumerate(POOL_TAPS) if ck in ((3, 0), (2, 0), (1, TAPS_DVE))]
ACT_TAPS = [n for n in range(2, len(POOL_TAPS)) if n not in FIRST_TAPS and (n - 2) % (TAP_BATCH + 1) < TAP_BATCH]
OUT1_ORDER = (2, 3, 0, 1)
C3_COLS = [(5 + w) * HALF + 256 * j for j in range(2) for w in (1, 2)] + [5 * HALF, 5 * HALF + 256]
SB_START = I_ZV + 1
ARENA, ARENA_WORDS = 16512, 53184

INPUTS = ["x", "mem", "positions", "norm_mix_w", "w_in", "conv_w", "conv_b", "conv_ln_w", "conv_ln_b", "ret_gn_w", "w_out",
          "norm_xattn_w", "norm_mem_w", "xq_w", "xkv_w", "xo_w", "norm_mlp_w", "mlp_up_w", "mlp_down_w", "norm_f_w",
          "mem_2", "norm_mix_g_2", "w_in_2", "sgu_ln_g_2", "sgu_ln_b_2", "w_spatial_2", "b_spatial_2", "conv_w_2",
          "w_branch_2", "w_out_2", "norm_xa_g_2", "mem_norm_g_2", "w_q_xa_2", "w_k_xa_2", "w_v_xa_2", "w_o_xa_2",
          "norm_ffn_g_2", "w_gate_ffn_2", "w_up_ffn_2", "w_down_ffn_2", "final_g_2"]


def ff2_gate(g):
    return I_FF2 if g == 0 else I_FF2 + 3 * g - 1


def raw_pieces(n, tb):
    if n == R_MIX:
        return [(bank, 2 * m, 2 * m + 2) for m, bank in enumerate((5, 6, 7, 0) if tb else (0, 1, 2, 3))]
    if tb == 0:
        return [(0, 0, 4), (1, 4, 8)]
    return [(bank, 2 * m, 2 * m + 2) for m, bank in enumerate((0, 2, 1, 3))]


def pieces_before(n, tb):
    return sum(len(raw_pieces(m, t)) for m in range(n + 1) for t in range(2) if (m, t) < (n, tb))


def build(nc, a, out):
    with ExitStack() as ctx:
        arena = ctx.enter_context(nc.sbuf_tensor("arena", [P, ARENA_WORDS], F32))
        cursor = [0]

        def at(name, shape, off, dt=F32):
            assert off + int(np.prod(shape[1:])) <= ARENA_WORDS, (name, off)
            return nc.alloc_sbuf_tensor_at(name, shape, dt, offset=ARENA + 4 * off)

        def new(name, shape, dt=F32):
            t = at(name, shape, cursor[0], dt)
            cursor[0] += -(-int(np.prod(shape[1:])) // 8) * 8
            return t

        w_ring = new("w_ring", [P, RING, SLAB])
        w_hi = new("w_hi", [P, RING, SLAB], F32R)
        w_lo = new("w_lo", [P, RING, SLAB], F32R)
        h = new("h", [P, TB, D])
        xh = new("xh", [P, KD, S], F32R)
        xl = new("xl", [P, KD, S], F32R)
        xn0 = cursor[0]
        xn = new("xn", [P, TB, D])
        gain = new("gain", [P, D])
        r_row = new("r_row", [P, 2, S])
        diag = new("diag", [P, TB, P])
        cols_g = new("cols_g", [P, KD * len(GAIN_COLS)])
        ident = new("ident", [P, P])
        ones = new("ones", [P, P])
        later = new("later", [P, P])
        earlier = new("earlier", [P, P])
        cols_a = new("cols_a", [P, ROWS_A])
        cols_b = new("cols_b", [P, CONV_W * 4])
        stat = new("stat", [P, 256])
        ln_g = new("ln_g", [P, HALF])
        ln_b = new("ln_b", [P, HALF])
        b_sp = new("b_sp", [P, SGU_GROUPS, P])
        ws_t = new("ws_t", [P, SGU_GROUPS, P])
        kv0 = cursor[0]
        kT = new("kT", [P, KD, NMEM])
        vm = new("vm", [P, 2, D])
        split0 = cursor[0]
        mem_h = new("mem_h", [P, KD, NMEM], F32R)
        mem_l = new("mem_l", [P, KD, NMEM], F32R)
        t0 = cursor[0]
        k_at, v_at = [(split0, split0 + 2 * D), (kv0, split0)], [(kv0, kv0 + 2 * D), (kv0 + 2 * D, split0 + 2 * D)]
        k_split = [[at(f"k{b + 1}_{part}", [P, KD, NMEM], off, F32R) for part, off in zip("hl", k_at[b])] for b in range(2)]
        v_split = [[at(f"v{b + 1}_{part}", [P, 2, D], off, F32R) for part, off in zip("hl", v_at[b])] for b in range(2)]

        u_pad = new("u_pad", [P, 4, CONV_W - 1 + S])
        c_acc = new("c_acc", [P, 4, S])
        c_tap = at("c_tap", [P, S], xn0)
        c_rest = at("c_rest", [P, S], xn0 + S)
        c_prod = at("c_prod", [P, TAP_BATCH, S], xn0 + 2 * S)
        rgs = new("rgs", [P, 4, S])
        mt0 = cursor[0]
        qkT = new("qkT", [P, 4, S])
        rv = new("rv", [P, TB, HALF])
        mem_tok = at("mem_tok", [P, 2, D], mt0)
        m1 = cursor[0]
        sig1 = at("sig1", [P, 2, S], m1)
        rope_t = at("rope_t", [P, 4, 256], m1)
        dec = at("dec", [P, RET_HEADS, S], kv0)
        s_dec = at("s_dec", [P, 2, RET_COLS], m1 + 2 * S)
        n_v, n_y, n_t = (at(f"n_{x}", [P, S], m1 + S * i) for i, x in enumerate("vyt"))
        cursor[0] = m1 + 2 * S + 2 * RET_COLS
        dist_i = at("dist_i", [P, S], cursor[0], I32)
        dist = new("dist", [P, S])
        ang = new("ang", [P, 2, TB, ROPE_HALF])
        sincos = new("sincos", [P, 2, TB, ROPE_HALF])
        turns = new("turns", [P, TB, ROPE_HALF])
        pos_i = new("pos_i", [P, TB], I32)
        pos_f = new("pos_f", [P, TB])
        freq = new("freq", [P, ROPE_HALF])
        qk = at("qk", [P, TB, HALF], kv0 + 2 * D)
        ry = at("ry", [P, TB, HALF], kv0 + 2 * D)
        qkr = at("qkr", [P, TB, HALF], kv0 + 3 * D)
        ry_sq = at("ry_sq", [P, TB, HALF], kv0 + 3 * D)
        retT = at("retT", [P, 4, S], kv0 + 3 * D)
        c_sq = at("c_sq", [P, 4, S], t0)
        c_out = at("c_out", [P, 4, S], t0)
        rows_a = at("rows_a", [ROWS_A, P], kv0)
        rows_b = at("rows_b", [CONV_W * 4, P], kv0 + P)
        ws_rows = at("ws_rows", [P, SGU_GROUPS, P], kv0 + 2 * P)
        rows_g = at("rows_g", [KD * len(GAIN_COLS), P], kv0 + 6 * P)

        cursor[0] = t0
        q_h, q_l = new("q_h", [P, KD, S], F32R), new("q_l", [P, KD, S], F32R)
        prob = new("prob", [P, 2 * TB, NMEM])
        probT_h, probT_l = new("probT_h", [P, 2, 2, S], F32R), new("probT_l", [P, 2, 2, S], F32R)

        cursor[0] = t0
        ff_r = new("ff_r", [P, 2, 2 * S])
        ff_u = new("ff_u", [P, 2, 2 * S])
        hg_sq = at("hg_sq", [P, TB, D], t0)
        ff_h = at("ff_h", [P, 4, S], split0, F32R)
        ff_l = at("ff_l", [P, 4, S], split0 + D, F32R)

        cursor[0] = t0
        mem2_tok = at("mem2_tok", [P, 2, D], t0)
        qkT2 = new("qkT2", [P, 8, S])
        sb0 = cursor[0]
        mem2_h = at("mem2_h", [P, KD, NMEM], sb0, F32R)
        mem2_l = at("mem2_l", [P, KD, NMEM], sb0 + 2 * D, F32R)
        mem2_sq = at("mem2_sq", [P, 2, D], sb0)
        sb_e = new("sb_e", [P, 2, SB_COLS])
        sb_l = new("sb_l", [P, 2, SB_COLS])
        sb_m = new("sb_m", [P, 2, SB_COLS])
        sb_a = new("sb_a", [P, 2, SB_COLS])
        ug = new("ug", [P, 4, S])
        v2 = new("v2", [P, TB, HALF])
        y3_pad = at("y3_pad", [P, 4, CONV3 - 1 + S], kv0)
        cc_s = at("cc_s", [P, 2, S], kv0 + 4 * (CONV3 - 1 + S))
        acc3 = at("acc3", [P, 4, S], kv0 + 4 * (CONV3 - 1 + S) + 2 * S)
        merged = at("merged", [P, KD, S], kv0)
        vg = at("vg", [P, TB, HALF], kv0 + 3 * D)
        sig2 = at("sig2", [P, 4, S], kv0 + 3 * D)
        y_h = [at("ya_h", [P, 4, S], xn0, F32R), at("yb_h", [P, 4, S], split0, F32R),
               at("yc_h", [P, 4, S], split0 + 2 * D, F32R)]
        y_l = [at("ya_l", [P, 4, S], xn0 + D, F32R), at("yb_l", [P, 4, S], split0 + D, F32R),
               at("yc_l", [P, 4, S], split0 + 3 * D, F32R)]

        used = [0]

        def cols(n):
            used[0] += n
            assert used[0] <= 256
            return stat[:, used[0] - n:used[0]]

        sq_sum = cols(2 * 9)
        sq_last = cols(4)
        nv, ny, nt = cols(2), cols(2), cols(2)
        r_mix, r_mem, r_xa, r_mlp, r_f, r_mix2, r_ff2 = (cols(2) for _ in range(7))
        xmax, xneg, xsum, xinv = cols(8), cols(8), cols(8), cols(8)
        r_mean, r_var, r_y, r_t = cols(16), cols(16), cols(16), cols(16)
        bn6, bn2 = cols(6 * TB), cols(2 * TB)

        ps = ctx.enter_context(nc.psum_tensor("ps", [P, 8, 512], F32))

        def tok(b):
            return ps[:, b, :]

        def feat(b):
            return ps[:, 4 + b, :]

        def blocks(x):
            return x.rearrange("p (t n) -> p t n", n=S)

        def sem(name):
            return ctx.enter_context(nc.semaphore(name))

        w_loaded = [sem(f"w_loaded{s}") for s in range(RING)]
        hi_done, lo_done, slab_used = sem("hi_done"), sem("lo_done"), sem("slab_used")
        first_loaded, first_hi, first_lo = sem("first_loaded"), sem("first_hi"), sem("first_lo")
        x_loaded = [sem("x_loaded0"), sem("x_loaded1")]
        mem_loaded, mem2_loaded = sem("mem_loaded"), sem("mem2_loaded")
        rows_loaded, pos_loaded, sgu_loaded = sem("rows_loaded"), sem("pos_loaded"), sem("sgu_loaded")
        gain_loaded, gain_used = sem("gain_loaded"), sem("gain_used")
        gain_mix_loaded, gains_t, gains_ready = sem("gain_mix_loaded"), sem("gains_t"), sem("gains_ready")
        raw_t, raw_hi, raw_lo, hg_ready, h_scaled = sem("raw_t"), sem("raw_hi"), sem("raw_lo"), sem("hg_ready"), sem("h_scaled")
        diag_ready, row_t, row_ready = sem("diag_ready"), sem("row_t"), sem("row_ready")
        sig_in, rg_in, ug_in, gate_in, glu_in_ready = (sem(x) for x in ("sig_in", "rg_in", "ug_in", "gate_in", "glu_in_ready"))
        fill, const_ready, dist_ready, dist_set, freq_ready = sem("fill"), sem("const_ready"), sem("dist_ready"), sem("dist_set"), sem("freq_ready")
        pad_ready, ws_masked, pad3_ready = sem("pad_ready"), sem("ws_masked"), sem("pad3_ready")
        act_step, dve_step = sem("act_step"), sem("dve_step")
        norm_sq, norm_xn, norm_t, norm_hi, norm_lo = (sem(f"norm_{x}") for x in ("sq", "xn", "t", "hi", "lo"))
        rows_t, cols_ready = sem("rows_t"), sem("cols_ready")
        ang_ready, sincos_ready = sem("ang_ready"), sem("sincos_ready")
        sig_ready, u_ready, rg_ready, rv_ready, qk_ready = (sem(x) for x in ("sig_ready", "u_ready", "rg_ready", "rv_ready", "qk_ready"))
        rope_ready, qk_t, qkT_ready = sem("rope_ready"), sem("qk_t"), sem("qkT_ready")
        ret_s, dec_ready, s_dec_ready, ret_pv = sem("ret_s"), sem("dec_ready"), sem("s_dec_ready"), sem("ret_pv")
        ry_centred, ry_squared, ry_ready, ry_t = sem("ry_centred"), sem("ry_squared"), sem("ry_ready"), sem("ry_t")
        ret_ready, ret_hi, ret_lo = sem("ret_ready"), sem("ret_hi"), sem("ret_lo")
        conv_step, conv_tap, conv_prod, conv_last = sem("conv_step"), sem("conv_tap"), sem("conv_prod"), sem("conv_last")
        conv_mean, conv_centred = sem("conv_mean"), sem("conv_centred")
        conv_squared, conv_var, conv_normed = sem("conv_squared"), sem("conv_var"), sem("conv_normed")
        conv_out, conv_hi, conv_lo = sem("conv_out"), sem("conv_hi"), sem("conv_lo")
        k_ready, v_ready = sem("k_ready"), sem("v_ready")
        k1_hi, k1_lo, v1_hi, v1_lo, k2_lo, v2_lo = (sem(x) for x in ("k1_hi", "k1_lo", "v1_hi", "v1_lo", "k2_lo", "v2_lo"))
        xq_hi, xp_hi = sem("xq_hi"), sem("xp_hi")
        tb0_done, h_updated = sem("tb0_done"), sem("h_updated")
        xq_ready, xs_ready, xmax_ready, xexp_ready = sem("xq_ready"), sem("xs_ready"), sem("xmax_ready"), sem("xexp_ready")
        xp_ready, xp_t, xpT_ready = sem("xp_ready"), sem("xp_t"), sem("xpT_ready")
        xo_ready, xo_hi, xo_lo = sem("xo_ready"), sem("xo_hi"), sem("xo_lo")
        relu_ready, relu_sq, ff_hi, ff_lo = sem("relu_ready"), sem("relu_sq"), sem("ff_hi"), sem("ff_lo")
        silu_ready, glu_ready, glu_hi, glu_lo = sem("silu_ready"), sem("glu_ready"), sem("glu_hi"), sem("glu_lo")
        sbqk_ready, sbv_ready, ug_ready, vg_ready, vn_ready = (sem(x) for x in ("sbqk_ready", "sbv_ready", "ug_ready", "vg_ready", "vn_ready"))
        sb_z, sb_z_read, sb_log, sb_pen, sb_cum, sb_arg = sem("sb_z"), sem("sb_z_read"), sem("sb_log"), sem("sb_pen"), sem("sb_cum"), sem("sb_arg")
        sb_exp, sb_prob, sb_out, sb_hi, sb_lo = sem("sb_exp"), sem("sb_prob"), sem("sb_out"), sem("sb_hi"), sem("sb_lo")
        sgu_mixed, yb_ready, yb_hi, yb_lo = sem("sgu_mixed"), sem("yb_ready"), sem("yb_hi"), sem("yb_lo")
        y3_ready, yc_ready, yc_hi, yc_lo = sem("y3_ready"), sem("yc_ready"), sem("yc_hi"), sem("yc_lo")
        gate_ready, merge_done, merged_hi, merged_lo = sem("gate_ready"), sem("merge_done"), sem("merged_hi"), sem("merged_lo")
        last_sq, y_ready, out_lead, out_tail, stored = (sem(x) for x in ("last_sq", "y_ready", "out_lead", "out_tail", "stored"))
        sig_scaled = sem("sig_scaled")
        gain_product, last_half = sem("gain_product"), sem("last_half")

        block = ctx.enter_context(nc.Block())

        UPD = {I_OUT1: 0, I_O1: 1, I_FF1: 2, I_OUT2: 3, I_O2: 4, I_FF2: 5}

        @block.sync
        def _(sp):
            def load(i, src, step=0, wait_step=0):
                s = PLACE[i]
                if BEFORE[i] is not None:
                    sp.wait_ge(lo_done, BEFORE[i] + 1 + wait_step)
                dst = w_ring[:, s, :].rearrange("p (k n) -> p k n", n=src.shape[2])
                sp.dma_start(dst, src).then_inc(w_loaded[s], 16)

            def panel_a(w, col, n=256):
                return w.rearrange("(k p) n -> p k n", p=P)[:, :, col:col + n]

            def rows_b_form(w, row, col=0, n=D, nk=2):
                return w[row:row + nk * P, col:col + n].rearrange("(k p) n -> p k n", p=P)

            sp.dma_start(rows_g[0:KD, :], a[GAIN_COLS[0]].rearrange("(f p) -> f p", p=P)).then_inc(gain_mix_loaded, 16)
            w_in = a["w_in"]
            ring0 = w_ring[:, 0, :].rearrange("p (k n) -> p k n", n=256)
            sp.dma_start(ring0[:, 0:4, :], panel_a(w_in, 0)[:, 0:4, :]).then_inc(first_loaded, 16)
            for tb in range(TB):
                sp.dma_start(h[:, tb, :], a["x"][0, tb * P:(tb + 1) * P, :]).then_inc(x_loaded[tb], 16)
            sp.dma_start(ring0[:, 4:8, :], panel_a(w_in, 0)[:, 4:8, :]).then_inc(w_loaded[0], 16)
            load(I_CONV + 1, panel_a(w_in, HALF))
            load(I_CONV + 2, panel_a(w_in, 256))
            sp.dma_start(mem_tok[:, :, :], a["mem"].rearrange("a (t p) d -> p (a t) d", p=P)).then_inc(mem_loaded, 16)
            load(I_CONV + 3, panel_a(w_in, HALF + 256))
            for name, r in ROW_OF.items():
                w = a[name]
                w = w.squeeze(0).rearrange("k (c p) -> (k c) p", p=P) if name == "conv_w_2" else w.rearrange("(c p) -> c p", p=P)
                sp.dma_start(rows_a[r:r + w.shape[0], :], w).then_inc(rows_loaded, 16)
            sp.dma_start(rows_b[:, :], a["conv_w"].rearrange("k (c p) -> (k c) p", p=P)).then_inc(rows_loaded, 16)
            sp.dma_start(ws_rows[:, :, :], a["w_spatial_2"].squeeze(0).rearrange("g t s -> t g s")).then_inc(rows_loaded, 16)
            for n, name in enumerate(GAIN_COLS[1:], 1):
                w = a[name]
                w = w if len(w.shape) == 1 else w.squeeze(0)
                sp.dma_start(rows_g[KD * n:KD * (n + 1), :], w.rearrange("(f p) -> f p", p=P)).then_inc(rows_loaded, 16)
            for j in range(2):
                load(I_QK + j, rows_b_form(w_in, 512 * j, 2 * HALF, HALF, 4))
            for j in range(2):
                load(I_RV + j, rows_b_form(w_in, 512 * j, 3 * HALF, HALF, 4))
            for j in range(2):
                load(I_RG + j, panel_a(w_in, 4 * HALF + 256 * j))
            for j in range(4):
                load(I_K1 + j, panel_a(a["xkv_w"], 256 * j))
            for j in range(4):
                load(I_V1 + j, rows_b_form(a["xkv_w"], 256 * j, D))
            for j, k in enumerate(OUT1_ORDER):
                load(I_OUT1 + j, rows_b_form(a["w_out"], 256 * k))
            for j in range(4):
                load(I_Q1 + j, panel_a(a["xq_w"], 256 * j))
            for j in range(4):
                load(I_O1 + j, rows_b_form(a["xo_w"], 256 * j))
            up = a["mlp_up_w"].rearrange("(k p) n -> p k n", p=P)
            down = a["mlp_down_w"].rearrange("(k p) n -> p k n", p=P)
            with sp.Fori(0, G1) as g:
                for c in range(2):
                    load(I_FF1 + c, up[:, :, bass.ds(g * 512 + 256 * c, 256)], wait_step=4 * g)
                for c in range(2):
                    load(I_FF1 + 2 + c, down[:, bass.ds(g * 4 + 2 * c, 2), :], wait_step=4 * g)
            w2 = a["w_in_2"].squeeze(0)
            for j in range(4):
                load(I_SBQK + j, panel_a(w2, 256 * j))
            for j in range(2):
                load(I_SBV + j, rows_b_form(w2, 512 * j, 2 * HALF, HALF, 4))
            for j in range(2):
                load(I_ZU + j, panel_a(w2, 3 * HALF + 256 * j))
            for j in range(2):
                load(I_ZV + j, rows_b_form(w2, 512 * j, 4 * HALF, HALF, 4))
            for j, col in enumerate(C3_COLS):
                load(I_C3 + j, panel_a(w2, col))
            wb = a["w_branch_2"].squeeze(0)
            for n, br in enumerate(BRANCH_ORDER):
                for half in range(2):
                    i = I_BR + 6 * n + 3 * half
                    for j in range(2):
                        load(i + j, panel_a(w2, 8 * HALF + D * br + HALF * half + 256 * j))
                    load(i + 2, panel_a(wb[br], HALF * half, HALF))
            for j in range(4):
                load(I_OUT2 + j, rows_b_form(a["w_out_2"].squeeze(0), 256 * j))
            for j in range(4):
                load(I_K2 + j, panel_a(a["w_k_xa_2"].squeeze(0), 256 * j))
            for j in range(4):
                load(I_V2 + j, rows_b_form(a["w_v_xa_2"].squeeze(0), 256 * j))
            for j in range(4):
                load(I_Q2 + j, panel_a(a["w_q_xa_2"].squeeze(0), 256 * j))
            for j in range(4):
                load(I_O2 + j, rows_b_form(a["w_o_xa_2"].squeeze(0), 256 * j))
            wg = a["w_gate_ffn_2"].squeeze(0).rearrange("(k p) n -> p k n", p=P)
            wu = a["w_up_ffn_2"].squeeze(0).rearrange("(k p) n -> p k n", p=P)
            wd = a["w_down_ffn_2"].squeeze(0).rearrange("(k p) n -> p k n", p=P)
            load(I_FF2, wg[:, :, 0:256])
            load(I_FF2 + 1, wu[:, :, 0:256])
            for g in range(1, 3):
                i = ff2_gate(g)
                load(i, wg[:, :, 256 * g:256 * g + 256])
                load(i + 1, wu[:, :, 256 * g:256 * g + 256])
                load(i + 2, wd[:, 2 * g - 2:2 * g, :])
            i = ff2_gate(3)
            with sp.Fori(0, G2 - 3) as t:
                load(i, wg[:, :, bass.ds(t * 256 + 768, 256)], wait_step=3 * t)
                load(i + 1, wu[:, :, bass.ds(t * 256 + 768, 256)], wait_step=3 * t)
                load(i + 2, wd[:, bass.ds(t * 2 + 4, 2), :], wait_step=3 * t)
            load(N_SLABS - 1, wd[:, 2 * G2 - 2:2 * G2, :])
            for tb in range(TB):
                for half in range(2):
                    c = slice(half * HALF, (half + 1) * HALF)
                    sp.wait_ge((out_lead, out_tail)[half], tb + 1)
                    sp.dma_start(out[0, tb * P:(tb + 1) * P, c], xn[:, tb, c]).then_inc(stored, 16)
            sp.wait_ge(stored, 16 * 2 * TB)

        @block.gpsimd
        def _(pool):
            def load_gain(n):
                if n > 0:
                    pool.wait_ge(gain_used, n)
                w = a[GAIN_ROWS[n]]
                w = w if len(w.shape) == 1 else w.squeeze(0)
                pool.dma_start(gain[:, :], w.partition_broadcast(P)).then_inc(gain_loaded, 16)

            pool.memset(ident[:, :], 0.0).then_inc(fill, 1)
            pool.memset(later[:, :], 1.0).then_inc(fill, 1)
            pool.memset(earlier[:, :], 1.0).then_inc(fill, 1)
            pool.wait_ge(fill, 3)
            pool.affine_select(out=ident[:, :], in_=ident[:, :], compare_op=ALU.not_equal, fill=1.0, base=0,
                               pattern=[[-1, P]], channel_multiplier=1).then_inc(const_ready, 1)
            pool.iota(dist_i[:, :], pattern=[[1, S]], base=0, channel_multiplier=-1).then_inc(dist_ready, 1)
            for f in range(ROPE_HALF):
                pool.memset(freq[:, f:f + 1], float(INV_FREQ[f])).then_inc(freq_ready, 1)
            pool.memset(u_pad[:, :, 0:CONV_W - 1], 0.0).then_inc(pad_ready, 1)
            pool.memset(ones[:, :], 1.0).then_inc(const_ready, 1)
            load_gain(G_MEM)
            pool.dma_start(pos_i[:, :], a["positions"].rearrange("a (t p) -> p (a t)", p=P), allow_slow_non_contiguous=True).then_inc(pos_loaded, 16)
            pool.dma_start(ln_g[:, :], a["sgu_ln_g_2"].squeeze(0).partition_broadcast(P)).then_inc(sgu_loaded, 16)
            pool.dma_start(ln_b[:, :], a["sgu_ln_b_2"].squeeze(0).partition_broadcast(P)).then_inc(sgu_loaded, 16)
            pool.dma_start(b_sp[:, :, :], a["b_spatial_2"].squeeze(0).rearrange("g t -> (g t)").partition_broadcast(P)
                           .rearrange("p (g t) -> p g t", g=SGU_GROUPS)).then_inc(sgu_loaded, 16)
            pool.affine_select(out=later[:, :], in_=later[:, :], compare_op=ALU.is_gt, fill=0.0, base=0,
                               pattern=[[-1, P]], channel_multiplier=1).then_inc(const_ready, 1)
            pool.affine_select(out=earlier[:, :], in_=earlier[:, :], compare_op=ALU.is_gt, fill=0.0, base=0,
                               pattern=[[1, P]], channel_multiplier=-1).then_inc(const_ready, 1)

            def scale_sigmoid(j):
                pool.wait_ge(row_ready, 1)
                pool.wait_ge(sig_ready, j + 1)
                pool.tensor_tensor(sig1[:, :, :], sig1[:, :, :], r_row[:, 0, :].unsqueeze(1).broadcast_to([P, 2, S]), ALU.mult).then_inc(sig_scaled, 1)

            scale_sigmoid(0)
            pool.wait_ge(const_ready, 4)
            pool.wait_ge(cols_ready, 4)
            pool.memset(ws_t[CHUNK:P, :, 0:CHUNK], 0.0).then_inc(ws_masked, 1)
            pool.wait_ge(ws_masked, 1)
            scale_sigmoid(1)
            pool.wait_ge(u_ready, 2)
            own = 0
            for n, (c, k) in enumerate(POOL_TAPS):
                tap, win, acc = cols_b[:, 4 * k + c:4 * k + c + 1], u_pad[:, c, k:k + S], c_acc[:, c, :] if c > 1 else c_rest[:, :]
                if k == 0:
                    bias = cols_a[:, ROW_OF["conv_b"] + c:ROW_OF["conv_b"] + c + 1]
                    pool.tensor_scalar(acc, win, tap, bias, ALU.mult, ALU.add).then_inc(conv_last, 1)
                    continue
                if n in FIRST_TAPS:
                    pool.tensor_scalar(acc, win, tap, None, ALU.mult).then_inc(conv_last, 1)
                    continue
                if n in ACT_TAPS:
                    m = ACT_TAPS.index(n)
                    prod = c_prod[:, m % TAP_BATCH, :]
                    pool.wait_ge(conv_prod, m + 1)
                else:
                    own += 1
                    prod = c_tap[:, :]
                    pool.wait_ge(conv_last, n)
                    pool.tensor_scalar(prod, win, tap, None, ALU.mult).then_inc(conv_tap, 1)
                    pool.wait_ge(conv_tap, own)
                pool.wait_ge(conv_last, n)
                pool.tensor_tensor(acc, acc, prod, ALU.add).then_inc(conv_last, 1)
            load_gain(G_F)
            pool.wait_ge(k1_hi, 1)
            pool.tensor_tensor(k_split[0][1][:, :, :], kT[:, :, :], k_split[0][0][:, :, :].bitcast(F32), ALU.subtract).then_inc(k1_lo, 1)
            pool.wait_ge(v1_hi, 1)
            pool.tensor_tensor(v_split[0][1][:, :, :], vm[:, :, :], v_split[0][0][:, :, :].bitcast(F32), ALU.subtract).then_inc(v1_lo, 1)
            pool.wait_ge(xo_ready, XA_HEADS)
            pool.memset(y3_pad[:, :, 0:CONV3 - 1], 0.0).then_inc(pad3_ready, 1)
            load_gain(G_MEM2)
            pool.wait_ge(sb_z, 4)
            pool.dma_start(mem2_tok[:, :, :], a["mem_2"].rearrange("a (t p) d -> p (a t) d", p=P)).then_inc(mem2_loaded, 16)
            load_gain(G_FINAL)
            pool.wait_ge(gain_loaded, 16 * (G_FINAL + 1))
            pool.wait_ge(h_updated, 6 * UPD[I_FF2] + 4)
            pool.tensor_tensor(xn[:, 1, HALF:], h[:, 1, HALF:], gain[:, HALF:], ALU.mult).then_inc(last_half, 1)

        @block.tensor
        def _(pe):
            def mm3(o, left, right, first, last):
                (lh, ll), (rh, rl) = left, right
                pe.matmul(o, lh, rh, start=first, stop=False)
                pe.matmul(o, lh, rl, start=False, stop=False)
                return pe.matmul(o, ll, rh, start=False, stop=last)

            def slab(i, n):
                s = PLACE[i]
                return tuple(w[:, s, :].rearrange("p (k n) -> p k n", n=n) for w in (w_hi, w_lo))

            def form_a(i, banks, xt, n=256, step=0, ready=None):
                if i == 0:
                    pe.wait_ge(first_lo, 1)
                else:
                    pe.wait_ge(lo_done, i + 1 + step)
                wh, wl = slab(i, n)
                nk = SLAB // n
                for b in range(n // P):
                    for k in range(nk):
                        if ready and b == 0:
                            if i == 0 and k == nk // 2:
                                pe.wait_ge(lo_done, 1)
                            ready(k)
                        c = slice(b * P, (b + 1) * P)
                        mm = mm3(feat(banks[b // 2])[:, (b % 2) * S:(b % 2 + 1) * S], (wh[:, k, c], wl[:, k, c]),
                                 (xt[0][:, k, :], xt[1][:, k, :]), k == 0, k == nk - 1)
                mm.then_inc(slab_used, 1)

            def form_b_rows(i, k0, xt, tbs, first, last, step=0, n=D):
                pe.wait_ge(lo_done, i + 1 + step)
                wh, wl = slab(i, n)
                nk = SLAB // n
                for kk in range(nk):
                    for tb in tbs:
                        t = slice(tb * P, (tb + 1) * P)
                        for half in range(n // HALF):
                            c = slice(half * HALF, (half + 1) * HALF)
                            mm = mm3(tok(2 * tb + half) if n == D else None, (xt[0][:, k0 + kk, t], xt[1][:, k0 + kk, t]),
                                     (wh[:, kk, c], wl[:, kk, c]), first and kk == 0, last and kk == nk - 1)
                return mm

            def form_b(i0, xt, order, ready, between, midway=None):
                for j in range(2):
                    ready(order[j])
                    form_b_rows(i0 + j, 2 * order[j], xt, (0, 1), j == 0, False).then_inc(slab_used, 1)
                if midway:
                    midway()
                for j in (2, 3):
                    ready(order[j])
                    mm = form_b_rows(i0 + j, 2 * order[j], xt, (0,), False, j == 3)
                mm.then_inc(tb0_done, 1)
                for j in (2, 3):
                    form_b_rows(i0 + j, 2 * order[j], xt, (1,), False, j == 3).then_inc(slab_used, 1)
                    if j == 2:
                        between()

            def form_b_half(i0, bank, xt):
                for j in range(2):
                    pe.wait_ge(lo_done, i0 + j + 1)
                    wh, wl = slab(i0 + j, HALF)
                    for kk in range(4):
                        k = 4 * j + kk
                        for tb in range(TB):
                            t = slice(tb * P, (tb + 1) * P)
                            mm = mm3(tok(bank + tb), (xt[0][:, k, t], xt[1][:, k, t]), (wh[:, kk, :], wl[:, kk, :]),
                                     k == 0, k == KD - 1)
                    mm.then_inc(slab_used, 1)

            def norm_transpose(n, src, bank=tok):
                for tb in range(TB):
                    pe.wait_ge(norm_xn, 2 * n + tb + 1)
                    for f in range(KD):
                        mm = pe.transpose(bank(2 * tb + f // 4)[:, (f % 4) * P:(f % 4 + 1) * P],
                                          src[:, tb, f * P:(f + 1) * P], ident[:, :])
                    mm.then_inc(norm_t, 1)

            def normed(n):
                pe.wait_ge(norm_lo, 4 * (n + 1))

            def raw_transpose(n, tb, upd=None):
                first = {bank: k1 for bank, k0, k1 in raw_pieces(n, 0)}
                for m, (bank, k0, k1) in enumerate(raw_pieces(n, tb)):
                    if upd is not None:
                        pe.wait_ge(h_updated, 6 * upd + 2 * tb + m + 1)
                    if tb == 1 and bank in first:
                        pe.wait_ge(raw_lo, 16 * n + first[bank])
                    for k in range(k0, k1):
                        mm = pe.transpose(ps[:, bank, (k - k0) * P:(k - k0 + 1) * P], h[:, tb, k * P:(k + 1) * P], ident[:, :])
                    mm.then_inc(raw_t, 1)

            def raw_ready(n):
                return lambda k: pe.wait_ge(raw_lo, 16 * n + 9 + k)

            def spread(m, bank):
                pe.wait_ge(const_ready, 2)
                for tb in range(TB):
                    pe.wait_ge(diag_ready, 2 * m + tb + 1)
                    mm = pe.matmul(bank[:, tb * P:(tb + 1) * P], ones[:, :], diag[:, tb, :], start=True, stop=True)
                mm.then_inc(row_t, 1)

            k_done, v_done = ((k1_lo, 1), (k2_lo, 4)), ((v1_lo, 1), (v2_lo, 4))

            def x_attention(b, i_q, i_o, ready, between):
                def scores(hd):
                    pe.wait_ge(xq_ready, 4 * b + hd + 1)
                    pe.wait_ge(*k_done[b])
                    for tb in range(TB):
                        u = TB * hd + tb
                        if u >= 4:
                            pe.wait_ge(xexp_ready, 8 * b + u - 3)
                        for kk in range(2):
                            f = 2 * hd + kk
                            mm = mm3(tok(u % 4)[:, 0:NMEM], [q[:, f, tb * P:(tb + 1) * P] for q in (q_h, q_l)],
                                     [k[:, f, :] for k in k_split[b]], kk == 0, kk == 1)
                        mm.then_inc(xs_ready, 1)

                def turn(hd):
                    for tb in range(TB):
                        u = TB * hd + tb
                        pe.wait_ge(xp_ready, 8 * b + u + 1)
                        for m in range(2):
                            mm = pe.transpose(feat(hd)[:, m * S + tb * P:m * S + (tb + 1) * P],
                                              prob[:, u % 4, m * P:(m + 1) * P], ident[:, :])
                    mm.then_inc(xp_t, 1)

                def values(hd):
                    pe.wait_ge(xpT_ready, 4 * b + hd + 1)
                    pe.wait_ge(*v_done[b])
                    for kk in range(2):
                        f = 2 * hd + kk
                        for m in range(2):
                            mm = mm3(feat(hd)[:, kk * S:(kk + 1) * S], [v[:, m, f * P:(f + 1) * P] for v in v_split[b]],
                                     [p[:, hd % 2, m, :] for p in (probT_h, probT_l)], m == 0, m == 1)
                    mm.then_inc(xo_ready, 1)

                form_a(i_q, (0,), (xh, xl), ready=ready)
                form_a(i_q + 1, (1,), (xh, xl))
                pe.wait_ge(*((v_ready, 4), (v2_lo, 4))[b])
                scores(0)
                form_a(i_q + 2, (2,), (xh, xl))
                scores(1)
                turn(0)
                form_a(i_q + 3, (3,), (xh, xl))
                scores(2)
                values(0)
                turn(1)
                scores(3)
                values(1)
                turn(2)
                pe.wait_ge(xexp_ready, 8 * (b + 1))

                def head(s):
                    if s == 1:
                        turn(3)
                        values(2)
                    if s == 2:
                        values(3)
                    pe.wait_ge(xo_lo, 4 * b + s + 1)

                form_b(i_o, (xh, xl), range(4), head, between)

            x_t, m_t = (xh, xl), (mem_h, mem_l)
            pe.wait_ge(const_ready, 1)
            pe.wait_ge(gain_mix_loaded, 16)
            pe.transpose(feat(3)[:, 0:KD], rows_g[0:KD, :], ident[0:KD, 0:KD]).then_inc(gains_t, 1)
            for tb in range(TB):
                pe.wait_ge(x_loaded[tb], 16)
                if tb == 1:
                    pe.wait_ge(gains_ready, 1)
                raw_transpose(R_MIX, tb)
            form_a(0, (0,), x_t, ready=raw_ready(R_MIX))
            form_a(1, (1,), x_t)
            spread(0, tok(0))
            form_a(2, (2,), x_t)
            pe.wait_ge(row_ready, 1)
            norm_transpose(N_MEM, mem_tok)
            pe.wait_ge(gains_ready, 1)
            form_a(3, (3,), x_t)
            pe.wait_ge(rows_loaded, 16 * (len(ROW_OF) + 2 + len(GAIN_COLS) - 1))
            normed(N_MEM)
            pe.transpose(tok(2)[:, 0:ROWS_A], rows_a[:, :], ident[0:ROWS_A, 0:ROWS_A])
            pe.transpose(tok(2)[:, P:P + 4 * CONV_W], rows_b[:, :], ident[0:4 * CONV_W, 0:4 * CONV_W])
            n = KD * len(GAIN_COLS)
            pe.transpose(tok(2)[:, 2 * P:2 * P + n], rows_g[:, :], ident[0:n, 0:n])
            for g in range(SGU_GROUPS):
                mm = pe.transpose(tok(3)[:, g * P:(g + 1) * P], ws_rows[:, g, :], ident[:, :])
            mm.then_inc(rows_t, 1)
            form_b_half(I_QK, 0, x_t)
            pe.wait_ge(cols_ready, 4)
            form_b_half(I_RV, 2, x_t)
            pe.wait_ge(rope_ready, 2)
            for f in range(4):
                for tb in range(TB):
                    mm = pe.transpose(tok(f // 2)[:, (f % 2) * S + tb * P:(f % 2) * S + (tb + 1) * P],
                                      qkr[:, tb, f * P:(f + 1) * P], ident[:, :])
                if f % 2:
                    mm.then_inc(qk_t, 1)
            pe.wait_ge(u_ready, 1)
            form_a(I_RG, (0,), x_t)

            def ret_scores(hd):
                pe.wait_ge(qkT_ready, 2)
                if hd == 2:
                    pe.wait_ge(rv_ready, 2)
                if hd >= 4:
                    pe.wait_ge(s_dec_ready, hd - 3)
                r = slice(RET_DK * (hd % 4), RET_DK * (hd % 4 + 1))
                f = hd // 4
                pe.matmul(tok(hd % 4)[:, 0:S], qkT[r, 2 + f, 0:P], qkT[r, f, 0:S], start=True, stop=True)
                pe.matmul(tok(hd % 4)[:, S:S + P], qkT[r, 2 + f, P:S], qkT[r, f, P:S],
                          start=True, stop=True).then_inc(ret_s, 1)

            def ret_values(hd):
                pe.wait_ge(s_dec_ready, hd + 1)
                pe.wait_ge(rv_ready, 2)
                pe.wait_ge(u_ready, 2)
                c = slice(hd * RET_DV, (hd + 1) * RET_DV)
                sd = s_dec[:, hd % 2, :]
                pe.matmul(feat(2)[:, c], sd[:, 0:P], rv[:, 0, c], start=True, stop=True)
                pe.matmul(feat(3)[:, c], sd[:, P:S], rv[:, 0, c], start=True, stop=False)
                pe.matmul(feat(3)[:, c], sd[:, S:S + P], rv[:, 1, c], start=False, stop=True).then_inc(ret_pv, 1)

            ret_scores(0)
            ret_scores(1)
            form_a(I_RG + 1, (1,), x_t)
            for j in range(4):
                for hd in (2 * j, 2 * j + 1):
                    if hd + 2 < RET_HEADS:
                        ret_scores(hd + 2)
                    ret_values(hd)
                if j < 2:
                    pe.wait_ge(rg_in, j + 1)
                else:
                    pe.wait_ge(k_ready, j - 1)
                form_a(I_K1 + j, (j % 2,), m_t)

            def ret_transpose():
                pe.wait_ge(k_ready, 3)
                pe.wait_ge(ry_ready, 1)
                for f in range(4):
                    for tb in range(TB):
                        mm = pe.transpose(feat(2 * (f // 2))[:, (f % 2) * S + tb * P:(f % 2) * S + (tb + 1) * P],
                                          ry[:, tb, f * P:(f + 1) * P], ident[:, :])
                mm.then_inc(ry_t, 1)

            pe.wait_ge(s_dec_ready, RET_HEADS)
            for j in range(4):
                form_b_rows(I_V1 + j, 2 * j, m_t, (0, 1), j == 0, j == 3).then_inc(slab_used, 1)
                if j == 1:
                    ret_transpose()
            pe.wait_ge(const_ready, 4)
            pe.wait_ge(conv_last, len(POOL_TAPS))
            pe.wait_ge(conv_step, CONV_W + TAPS_DVE + 1)
            pe.wait_ge(k_ready, 4)
            for tb in range(TB):
                for c in range(4):
                    mm = pe.matmul(feat(3 - 2 * tb)[:, 0:P], ones[:, :], c_acc[:, c, tb * P:(tb + 1) * P], start=c == 0, stop=c == 3)
                mm.then_inc(conv_mean, 1)
            pe.wait_ge(v_ready, 4)
            pe.wait_ge(ret_lo, 1)
            form_b_rows(I_OUT1, 2 * OUT1_ORDER[0], x_t, (0,), True, False)
            for tb in range(TB):
                pe.wait_ge(conv_squared, tb + 1)
                for c in range(4):
                    mm = pe.matmul(feat(2 * tb)[:, 0:P], ones[:, :], c_sq[:, c, tb * P:(tb + 1) * P], start=c == 0, stop=c == 3)
                mm.then_inc(conv_var, 1)
            form_b_rows(I_OUT1, 2 * OUT1_ORDER[0], x_t, (1,), True, False).then_inc(slab_used, 1)
            form_b_rows(I_OUT1 + 1, 2 * OUT1_ORDER[1], x_t, (0, 1), False, False).then_inc(slab_used, 1)
            pe.wait_ge(conv_lo, 1)
            for j in (2, 3):
                mm = form_b_rows(I_OUT1 + j, 2 * OUT1_ORDER[j], x_t, (0,), False, j == 3)
            mm.then_inc(tb0_done, 1)
            pe.wait_ge(conv_lo, 2)
            for j in (2, 3):
                form_b_rows(I_OUT1 + j, 2 * OUT1_ORDER[j], x_t, (1,), False, j == 3).then_inc(slab_used, 1)
                if j == 2:
                    raw_transpose(R_XA, 0, UPD[I_OUT1])
            raw_transpose(R_XA, 1, UPD[I_OUT1])
            pe.wait_ge(k_ready, 4)
            x_attention(0, I_Q1, I_O1, raw_ready(R_XA), lambda: raw_transpose(R_MLP, 0, UPD[I_O1]))
            raw_transpose(R_MLP, 1, UPD[I_O1])

            def mlp1(g, first=False, last=False):
                step = 0 if first else 4 * g
                i = I_FF1
                for c in range(2):
                    if first:
                        pe.wait_ge(xo_lo, 4)
                    else:
                        pe.wait_ge(relu_ready, 2 * g - 1 + c)
                    form_a(i + c, (c,), x_t, step=step, ready=raw_ready(R_MLP) if first and c == 0 else None)
                u_t = (ff_h, ff_l)
                two = 0 if first else 2 * g
                if last:
                    for c in range(2):
                        pe.wait_ge(ff_lo, two + c + 1)
                        mm = form_b_rows(i + 2 + c, 2 * c, u_t, (0,), False, c == 1, step=step)
                    mm.then_inc(tb0_done, 1)
                    for c in range(2):
                        form_b_rows(i + 2 + c, 2 * c, u_t, (1,), False, c == 1, step=step).then_inc(slab_used, 1)
                        if c == 0:
                            raw_transpose(R_MIX2, 0, UPD[I_FF1])
                else:
                    for c in range(2):
                        pe.wait_ge(ff_lo, two + c + 1)
                        form_b_rows(i + 2 + c, 2 * c, u_t, (0, 1), first and c == 0, False, step=step).then_inc(slab_used, 1)

            mlp1(0, first=True)
            with pe.Fori(1, G1 - 1) as g:
                mlp1(g)
            mlp1(G1 - 1, last=True)
            raw_transpose(R_MIX2, 1, UPD[I_FF1])
            for j in range(4):
                form_a(I_SBQK + j, (j,), x_t, ready=raw_ready(R_MIX2) if j == 0 else None)
                if j == 2:
                    spread(1, tok(3))
            form_b_half(I_SBV, 0, x_t)

            def sb_scores(p):
                if p == 0:
                    pe.wait_ge(sbv_ready, 2)
                    pe.wait_ge(sbqk_ready, 4)
                else:
                    pe.wait_ge(sb_z_read, p)
                for e in range(2):
                    r = slice(SB_DIM * e, SB_DIM * (e + 1))
                    pe.matmul(tok(e)[:, 0:S], qkT2[r, 4 + p, 0:P], qkT2[r, p, 0:S], start=True, stop=True)
                    mm = pe.matmul(tok(e)[:, S:S + P], qkT2[r, 4 + p, P:S], qkT2[r, p, P:S], start=True, stop=True)
                mm.then_inc(sb_z, 1)

            def sb_sums(p):
                pe.wait_ge(sb_pen, p + 1)
                if p == 0:
                    pe.wait_ge(vg_ready, 2)
                else:
                    pe.wait_ge(sb_lo, p)
                for e in range(2):
                    pe.matmul(tok(2 + e)[:, 0:S], later[:, :], sb_m[:, e, 0:S], start=True, stop=False)
                    pe.matmul(tok(2 + e)[:, P:S], ones[:, :], sb_m[:, e, S:S + P], start=False, stop=True)
                    mm = pe.matmul(tok(2 + e)[:, S:S + P], later[:, :], sb_m[:, e, S:S + P], start=True, stop=True)
                mm.then_inc(sb_cum, 1)

            def sb_values(p):
                pe.wait_ge(sb_prob, p + 1)
                for e in range(2):
                    r = slice(SB_DIM * e, SB_DIM * (e + 1))
                    c = slice((2 * p + e) * SB_DIM, (2 * p + e + 1) * SB_DIM)
                    pe.matmul(tok(2)[r, 0:S], v2[:, 0, c], sb_a[:, e, 0:S], start=True, stop=False)
                    mm = pe.matmul(tok(2)[r, P:S], v2[:, 1, c], sb_a[:, e, S:S + P], start=False, stop=True)
                mm.then_inc(sb_out, 1)

            SB_AT = {}

            def at_slab(i, step, p):
                SB_AT.setdefault(i, []).append((step, p))

            for p in range(4):
                at_slab(SB_START + 4 * p, sb_scores, p)
                at_slab(SB_START + 4 * p + 3, sb_sums, p)
                at_slab(SB_START + 4 * p + 6, sb_values, p)

            def beside(i):
                for step, p in SB_AT.get(i, ()):
                    step(p)

            pe.wait_ge(sbqk_ready, 2)
            form_a(I_ZU, (0,), x_t)
            form_a(I_ZU + 1, (1,), x_t)
            pe.wait_ge(row_ready, 2)
            form_b_half(I_ZV, 2, x_t)
            beside(I_ZV + 1)
            pe.wait_ge(sbqk_ready, 4)
            form_a(I_C3, (2,), x_t)
            beside(I_C3)
            form_a(I_C3 + 1, (3,), x_t)
            beside(I_C3 + 1)
            pe.wait_ge(ug_in, 2)
            form_a(I_C3 + 2, (0,), x_t)
            beside(I_C3 + 2)
            form_a(I_C3 + 3, (1,), x_t)
            beside(I_C3 + 3)
            pe.wait_ge(y3_ready, 1)
            form_a(I_C3 + 4, (2,), x_t)
            beside(I_C3 + 4)
            pe.wait_ge(vn_ready, 2)
            pe.wait_ge(ws_masked, 1)
            pe.wait_ge(y3_ready, 2)
            for g in range(SGU_GROUPS):
                for tb in range(TB):
                    o = feat(g // 2)[:, (g % 2) * S + tb * P:(g % 2) * S + (tb + 1) * P]
                    mm = pe.matmul(o, vg[:, tb, g * P:(g + 1) * P], ws_t[:, g, :], start=True, stop=True)
            mm.then_inc(sgu_mixed, 1)
            form_a(I_C3 + 5, (3,), x_t)
            beside(I_C3 + 5)
            for n, br in enumerate(BRANCH_ORDER):
                for half in range(2):
                    i = I_BR + 6 * n + 3 * half
                    r = 2 * n + half
                    if r == 0:
                        pe.wait_ge(yb_ready, 2)
                    for j in range(2):
                        if r > 0:
                            pe.wait_ge(gate_in, 2 * r - 1 + j)
                        form_a(i + j, (j,), x_t)
                        beside(i + j)
                    if r == 0:
                        pe.wait_ge(yc_ready, 2)
                    else:
                        pe.wait_ge(merge_done, r)
                    pe.wait_ge((sb_lo, yb_lo, yc_lo)[br], (4, 1, 1)[br])
                    form_a(i + 2, (2, 3), (y_h[br], y_l[br]), n=HALF)
                    beside(i + 2)

            def second_memory():
                pe.wait_ge(merge_done, 6)
                norm_transpose(N_MEM2, mem2_tok, feat)

            pe.wait_ge(sb_lo, 4)
            form_b(I_OUT2, x_t, range(4), lambda s: pe.wait_ge(merged_lo, 1 + s // 2),
                   lambda: raw_transpose(R_XA2, 0, UPD[I_OUT2]), second_memory)
            m2_t = (mem2_h, mem2_l)
            normed(N_MEM2)
            form_a(I_K2, (0,), m2_t)
            raw_transpose(R_XA2, 1, UPD[I_OUT2])
            form_a(I_K2 + 1, (1,), m2_t)
            form_a(I_K2 + 2, (2,), m2_t)
            form_a(I_K2 + 3, (3,), m2_t)
            raw_ready(R_XA2)(KD - 1)
            for j in range(4):
                form_b_rows(I_V2 + j, 2 * j, m2_t, (0, 1), j == 0, j == 3).then_inc(slab_used, 1)
            pe.wait_ge(k2_lo, 4)
            x_attention(1, I_Q2, I_O2, None, lambda: raw_transpose(R_FF2, 0, UPD[I_O2]))
            raw_transpose(R_FF2, 1, UPD[I_O2])

            def glu_in(i, banks=(0, 1), gate_done=None, up_done=None, step=0, ready=None):
                if gate_done is not None:
                    pe.wait_ge(glu_in_ready, gate_done)
                form_a(i, banks[:1], x_t, step=step, ready=ready)
                if up_done is not None:
                    pe.wait_ge(glu_ready, up_done)
                form_a(i + 1, banks[1:], x_t, step=step)

            def glu_out(i, done, first=False, step=0):
                pe.wait_ge(glu_lo, done)
                form_b_rows(i, 0, (ff_h, ff_l), (0, 1), first, False, step=step).then_inc(slab_used, 1)

            pe.wait_ge(xo_lo, 8)
            glu_in(I_FF2, (2, 3), ready=raw_ready(R_FF2))
            spread(2, tok(0))
            glu_in(ff2_gate(1))
            pe.wait_ge(row_ready, 3)
            glu_out(ff2_gate(1) + 2, 1, first=True)
            glu_in(ff2_gate(2), gate_done=2, up_done=2)
            glu_out(ff2_gate(2) + 2, 2)
            with pe.Fori(0, G2 - 4) as t:
                glu_in(ff2_gate(3), gate_done=t + 3, up_done=t + 3, step=3 * t)
                glu_out(ff2_gate(3) + 2, t + 3, step=3 * t)
            glu_in(ff2_gate(G2 - 1), gate_done=G2 - 1, up_done=G2 - 1)
            for tb in range(TB):
                pe.wait_ge(glu_lo, G2 - 1)
                mm = form_b_rows(N_SLABS - 2, 0, (ff_h, ff_l), (tb,), False, False)
                if tb == 1:
                    mm.then_inc(slab_used, 1)
                pe.wait_ge(glu_lo, G2)
                form_b_rows(N_SLABS - 1, 2, (ff_h, ff_l), (tb,), False, True).then_inc(tb0_done if tb == 0 else slab_used, 1)

        @block.scalar
        def _(act):
            count = [0]

            def after(ins):
                count[0] += 1
                ins.then_inc(act_step, 1)
                act.wait_ge(act_step, count[0])

            def hi(i, step=0, turn=0):
                s = PLACE[i]
                act.wait_ge(w_loaded[s], 16 * (USES[i] + 1) + 16 * turn)
                if BEFORE[i] is not None:
                    act.wait_ge(slab_used, BEFORE[i] + 1 + step)
                act.activation(w_hi[:, s, :], w_ring[:, s, :], ACT.Copy).then_inc(hi_done, 1)

            def norm_square(src, tb, use, junk=None):
                if use + tb > 0:
                    act.wait_ge(norm_sq, 2 * use + tb)
                act.activation(xn[:, tb, :] if junk is None else junk, src[:, tb, :], ACT.Square,
                               accum_out=sq_sum[:, 2 * use + tb:2 * use + tb + 1]).then_inc(norm_sq, 1)

            def norm_split_hi(n, tb, dst, bank=tok):
                act.wait_ge(norm_t, 2 * n + tb + 1)
                for half in range(2):
                    act.activation(dst[:, 4 * half:4 * half + 4, tb * P:(tb + 1) * P],
                                   bank(2 * tb + half).rearrange("p (f t) -> p f t", t=P), ACT.Copy).then_inc(norm_hi, 1)

            def raw_split_hi(n, tb, which=range(4)):
                for m, (bank, k0, k1) in enumerate(raw_pieces(n, tb)):
                    if m not in which:
                        continue
                    act.wait_ge(raw_t, pieces_before(n, tb) + m + 1)
                    for k in range(k0, k1):
                        act.activation(xh[:, k, tb * P:(tb + 1) * P], ps[:, bank, (k - k0) * P:(k - k0 + 1) * P], ACT.Copy,
                                       scale=cols_g[:, KD * n + k:KD * n + k + 1]).then_inc(raw_hi, 1)

            def row_copy(m, bank):
                act.wait_ge(row_t, m + 1)
                act.activation(r_row[:, 0, :], bank[:, 0:S], ACT.Copy).then_inc(row_ready, 1)

            def used_slab(i):
                act.wait_ge(slab_used, i + 1)

            def boundary(n, use, nxt):
                hi(nxt)
                hi(nxt + 1)
                raw_split_hi(n, 0)
                raw_split_hi(n, 1)
                hi(nxt + 2)
                for tb in range(TB):
                    norm_square(h, tb, use)
                hi(nxt + 3)

            act.wait_ge(gains_t, 1)
            act.activation(cols_g[:, 0:KD], feat(3)[:, 0:KD], ACT.Copy).then_inc(gains_ready, 1)
            act.wait_ge(gains_ready, 1)
            first, second = slice(0, SLAB // 2), slice(SLAB // 2, SLAB)
            act.wait_ge(first_loaded, 16)
            act.activation(w_hi[:, 0, first], w_ring[:, 0, first], ACT.Copy).then_inc(first_hi, 1)
            raw_split_hi(R_MIX, 0)
            raw_split_hi(R_MIX, 1, (0, 1))
            act.wait_ge(w_loaded[0], 16)
            act.activation(w_hi[:, 0, second], w_ring[:, 0, second], ACT.Copy).then_inc(hi_done, 1)
            raw_split_hi(R_MIX, 1, (2, 3))
            hi(1)
            norm_square(h, 0, Q_MIX)
            norm_square(h, 1, Q_MIX)
            hi(2)
            act.wait_ge(mem_loaded, 16)
            norm_square(mem_tok, 0, Q_MEM)
            norm_square(mem_tok, 1, Q_MEM)
            row_copy(0, tok(0))
            hi(3)
            hi(4)
            act.wait_ge(sig_in, 1)
            act.activation(sig1[:, :, :], sig1[:, :, :], ACT.Sigmoid).then_inc(sig_ready, 1)
            norm_split_hi(N_MEM, 0, mem_h)
            norm_split_hi(N_MEM, 1, mem_h)
            hi(5)
            hi(6)
            act.wait_ge(ang_ready, 1)
            act.activation(sincos[:, :, :, :].rearrange("p a t f -> p (a t f)"),
                           ang[:, :, :, :].rearrange("p a t f -> p (a t f)"), ACT.Sin).then_inc(sincos_ready, 1)
            act.wait_ge(rows_t, 1)
            act.activation(cols_a[:, :], tok(2)[:, 0:ROWS_A], ACT.Copy).then_inc(cols_ready, 1)
            act.activation(cols_b[:, :], tok(2)[:, P:P + 4 * CONV_W], ACT.Copy).then_inc(cols_ready, 1)
            act.activation(cols_g[:, KD:], tok(2)[:, 2 * P + KD:2 * P + KD * len(GAIN_COLS)], ACT.Copy).then_inc(cols_ready, 1)
            act.activation(ws_t[:, :, :].rearrange("p g t -> p (g t)"), tok(3), ACT.Copy).then_inc(cols_ready, 1)
            act.wait_ge(sig_in, 2)
            act.activation(sig1[:, :, :], sig1[:, :, :], ACT.Sigmoid).then_inc(sig_ready, 1)

            def tap_products(batch):
                for m, n in list(enumerate(ACT_TAPS))[TAP_BATCH * batch:TAP_BATCH * (batch + 1)]:
                    c, k = POOL_TAPS[n]
                    act.wait_ge(u_ready, 2)
                    if m >= TAP_BATCH:
                        act.wait_ge(conv_last, ACT_TAPS[m - TAP_BATCH] + 1)
                    act.activation(c_prod[:, m % TAP_BATCH, :], u_pad[:, c, k:k + S], ACT.Copy,
                                   scale=cols_b[:, 4 * k + c:4 * k + c + 1]).then_inc(conv_prod, 1)

            hi(7)
            tap_products(0)
            used_slab(I_QK + 1)
            for tb in range(TB):
                act.activation(qk[:, tb, :], tok(tb), ACT.Copy, scale=r_mix[:, tb:tb + 1]).then_inc(qk_ready, 1)
            hi(8)
            hi(9)
            tap_products(1)
            used_slab(I_RV + 1)
            for tb in range(TB):
                act.activation(rv[:, tb, :], tok(2 + tb), ACT.Copy, scale=r_mix[:, tb:tb + 1]).then_inc(rv_ready, 1)
            hi(10)
            hi(11)
            for b in range(2):
                act.wait_ge(qk_t, b + 1)
                act.activation(qkT[:, 2 * b:2 * b + 2, :], blocks(tok(b)), ACT.Copy).then_inc(qkT_ready, 1)
            tap_products(2)

            act.wait_ge(dist_set, 1)
            act.wait_ge(cols_ready, 4)
            for hd in range(RET_HEADS):
                act.activation(dec[:, hd, :], dist[:, :], ACT.Exp, scale=float(LOG_G[hd])).then_inc(dec_ready, 1)
            tap_products(3)
            act.wait_ge(rg_in, 1)
            act.activation(rgs[:, 0:2, :], rgs[:, 0:2, :], ACT.Silu).then_inc(rg_ready, 1)
            hi(12)
            act.wait_ge(rg_in, 2)
            act.activation(rgs[:, 2:4, :], rgs[:, 2:4, :], ACT.Silu).then_inc(rg_ready, 1)
            hi(13)
            tap_products(4)

            def keys(i, j, bank):
                used_slab(i + j)
                if i == I_K1:
                    act.wait_ge(s_dec_ready, 2 * j + 2)
                k = kT if i == I_K1 else k_split[1][0]
                act.activation(k[:, 2 * j:2 * j + 2, :], blocks(feat(bank)), ACT.Copy).then_inc(k_ready, 1)

            def values(i):
                used_slab(i + 3)
                for m in range(2):
                    for half in range(2):
                        v = vm if i == I_V1 else v_split[1][0]
                        act.activation(v[:, m, half * HALF:(half + 1) * HALF], tok(2 * m + half), ACT.Copy).then_inc(v_ready, 1)

            keys(I_K1, 0, 0)
            hi(14)
            tap_products(5)
            keys(I_K1, 1, 1)
            hi(15)
            tap_products(6)
            keys(I_K1, 2, 0)
            hi(16)
            tap_products(7)
            act.wait_ge(ry_centred, 1)
            act.activation(ry_sq[:, :, :], ry[:, :, :], ACT.Square).then_inc(ry_squared, 1)
            keys(I_K1, 3, 1)
            hi(17)
            tap_products(8)
            hi(18)
            hi(19)
            tap_products(9)
            tap_products(10)
            act.wait_ge(ret_ready, 1)
            used_slab(I_RG + 1)
            act.activation(xh[:, 4:8, :], retT[:, :, :], ACT.Copy).then_inc(ret_hi, 1)
            hi(20)
            act.wait_ge(ret_lo, 1)
            values(I_V1)

            def conv_square(tb):
                t = slice(tb * P, (tb + 1) * P)
                act.wait_ge(conv_centred, tb + 1)
                act.activation(c_sq[:, :, t], c_acc[:, :, t], ACT.Square).then_inc(conv_squared, 1)

            hi(21)
            conv_square(0)
            conv_square(1)
            act.wait_ge(k_ready, 4)
            act.activation(k_split[0][0][:, :, :], kT[:, :, :], ACT.Copy).then_inc(k1_hi, 1)
            for tb in range(TB):
                t = slice(tb * P, (tb + 1) * P)
                act.wait_ge(conv_normed, tb + 1)
                for c in range(4):
                    ins = act.activation(c_out[:, c, t], c_acc[:, c, t], ACT.Silu, bias=cols_a[:, ROW_OF["conv_ln_b"] + c:ROW_OF["conv_ln_b"] + c + 1],
                                         scale=cols_a[:, ROW_OF["conv_ln_w"] + c:ROW_OF["conv_ln_w"] + c + 1])
                    ins.then_inc(conv_out, 1)
                act.wait_ge(conv_out, 4 * tb + 4)
                act.activation(xh[:, 0:4, t], c_out[:, :, t], ACT.Copy).then_inc(conv_hi, 1)
            boundary(R_XA, Q_XA, I_Q1)
            act.wait_ge(k1_lo, 1)
            act.wait_ge(v_ready, 4)
            act.activation(v_split[0][0][:, :, :], vm[:, :, :], ACT.Copy).then_inc(v1_hi, 1)

            def x_attention(b, i_q, i_o):
                def q(j):
                    used_slab(i_q + j)
                    act.activation(q_h[:, 2 * j:2 * j + 2, :], blocks(feat(j)), ACT.Copy).then_inc(xq_hi, 1)
                    if j < 3:
                        hi(i_o + j)

                def exps(hd):
                    for u in range(TB * hd, TB * hd + TB):
                        act.wait_ge(xmax_ready, 8 * b + u + 1)
                        act.activation(prob[:, u % 4, :], tok(u % 4)[:, 0:NMEM], ACT.Exp, bias=xneg[:, u:u + 1], scale=r_xa[:, u % TB:u % TB + 1],
                                       accum_out=xsum[:, u:u + 1]).then_inc(xexp_ready, 1)

                def p_t(hd):
                    act.wait_ge(xp_t, 4 * b + hd + 1)
                    if hd >= 2:
                        act.wait_ge(xo_ready, 4 * b + hd - 1)
                    act.activation(probT_h[:, hd % 2, :, :], blocks(feat(hd)), ACT.Copy).then_inc(xp_hi, 1)

                def out_hi(hd):
                    act.wait_ge(xo_ready, 4 * b + hd + 1)
                    act.activation(xh[:, 2 * hd:2 * hd + 2, :], blocks(feat(hd)), ACT.Copy).then_inc(xo_hi, 1)

                q(0)
                q(1)
                exps(0)
                q(2)
                p_t(0)
                exps(1)
                q(3)
                p_t(1)
                exps(2)
                exps(3)
                out_hi(0)
                out_hi(1)
                p_t(2)
                hi(i_o + 3)
                p_t(3)
                out_hi(2)
                out_hi(3)

            x_attention(0, I_Q1, I_O1)
            boundary(R_MLP, Q_MLP, I_FF1)

            def mlp1(g, first=False, splits=True):
                step = 0 if first else 4 * g
                two = 0 if first else 2 * g
                for c in range(2):
                    act.wait_ge(slab_used, I_FF1 + c + 1 + step)
                    if not first:
                        act.wait_ge(ff_lo, two - 1 + c)
                    act.activation(ff_r[:, c, :], feat(c), ACT.Relu).then_inc(relu_ready, 1)
                    act.wait_ge(relu_ready, two + c + 1)
                    act.activation(ff_h[:, 2 * c:2 * c + 2, :], blocks(ff_r[:, c, :]), ACT.Square).then_inc(ff_hi, 1)
                    if splits:
                        hi(I_FF1 + 4 + c, step, 0 if first else g)
                if splits:
                    for c in range(2, 4):
                        hi(I_FF1 + 4 + c, step, 0 if first else g)

            mlp1(0, first=True)
            with act.Fori(1, G1 - 1) as g:
                mlp1(g)
            mlp1(G1 - 1, splits=False)
            hi(I_SBQK)
            hi(I_SBQK + 1)
            act.wait_ge(gain_product, 1)
            raw_split_hi(R_MIX2, 0)
            raw_split_hi(R_MIX2, 1)
            for tb in range(TB):
                norm_square(h, tb, Q_F, hg_sq[:, tb, :])
            hi(I_SBQK + 2)
            for tb in range(TB):
                act.wait_ge(hg_ready, tb + 1)
                norm_square(xn, tb, Q_MIX2, hg_sq[:, tb, :])
            hi(I_SBQK + 3)

            def sb_logs(p):
                act.wait_ge(sb_z, p + 1)
                z = ps[:, 0:2, 0:SB_COLS]
                if p > 0:
                    act.wait_ge(sb_z_read, p)
                    act.wait_ge(sb_exp, p)
                after(act.activation(sb_e[:, :, :], z, ACT.Abs))
                after(act.activation(sb_e[:, :, :], sb_e[:, :, :], ACT.Exp, scale=-1.0))
                act.activation(sb_l[:, :, :], sb_e[:, :, :], ACT.Ln, bias=1.0).then_inc(sb_log, 1)

            def sb_exps(p):
                act.wait_ge(sb_arg, p + 1)
                if p > 0:
                    act.wait_ge(sb_out, p)
                act.activation(sb_a[:, :, :], sb_e[:, :, :], ACT.Exp).then_inc(sb_exp, 1)

            def sb_split(p):
                act.wait_ge(sb_out, p + 1)
                act.activation(y_h[0][:, p, :], tok(2)[:, 0:S], ACT.Copy).then_inc(sb_hi, 1)

            SB_AT, SB_EARLY = {}, {}

            def at_slab(i, step, p, table):
                table.setdefault(i, []).append((step, p))

            for p in range(4):
                if p != 2:
                    at_slab(SB_START + 4 * p, sb_logs, p, SB_AT)
                if p != 1:
                    at_slab(SB_START + 4 * p + 4, sb_exps, p, SB_EARLY)
                at_slab(SB_START + 4 * p + (5 if p == 1 else 6), sb_split, p, SB_EARLY)

            def early(i):
                for step, p in SB_EARLY.get(i, ()):
                    step(p)

            def beside(i):
                for step, p in SB_AT.get(i, ()):
                    step(p)

            for j in range(4):
                hi(I_SBQK + 4 + j)
                if j == 2:
                    row_copy(1, tok(3))
            used_slab(I_SBV + 1)
            for tb in range(TB):
                act.activation(v2[:, tb, :], tok(tb), ACT.Copy, scale=r_mix2[:, tb:tb + 1]).then_inc(sbv_ready, 1)
            hi(I_SBV + 4)
            hi(I_SBV + 5)
            for j in range(2):
                act.wait_ge(ug_in, j + 1)
                act.activation(ug[:, 2 * j:2 * j + 2, :], ug[:, 2 * j:2 * j + 2, :], ACT.Gelu).then_inc(ug_ready, 1)
                hi(I_ZU + 4 + j)
            used_slab(I_ZV + 1)
            for tb in range(TB):
                act.activation(vg[:, tb, :], tok(2 + tb), ACT.Gelu, scale=r_mix2[:, tb:tb + 1]).then_inc(vg_ready, 1)
            hi(I_ZV + 4)
            hi(I_ZV + 5)
            beside(I_ZV + 1)
            for j in range(2):
                early(I_C3 + 2 * j)
                hi(I_C3 + 2 * j + 4)
                beside(I_C3 + 2 * j)
                early(I_C3 + 2 * j + 1)
                hi(I_C3 + 2 * j + 5)
                beside(I_C3 + 2 * j + 1)
            for j in range(2):
                early(I_C3 + 4 + j)
                hi(I_C3 + 8 + j)
                beside(I_C3 + 4 + j)
            act.wait_ge(yb_ready, 2)
            act.activation(y_h[1][:, :, :], ug[:, :, :], ACT.Copy).then_inc(yb_hi, 1)
            act.wait_ge(yc_ready, 2)
            act.activation(y_h[2][:, :, :], acc3[:, :, :], ACT.Copy).then_inc(yc_hi, 1)

            def merged_split(half):
                act.wait_ge(merge_done, 5 + half)
                act.activation(xh[:, 4 * half:4 * half + 4, :], merged[:, 4 * half:4 * half + 4, :], ACT.Copy).then_inc(merged_hi, 1)

            for n in range(BRANCHES):
                for half in range(2):
                    i = I_BR + 6 * n + 3 * half
                    r = 2 * n + half
                    if r == 0:
                        sb_exps(1)
                        hi(i + 4)
                        hi(i + 5)
                        sb_logs(2)
                    for j in range(2):
                        act.wait_ge(gate_in, 2 * r + j + 1)
                        act.activation(sig2[:, 2 * j:2 * j + 2, :], sig2[:, 2 * j:2 * j + 2, :], ACT.Sigmoid).then_inc(gate_ready, 1)
                        if 0 < r < 5:
                            early(i + j)
                            hi(i + j + 4)
                            beside(i + j)
                    if r == 5:
                        merged_split(0)
                        hi(i + 4)
                        hi(i + 5)
                    early(i + 2)
                    if r < 5:
                        hi(i + 6)
                    beside(i + 2)
                    if r == 3:
                        act.wait_ge(mem2_loaded, 16)
                        act.wait_ge(sb_out, 4)
                        for tb in range(TB):
                            norm_square(mem2_tok, tb, Q_MEM2, mem2_sq[:, tb, :])
            merged_split(1)
            hi(I_OUT2 + 3)
            act.wait_ge(norm_sq, 2 * Q_MEM2 + 2)
            norm_split_hi(N_MEM2, 0, mem2_h, feat)
            norm_split_hi(N_MEM2, 1, mem2_h, feat)
            hi(I_K2)
            hi(I_K2 + 1)
            raw_split_hi(R_XA2, 0)
            hi(I_K2 + 2)
            hi(I_K2 + 3)
            keys(I_K2, 0, 0)
            raw_split_hi(R_XA2, 1)
            hi(I_K2 + 4)
            for tb in range(TB):
                norm_square(h, tb, Q_XA2)
            keys(I_K2, 1, 1)
            hi(I_K2 + 5)
            keys(I_K2, 2, 2)
            hi(I_K2 + 6)
            keys(I_K2, 3, 3)
            hi(I_K2 + 7)
            for j in range(4):
                hi(I_V2 + 4 + j)
                if j == 3:
                    values(I_V2)
            x_attention(1, I_Q2, I_O2)
            boundary(R_FF2, Q_FF2, I_FF2)
            row_copy(2, tok(0))

            def glu(g, i, first=False, last=False, step=0, turn=0):
                nxt = ff2_gate(1) if first else i + 3
                if last:
                    hi(N_SLABS - 1)
                elif not first:
                    hi(nxt, step, turn)
                act.wait_ge(glu_in_ready, g + 1)
                if not first:
                    act.wait_ge(glu_ready, g)
                act.activation(ff_r[:, 0, :], ff_u[:, 1, :], ACT.Silu).then_inc(silu_ready, 1)
                if not first and not last:
                    hi(nxt + 1, step, turn)
                    act.wait_ge(slab_used, i + 3 + step)
                act.wait_ge(glu_ready, g + 1)
                act.activation(ff_h[:, 2:4, :] if last else ff_h[:, 0:2, :], blocks(ff_u[:, 0, :]), ACT.Copy).then_inc(glu_hi, 1)
                if not last:
                    hi(nxt + 2, step, turn)

            glu(0, I_FF2, first=True)
            glu(1, ff2_gate(1))
            glu(2, ff2_gate(2))
            with act.Fori(0, G2 - 4) as t:
                glu(t + 3, ff2_gate(3), step=3 * t, turn=t)
            glu(G2 - 1, ff2_gate(G2 - 1), last=True)
            for tb in range(TB):
                for half in range(2):
                    act.wait_ge(h_updated, 6 * UPD[I_FF2] + 2 * tb + half + 1)
                    c = slice(half * HALF, (half + 1) * HALF)
                    act.activation(hg_sq[:, tb, c], h[:, tb, c], ACT.Square, accum_out=sq_last[:, 2 * tb + half:2 * tb + half + 1]).then_inc(last_sq, 1)
                act.wait_ge(y_ready, tb + 1)
                if tb == 1:
                    act.wait_ge(last_half, 1)
                act.activation(xn[:, tb, HALF:], xn[:, tb, HALF:], ACT.Copy, scale=ny[:, tb:tb + 1]).then_inc(out_tail, 1)

        @block.vector
        def _(dve):
            count = [0]

            def after(ins):
                count[0] += 1
                ins.then_inc(dve_step, 1)
                dve.wait_ge(dve_step, count[0])

            def lo(i, step=0):
                s = PLACE[i]
                dve.wait_ge(hi_done, i + 1 + step)
                dve.tensor_tensor(w_lo[:, s, :], w_ring[:, s, :], w_hi[:, s, :].bitcast(F32), ALU.subtract).then_inc(lo_done, 1)

            def rsqrt(v, y, t):
                after(dve.tensor_scalar(y.bitcast(I32), v.bitcast(I32), -0.5, RSQRT_MAGIC, ALU.mult, ALU.add))
                for _ in range(3):
                    after(dve.tensor_tensor(t, y, y, ALU.mult))
                    after(dve.scalar_tensor_tensor(t, t, -0.5, v, ALU.mult, ALU.mult))
                    after(dve.scalar_tensor_tensor(y, t, 1.5, y, ALU.add, ALU.mult))

            def norm_split_lo(n, tb, hi_t, lo_t, bank=tok):
                for half in range(2):
                    dve.wait_ge(norm_hi, 4 * n + 2 * tb + half + 1)
                    f, t = slice(4 * half, 4 * half + 4), slice(tb * P, (tb + 1) * P)
                    dve.tensor_tensor(lo_t[:, f, t], bank(2 * tb + half).rearrange("p (f t) -> p f t", t=P),
                                      hi_t[:, f, t].bitcast(F32), ALU.subtract).then_inc(norm_lo, 1)

            def raw_split_lo(n, tb, which=range(4)):
                t = slice(tb * P, (tb + 1) * P)
                for m, (bank, k0, k1) in enumerate(raw_pieces(n, tb)):
                    if m not in which:
                        continue
                    dve.wait_ge(raw_hi, 16 * n + 8 * tb + k1)
                    for k in range(k0, k1):
                        dve.scalar_tensor_tensor(xl[:, k, t], ps[:, bank, (k - k0) * P:(k - k0 + 1) * P], cols_g[:, KD * n + k:KD * n + k + 1],
                                                 xh[:, k, t].bitcast(F32), ALU.mult, ALU.subtract).then_inc(raw_lo, 1)

            def token_scales(use, r):
                dve.wait_ge(norm_sq, 2 * use + 2)
                after(dve.tensor_scalar(nv, sq_sum[:, 2 * use:2 * use + 2], 1.0 / D, EPS, ALU.mult, ALU.add))
                rsqrt(nv, r, nt)

            def memory_rows(n, src, g, r):
                dve.wait_ge(gain_loaded, 16 * (g + 1))
                for tb in range(TB):
                    dve.scalar_tensor_tensor(src[:, tb, :], src[:, tb, :], r[:, tb:tb + 1], gain[:, :], ALU.mult, ALU.mult).then_inc(norm_xn, 1)
                dve.wait_ge(norm_xn, 2 * n + 2)
                dve.sem_inc(gain_used, 1)

            def scales_on_diagonal(r):
                for tb in range(TB):
                    dve.tensor_scalar(diag[:, tb, :], ident[:, :], r[:, tb:tb + 1], None, ALU.mult).then_inc(diag_ready, 1)

            def row_of_scales(n):
                return r_row[:, n, :].unsqueeze(1).broadcast_to([P, 2, S])

            def update(upd, last_slab, scale=None):
                def add(tb, part, parts):
                    if tb == 0:
                        dve.wait_ge(tb0_done, upd + 1)
                    else:
                        dve.wait_ge(slab_used, last_slab + 1)
                    n = D // parts
                    c = slice(part * n, (part + 1) * n)
                    new = tok(2 * tb + part * n // HALF)[:, part * n % HALF:part * n % HALF + n]
                    if scale is None:
                        ins = dve.tensor_tensor(h[:, tb, c], new, h[:, tb, c], ALU.add)
                    else:
                        ins = dve.scalar_tensor_tensor(h[:, tb, c], new, scale[:, tb:tb + 1], h[:, tb, c], ALU.mult, ALU.add)
                    ins.then_inc(h_updated, 1)

                def block(tb):
                    parts = 2 + 2 * tb
                    for part in range(parts):
                        add(tb, part, parts)
                return add, block

            def boundary(n, upd, last_slab, use, r, nxt):
                _, update_block = update(upd, last_slab)
                lo(nxt)
                if n != R_XA:
                    lo(nxt + 1)
                for tb in range(TB):
                    update_block(tb)
                    raw_split_lo(n, tb)
                if n == R_XA:
                    lo(nxt + 1)
                lo(nxt + 2)
                token_scales(use, r)
                if n != R_XA:
                    lo(nxt + 3)

            dve.wait_ge(gains_ready, 1)
            first, second = slice(0, SLAB // 2), slice(SLAB // 2, SLAB)
            dve.wait_ge(first_hi, 1)
            dve.tensor_tensor(w_lo[:, 0, first], w_ring[:, 0, first], w_hi[:, 0, first].bitcast(F32), ALU.subtract).then_inc(first_lo, 1)
            raw_split_lo(R_MIX, 0)
            raw_split_lo(R_MIX, 1, (0, 1))
            dve.wait_ge(hi_done, 1)
            dve.tensor_tensor(w_lo[:, 0, second], w_ring[:, 0, second], w_hi[:, 0, second].bitcast(F32), ALU.subtract).then_inc(lo_done, 1)
            raw_split_lo(R_MIX, 1, (2, 3))
            lo(1)
            token_scales(Q_MIX, r_mix)
            dve.wait_ge(const_ready, 1)
            scales_on_diagonal(r_mix)
            lo(2)
            token_scales(Q_MEM, r_mem)
            memory_rows(N_MEM, mem_tok, G_MEM, r_mem)

            def scaled_gate(j):
                dve.wait_ge(slab_used, 2 * j + 2)
                dve.wait_ge(row_ready, 1)
                dve.tensor_tensor(sig1[:, :, :], blocks(feat(2 * j + 1)), row_of_scales(0), ALU.mult).then_inc(sig_in, 1)

            def gate_conv(j):
                dve.wait_ge(sig_scaled, j + 1)
                dve.wait_ge(pad_ready, 1)
                after(dve.tensor_tensor(u_pad[:, 2 * j:2 * j + 2, CONV_W - 1:], blocks(feat(2 * j)), sig1[:, :, :], ALU.mult))
                dve.sem_inc(u_ready, 1)

            done = [0]
            order = [(k, c) for k in range(CONV_W) for c in range(2) if c == 0 or k < TAPS_DVE]
            order = [(k, c, order.index((k - 1, c)) if k else None) for k, c in order]

            def conv(n):
                for m in range(done[0], min(done[0] + n, len(order))):
                    k, c, prev = order[m]
                    if m == 0:
                        dve.wait_ge(u_ready, 2)
                        dve.wait_ge(cols_ready, 2)
                    tap, win = cols_b[:, 4 * k + c:4 * k + c + 1], u_pad[:, c, k:k + S]
                    if k == 0:
                        bias = cols_a[:, ROW_OF["conv_b"] + c:ROW_OF["conv_b"] + c + 1]
                        ins = dve.tensor_scalar(c_acc[:, c, :], win, tap, bias, ALU.mult, ALU.add)
                    else:
                        dve.wait_ge(conv_step, prev + 1)
                        ins = dve.scalar_tensor_tensor(c_acc[:, c, :], win, tap, c_acc[:, c, :], ALU.mult, ALU.add)
                    ins.then_inc(conv_step, 1)
                    done[0] = m + 1

            lo(3)
            scaled_gate(0)
            lo(4)
            norm_split_lo(N_MEM, 0, mem_h, mem_l)
            norm_split_lo(N_MEM, 1, mem_h, mem_l)
            gate_conv(0)
            lo(5)
            lo(6)
            dve.wait_ge(pos_loaded, 16)
            dve.wait_ge(freq_ready, ROPE_HALF)
            after(dve.tensor_copy(pos_f[:, :], pos_i[:, :]))
            sin_a, cos_a = ang[:, 0, :, :], ang[:, 1, :, :]
            shape = [P, TB, ROPE_HALF]
            after(dve.tensor_tensor(sin_a, pos_f[:, :].unsqueeze(2).broadcast_to(shape), freq[:, :].unsqueeze(1).broadcast_to(shape), ALU.mult))
            after(dve.tensor_scalar(turns[:, :, :], sin_a, 1.0 / (2 * PI), ROUND, ALU.mult, ALU.add))
            after(dve.tensor_scalar(turns[:, :, :], turns[:, :, :], ROUND, None, ALU.subtract))
            for part in (TWO_PI_A, TWO_PI_B, TWO_PI_C):
                after(dve.scalar_tensor_tensor(sin_a, turns[:, :, :], -part, sin_a, ALU.mult, ALU.add))
            after(dve.tensor_scalar(sin_a, sin_a, SIN_MAX, -SIN_MAX, ALU.min, ALU.max))
            after(dve.scalar_tensor_tensor(cos_a, sin_a, -1.0, sin_a, ALU.mult, ALU.max))
            dve.tensor_scalar(cos_a, cos_a, -1.0, PI / 2, ALU.mult, ALU.add).then_inc(ang_ready, 1)
            dve.wait_ge(cols_ready, 3)
            both = cols_g[:, KD * R_MIX2:KD * (R_MIX2 + 1)]
            dve.tensor_tensor(both, both, cols_g[:, KD * C_F:KD * (C_F + 1)], ALU.mult).then_inc(gain_product, 1)

            scaled_gate(1)
            gate_conv(1)
            lo(7)
            dve.wait_ge(sincos_ready, 1)
            dve.wait_ge(qk_ready, 2)
            for tb in range(TB):
                view = qk[:, tb, :].rearrange("p (g e f) -> p g e f", e=2, f=ROPE_HALF)
                res = qkr[:, tb, :].rearrange("p (g e f) -> p g e f", e=2, f=ROPE_HALF)
                t = [rope_t[:, j, :].rearrange("p (g f) -> p g f", f=ROPE_HALF) for j in range(4)]
                sin, cos = (sincos[:, e, tb, :].unsqueeze(1).broadcast_to([P, 2 * RET_HEADS, ROPE_HALF]) for e in range(2))
                dve.tensor_tensor(t[0], view[:, :, 0, :], cos, ALU.mult)
                dve.tensor_tensor(t[1], view[:, :, 1, :], sin, ALU.mult)
                dve.tensor_tensor(t[2], view[:, :, 0, :], sin, ALU.mult)
                after(dve.tensor_tensor(t[3], view[:, :, 1, :], cos, ALU.mult))
                dve.tensor_tensor(res[:, :, 0, :], t[0], t[1], ALU.subtract)
                after(dve.tensor_tensor(res[:, :, 1, :], t[2], t[3], ALU.add))
                dve.sem_inc(rope_ready, 1)
            lo(8)
            lo(9)
            dve.wait_ge(dist_ready, 1)
            after(dve.tensor_copy(dist[:, :], dist_i[:, :]))
            after(dve.scalar_tensor_tensor(dist[:, :], dist[:, :], -1.0, dist[:, :], ALU.mult, ALU.max))
            dve.memset(dist[CHUNK:P, 0:CHUNK], FAR).then_inc(dist_set, 1)
            conv(12)
            lo(10)
            lo(11)

            def ret_decay(hd):
                dve.wait_ge(ret_s, hd + 1)
                dve.wait_ge(dec_ready, hd + 1)
                if hd >= 2:
                    dve.wait_ge(ret_pv, hd - 1)
                sc = RET_DK ** -0.5
                dve.scalar_tensor_tensor(s_dec[:, hd % 2, 0:S], tok(hd % 4)[:, 0:S], sc, dec[:, hd, :], ALU.mult, ALU.mult)
                after(dve.scalar_tensor_tensor(s_dec[:, hd % 2, S:S + P], tok(hd % 4)[:, S:S + P], sc, dec[:, hd, 0:P], ALU.mult, ALU.mult))
                dve.sem_inc(s_dec_ready, 1)

            def scaled_gate_ret(j):
                dve.wait_ge(slab_used, I_RG + j + 1)
                dve.tensor_tensor(rgs[:, 2 * j:2 * j + 2, :], blocks(feat(j)), row_of_scales(0), ALU.mult).then_inc(rg_in, 1)

            ret_decay(0)
            ret_decay(1)
            scaled_gate_ret(0)
            conv(8)
            lo(12)
            scaled_gate_ret(1)
            for j in range(1, 4):
                ret_decay(2 * j)
                ret_decay(2 * j + 1)
                conv(7)
                lo(12 + j)
            dve.wait_ge(ret_pv, RET_HEADS)
            heads = [feat(2 + tb).rearrange("p (g e) -> p g e", e=RET_DV) for tb in range(TB)]
            H8 = [slice(RET_HEADS * tb, RET_HEADS * (tb + 1)) for tb in range(TB)]
            dve.tensor_reduce(r_mean[:, H8[0]], heads[0], AX_X, ALU.add)
            after(dve.tensor_reduce(r_mean[:, H8[1]], heads[1], AX_X, ALU.add))
            after(dve.tensor_scalar(r_mean, r_mean, -1.0 / RET_DV, None, ALU.mult))
            for tb in range(TB):
                after(dve.tensor_tensor(ry[:, tb, :].rearrange("p (g e) -> p g e", e=RET_DV), heads[tb],
                                        r_mean[:, H8[tb]].unsqueeze(2).broadcast_to([P, RET_HEADS, RET_DV]), ALU.add))
            dve.sem_inc(ry_centred, 1)
            conv(4)
            lo(16)
            dve.wait_ge(ry_squared, 1)
            all_heads = [x[:, :, :].rearrange("p t (g e) -> p (t g) e", e=RET_DV) for x in (ry, ry_sq)]
            after(dve.tensor_reduce(r_var, all_heads[1], AX_X, ALU.add))
            after(dve.tensor_scalar(r_var, r_var, 1.0 / RET_DV, EPS, ALU.mult, ALU.add))
            rsqrt(r_var, r_y, r_t)
            dve.tensor_tensor(all_heads[0], all_heads[0], r_y.unsqueeze(2).broadcast_to([P, 2 * RET_HEADS, RET_DV]), ALU.mult).then_inc(ry_ready, 1)
            conv(6)
            lo(17)
            conv(6)
            lo(18)
            dve.wait_ge(ry_t, 1)
            for f in range(4):
                w = cols_a[:, ROW_OF["ret_gn_w"] + f:ROW_OF["ret_gn_w"] + f + 1]
                ins = dve.scalar_tensor_tensor(retT[:, f, :], feat(2 * (f // 2))[:, (f % 2) * S:(f % 2 + 1) * S], w, rgs[:, f, :], ALU.mult, ALU.mult)
            ins.then_inc(ret_ready, 1)
            dve.wait_ge(ret_hi, 1)
            dve.tensor_tensor(xl[:, 4:8, :], retT[:, :, :], xh[:, 4:8, :].bitcast(F32), ALU.subtract).then_inc(ret_lo, 1)
            conv(len(order))
            dve.wait_ge(conv_last, len(POOL_TAPS))
            dve.wait_ge(conv_step, len(order))
            dve.tensor_tensor(c_acc[:, 1, :], c_acc[:, 1, :], c_rest[:, :], ALU.add).then_inc(conv_step, 1)
            lo(19)
            for tb in range(TB):
                t = slice(tb * P, (tb + 1) * P)
                dve.wait_ge(conv_mean, tb + 1)
                dve.scalar_tensor_tensor(c_acc[:, :, t], feat(3 - 2 * tb)[:, 0:P].unsqueeze(1).broadcast_to([P, 4, P]), -1.0 / HALF,
                                         c_acc[:, :, t], ALU.mult, ALU.add).then_inc(conv_centred, 1)
            lo(20)

            def conv_rsqrt(tb):
                t = slice(tb * P, (tb + 1) * P)
                dve.wait_ge(conv_var, tb + 1)
                after(dve.tensor_scalar(n_v[:, t], feat(2 * tb)[:, 0:P], 1.0 / HALF, EPS, ALU.mult, ALU.add))
                rsqrt(n_v[:, t], n_y[:, t], n_t[:, t])

            def conv_norm(tb):
                t = slice(tb * P, (tb + 1) * P)
                dve.wait_ge(conv_centred, tb + 1)
                dve.tensor_tensor(c_acc[:, :, t], c_acc[:, :, t], n_y[:, t].unsqueeze(1).broadcast_to([P, 4, P]), ALU.mult).then_inc(conv_normed, 1)

            def conv_rest(tb):
                t = slice(tb * P, (tb + 1) * P)
                dve.wait_ge(conv_hi, tb + 1)
                dve.tensor_tensor(xl[:, 0:4, t], c_out[:, :, t], xh[:, 0:4, t].bitcast(F32), ALU.subtract).then_inc(conv_lo, 1)

            conv_rsqrt(0)
            conv_norm(0)
            conv_rsqrt(1)
            conv_rest(0)
            conv_norm(1)
            lo(21)
            conv_rest(1)
            boundary(R_XA, UPD[I_OUT1], I_OUT1 + 3, Q_XA, r_xa, I_Q1)
            after(dve.tensor_scalar(r_xa, r_xa, XA_SCALE, None, ALU.mult))

            def x_attention(b, i_o):
                def maxima(hd):
                    for u in range(TB * hd, TB * hd + TB):
                        dve.wait_ge(xs_ready, 8 * b + u + 1)
                        after(dve.tensor_reduce(xmax[:, u:u + 1], tok(u % 4)[:, 0:NMEM], AX_X, ALU.max))
                        dve.tensor_scalar(xneg[:, u:u + 1], xmax[:, u:u + 1], r_xa[:, u % TB:u % TB + 1], -1.0, ALU.mult, ALU.mult).then_inc(xmax_ready, 1)

                def normalise(hd):
                    for u in range(TB * hd, TB * hd + TB):
                        dve.wait_ge(xexp_ready, 8 * b + u + 1)
                        after(dve.reciprocal(xinv[:, u:u + 1], xsum[:, u:u + 1]))
                        dve.tensor_scalar(prob[:, u % 4, :], prob[:, u % 4, :], xinv[:, u:u + 1], None, ALU.mult).then_inc(xp_ready, 1)

                def out_lo(hd):
                    dve.wait_ge(xo_hi, 4 * b + hd + 1)
                    f = slice(2 * hd, 2 * hd + 2)
                    dve.tensor_tensor(xl[:, f, :], blocks(feat(hd)), xh[:, f, :].bitcast(F32), ALU.subtract).then_inc(xo_lo, 1)

                def q_lo(j):
                    dve.wait_ge(xq_hi, 4 * b + j + 1)
                    f = slice(2 * j, 2 * j + 2)
                    dve.tensor_tensor(q_l[:, f, :], blocks(feat(j)), q_h[:, f, :].bitcast(F32), ALU.subtract).then_inc(xq_ready, 1)

                def p_lo(hd):
                    dve.wait_ge(xp_hi, 4 * b + hd + 1)
                    dve.tensor_tensor(probT_l[:, hd % 2, :, :], blocks(feat(hd)), probT_h[:, hd % 2, :, :].bitcast(F32), ALU.subtract).then_inc(xpT_ready, 1)

                q_lo(0)
                if b == 0:
                    lo(I_Q1 + 3)
                lo(i_o)
                q_lo(1)
                lo(i_o + 1)
                maxima(0)
                normalise(0)
                q_lo(2)
                p_lo(0)
                lo(i_o + 2)
                maxima(1)
                normalise(1)
                q_lo(3)
                maxima(2)
                p_lo(1)
                maxima(3)
                normalise(2)
                out_lo(0)
                normalise(3)
                out_lo(1)
                p_lo(2)
                lo(i_o + 3)
                p_lo(3)
                out_lo(2)
                out_lo(3)

            x_attention(0, I_O1)
            boundary(R_MLP, UPD[I_O1], I_O1 + 3, Q_MLP, r_mlp, I_FF1)
            after(dve.tensor_tensor(r_mlp, r_mlp, r_mlp, ALU.mult))

            def mlp1(g, first=False, splits=True):
                step = 0 if first else 4 * g
                two = 0 if first else 2 * g
                for c in range(2):
                    dve.wait_ge(relu_ready, two + c + 1)
                    dve.tensor_tensor(ff_u[:, c, :], ff_r[:, c, :], ff_r[:, c, :], ALU.mult).then_inc(relu_sq, 1)
                    dve.wait_ge(relu_sq, two + c + 1)
                    dve.wait_ge(ff_hi, two + c + 1)
                    f = slice(2 * c, 2 * c + 2)
                    dve.tensor_tensor(ff_l[:, f, :], blocks(ff_u[:, c, :]), ff_h[:, f, :].bitcast(F32), ALU.subtract).then_inc(ff_lo, 1)
                    if splits:
                        lo(I_FF1 + 4 + c, step)
                if splits:
                    for c in range(2, 4):
                        lo(I_FF1 + 4 + c, step)

            mlp1(0, first=True)
            with dve.Fori(1, G1 - 1) as g:
                mlp1(g)
            mlp1(G1 - 1, splits=False)
            _, update_block = update(UPD[I_FF1], I_SBQK - 1, r_mlp)
            lo(I_SBQK)
            lo(I_SBQK + 1)
            dve.wait_ge(gain_product, 1)
            for tb in range(TB):
                update_block(tb)
                raw_split_lo(R_MIX2, tb)
            dve.wait_ge(gain_loaded, 16 * (G_F + 1))
            dve.wait_ge(h_updated, 6 * UPD[I_FF1] + 6)
            for tb in range(TB):
                dve.tensor_tensor(xn[:, tb, :], h[:, tb, :], gain[:, :], ALU.mult).then_inc(hg_ready, 1)
            dve.wait_ge(hg_ready, TB)
            dve.sem_inc(gain_used, 1)
            token_scales(Q_F, r_f)
            lo(I_SBQK + 2)
            dve.wait_ge(norm_sq, 2 * Q_MIX2 + 2)
            after(dve.tensor_tensor(nv, r_f, r_f, ALU.mult))
            after(dve.tensor_tensor(nv, nv, sq_sum[:, 2 * Q_MIX2:2 * Q_MIX2 + 2], ALU.mult))
            after(dve.tensor_scalar(nv, nv, 1.0 / D, EPS, ALU.mult, ALU.add))
            rsqrt(nv, r_mix2, nt)
            after(dve.tensor_tensor(r_mix2, r_mix2, r_f, ALU.mult))
            scales_on_diagonal(r_mix2)
            lo(I_SBQK + 3)
            for j in range(4):
                lo(I_SBQK + 4 + j)
                if j == 0:
                    dve.wait_ge(row_ready, 2)
                dve.wait_ge(slab_used, I_SBQK + j + 1)
                dve.scalar_tensor_tensor(qkT2[:, 2 * j:2 * j + 2, :], blocks(feat(j)), SB_DIM ** -0.5 if j < 2 else 1.0, row_of_scales(0),
                                         ALU.mult, ALU.mult).then_inc(sbqk_ready, 1)
            for tb in range(TB):
                dve.tensor_scalar(h[:, tb, :], xn[:, tb, :], r_f[:, tb:tb + 1], None, ALU.mult).then_inc(h_scaled, 1)
            dve.tensor_tensor(r_row[:, 1, :], r_row[:, 0, :], r_row[:, 0, :], ALU.mult).then_inc(h_scaled, 1)
            lo(I_ZV)
            lo(I_ZV + 1)
            for j in range(2):
                dve.wait_ge(slab_used, I_ZU + j + 1)
                dve.tensor_tensor(ug[:, 2 * j:2 * j + 2, :], blocks(feat(j)), row_of_scales(0), ALU.mult).then_inc(ug_in, 1)
                lo(I_ZV + 2 + j)

            def sb_mask(x):
                v = x[:, :, :].rearrange("p e (b t) -> p e b t", t=P)[:, :, 0:3:2, :]
                m = earlier[:, :].unsqueeze(1).unsqueeze(1).broadcast_to([P, 2, 2, P])
                return dve.tensor_tensor(v, v, m, ALU.mult)

            z = ps[:, 0:2, 0:SB_COLS]

            def sb_penalty(p):
                dve.wait_ge(sb_log, p + 1)
                dve.wait_ge(const_ready, 4)
                if p > 0:
                    dve.wait_ge(sb_cum, p)
                after(dve.scalar_tensor_tensor(sb_m[:, :, :], z, 0.0, sb_l[:, :, :], ALU.max, ALU.add))
                after(sb_mask(sb_m))
                dve.sem_inc(sb_pen, 1)
                dve.scalar_tensor_tensor(sb_e[:, :, :], z, 0.0, sb_l[:, :, :], ALU.min, ALU.subtract).then_inc(sb_z_read, 1)

            def sb_argument(p):
                dve.wait_ge(sb_cum, p + 1)
                dve.wait_ge(sb_z_read, p + 1)
                dve.tensor_tensor(sb_e[:, :, :], sb_e[:, :, :], ps[:, 2:4, 0:SB_COLS], ALU.subtract).then_inc(sb_arg, 1)

            def sb_masked(p):
                dve.wait_ge(sb_exp, p + 1)
                sb_mask(sb_a).then_inc(sb_prob, 1)

            def sb_split(p):
                dve.wait_ge(sb_hi, p + 1)
                dve.tensor_tensor(y_l[0][:, p, :], tok(2)[:, 0:S], y_h[0][:, p, :].bitcast(F32), ALU.subtract).then_inc(sb_lo, 1)

            SB_AT, SB_EARLY = {}, {}

            def at_slab(i, step, p, table=SB_AT):
                table.setdefault(i, []).append((step, p))

            for p in range(4):
                if p != 2:
                    at_slab(SB_START + 4 * p + 1, sb_penalty, p, SB_EARLY)
                if p != 1:
                    at_slab(SB_START + 4 * p + 3, sb_argument, p)
                    at_slab(SB_START + 4 * p + 5, sb_masked, p, SB_EARLY)
                at_slab(SB_START + 4 * p + (5 if p == 1 else 6), sb_split, p, SB_EARLY)

            def early(i):
                for step, p in SB_EARLY.get(i, ()):
                    step(p)

            def beside(i):
                for step, p in SB_AT.get(i, ()):
                    step(p)

            dve.wait_ge(sgu_loaded, 48)
            for tb in range(TB):
                dve.wait_ge(vg_ready, tb + 1)
                six, two = bn6[:, 6 * tb:6 * tb + 6], bn2[:, 2 * tb:2 * tb + 2]
                v, y, t = nv[:, tb:tb + 1], ny[:, tb:tb + 1], nt[:, tb:tb + 1]
                after(dve.bn_stats(six, vg[:, tb, :]))
                after(dve.bn_aggr(two, six))
                after(dve.tensor_scalar(v, two[:, 1:2], LN_EPS, None, ALU.add))
                rsqrt(v, y, t)
                after(dve.tensor_scalar(vg[:, tb, :], vg[:, tb, :], two[:, 0:1], y, ALU.subtract, ALU.mult))
                after(dve.tensor_tensor(vg[:, tb, :], vg[:, tb, :], ln_g[:, :], ALU.mult))
                dve.tensor_tensor(vg[:, tb, :], vg[:, tb, :], ln_b[:, :], ALU.add).then_inc(vn_ready, 1)
                lo(I_ZV + 4 + tb)
            tap3 = ROW_OF["conv_w_2"]
            for j in range(2):
                early(I_C3 + 2 * j)
                lo(I_C3 + 2 * j + 4)
                beside(I_C3 + 2 * j)
                dve.wait_ge(slab_used, I_C3 + 2 * j + 1)
                dve.wait_ge(h_scaled, TB + 1)
                if j:
                    dve.wait_ge(y3_ready, 1)
                after(dve.tensor_tensor(cc_s[:, :, :], blocks(feat(2 - 2 * j)), row_of_scales(1), ALU.mult))
                dve.wait_ge(pad3_ready, 1)
                dve.wait_ge(slab_used, I_C3 + 2 * j + 2)
                dve.tensor_tensor(y3_pad[:, 2 * j:2 * j + 2, CONV3 - 1:], blocks(feat(3 - 2 * j)), cc_s[:, :, :], ALU.mult).then_inc(y3_ready, 1)
                early(I_C3 + 2 * j + 1)
                lo(I_C3 + 2 * j + 5)
                beside(I_C3 + 2 * j + 1)
            early(I_C3 + 4)
            dve.wait_ge(sgu_mixed, 1)
            dve.wait_ge(ug_ready, 2)
            for j in range(2):
                g = slice(2 * j, 2 * j + 2)
                mixed = feat(j).rearrange("p (g b t) -> p g b t", g=2, t=P)
                after(dve.tensor_tensor(vg[:, j, :].rearrange("p (g b t) -> p g b t", g=2, t=P), mixed,
                                        b_sp[:, g, :].unsqueeze(2).broadcast_to([P, 2, TB, P]), ALU.add))
                dve.tensor_tensor(ug[:, g, :], blocks(vg[:, j, :]), ug[:, g, :], ALU.mult).then_inc(yb_ready, 1)
            dve.wait_ge(y3_ready, 2)
            for k in range(CONV3):
                for c in range(4):
                    tap, win = cols_a[:, tap3 + 4 * k + c:tap3 + 4 * k + c + 1], y3_pad[:, c, k:k + S]
                    if k == 0:
                        ins = dve.tensor_scalar(acc3[:, c, :], win, tap, None, ALU.mult)
                    else:
                        ins = dve.scalar_tensor_tensor(acc3[:, c, :], win, tap, acc3[:, c, :], ALU.mult, ALU.add)
                    if c == 3:
                        after(ins)
                if k == 0:
                    early(I_C3 + 5)
            after(dve.tensor_tensor(acc3[:, :, :], acc3[:, :, :], r_row[:, 0, :].unsqueeze(1).broadcast_to([P, 4, S]), ALU.mult))
            for j in range(2):
                lo(I_C3 + 8 + j)
                beside(I_C3 + 4 + j)
                dve.wait_ge(slab_used, I_C3 + 5 + j)
                dve.tensor_tensor(acc3[:, 2 * j:2 * j + 2, :], blocks(feat(2 + j)), acc3[:, 2 * j:2 * j + 2, :], ALU.mult).then_inc(yc_ready, 1)
            dve.wait_ge(yb_hi, 1)
            dve.tensor_tensor(y_l[1][:, :, :], ug[:, :, :], y_h[1][:, :, :].bitcast(F32), ALU.subtract).then_inc(yb_lo, 1)
            sb_argument(1)
            dve.wait_ge(yc_hi, 1)
            dve.tensor_tensor(y_l[2][:, :, :], acc3[:, :, :], y_h[2][:, :, :].bitcast(F32), ALU.subtract).then_inc(yc_lo, 1)

            def merged_split(half):
                dve.wait_ge(merged_hi, half + 1)
                f = slice(4 * half, 4 * half + 4)
                dve.tensor_tensor(xl[:, f, :], merged[:, f, :], xh[:, f, :].bitcast(F32), ALU.subtract).then_inc(merged_lo, 1)

            for n in range(BRANCHES):
                for half in range(2):
                    i = I_BR + 6 * n + 3 * half
                    r = 2 * n + half
                    for j in range(2):
                        dve.wait_ge(slab_used, i + j + 1)
                        dve.tensor_tensor(sig2[:, 2 * j:2 * j + 2, :], blocks(feat(j)), row_of_scales(0), ALU.mult).then_inc(gate_in, 1)
                        if 0 < r < 5:
                            early(i + j)
                            lo(i + j + 4)
                            beside(i + j)
                    if r == 0:
                        sb_masked(1)
                        lo(i + 4)
                        lo(i + 5)
                        sb_penalty(2)
                    if r == 5:
                        merged_split(0)
                        lo(i + 4)
                        lo(i + 5)
                    dve.wait_ge(gate_ready, 2 * r + 2)
                    dve.wait_ge(slab_used, i + 3)
                    m = merged[:, 4 * half:4 * half + 4, :]
                    if n == 0:
                        for j in range(2):
                            ins = dve.tensor_tensor(m[:, 2 * j:2 * j + 2, :], blocks(feat(2 + j)), sig2[:, 2 * j:2 * j + 2, :], ALU.mult)
                            after(ins)
                    else:
                        for j in range(2):
                            s2 = sig2[:, 2 * j:2 * j + 2, :]
                            after(dve.tensor_tensor(s2, blocks(feat(2 + j)), s2, ALU.mult))
                        after(dve.tensor_tensor(m, m, sig2[:, :, :], ALU.add))
                    dve.sem_inc(merge_done, 1)
                    early(i + 2)
                    if r < 5:
                        lo(i + 6)
                    if r == 4:
                        token_scales(Q_MEM2, r_mem)
                    beside(i + 2)
            merged_split(1)
            memory_rows(N_MEM2, mem2_tok, G_MEM2, r_mem)
            lo(I_OUT2 + 3)
            norm_split_lo(N_MEM2, 0, mem2_h, mem2_l, feat)
            norm_split_lo(N_MEM2, 1, mem2_h, mem2_l, feat)
            _, update_block = update(UPD[I_OUT2], I_OUT2 + 3)
            lo(I_K2)
            lo(I_K2 + 1)
            update_block(0)
            raw_split_lo(R_XA2, 0)
            update_block(1)
            lo(I_K2 + 2)
            lo(I_K2 + 3)
            raw_split_lo(R_XA2, 1)
            lo(I_K2 + 4)
            token_scales(Q_XA2, r_xa)
            after(dve.tensor_scalar(r_xa, r_xa, XA_SCALE, None, ALU.mult))

            def k_lo(j):
                dve.wait_ge(k_ready, 4 + j + 1)
                f = slice(2 * j, 2 * j + 2)
                dve.tensor_tensor(k_split[1][1][:, f, :], blocks(feat(j)), k_split[1][0][:, f, :].bitcast(F32), ALU.subtract).then_inc(k2_lo, 1)

            k_lo(0)
            for j in range(1, 4):
                k_lo(j)
                lo(I_K2 + 4 + j)
            for j in range(4):
                lo(I_Q2 + j)
            for m in range(2):
                for half in range(2):
                    dve.wait_ge(v_ready, 4 + 2 * m + half + 1)
                    c = slice(half * HALF, (half + 1) * HALF)
                    dve.tensor_tensor(v_split[1][1][:, m, c], tok(2 * m + half), v_split[1][0][:, m, c].bitcast(F32), ALU.subtract).then_inc(v2_lo, 1)
            x_attention(1, I_O2)
            boundary(R_FF2, UPD[I_O2], I_O2 + 3, Q_FF2, r_ff2, I_FF2)
            scales_on_diagonal(r_ff2)

            def glu(g, i, first=False, last=False, step=0):
                nxt = ff2_gate(1) if first else i + 3
                dve.wait_ge(slab_used, i + 1 + step)
                if first:
                    dve.wait_ge(row_ready, 3)
                dve.tensor_tensor(blocks(ff_u[:, 1, :]), blocks(feat(2 if first else 0)), row_of_scales(0), ALU.mult).then_inc(glu_in_ready, 1)
                if last:
                    lo(N_SLABS - 1)
                elif not first:
                    lo(nxt, step)
                dve.wait_ge(silu_ready, g + 1)
                dve.wait_ge(slab_used, i + 2 + step)
                if not first:
                    dve.wait_ge(glu_lo, g)
                dve.tensor_tensor(ff_u[:, 0, :], feat(3 if first else 1), ff_r[:, 0, :], ALU.mult).then_inc(glu_ready, 1)
                if not first and not last:
                    lo(nxt + 1, step)
                dve.wait_ge(glu_hi, g + 1)
                f = slice(2, 4) if last else slice(0, 2)
                dve.tensor_tensor(ff_l[:, f, :], blocks(ff_u[:, 0, :]), ff_h[:, f, :].bitcast(F32), ALU.subtract).then_inc(glu_lo, 1)
                if not last:
                    lo(nxt + 2, step)

            glu(0, I_FF2, first=True)
            glu(1, ff2_gate(1))
            glu(2, ff2_gate(2))
            with dve.Fori(0, G2 - 4) as t:
                glu(t + 3, ff2_gate(3), step=3 * t)
            glu(G2 - 1, ff2_gate(G2 - 1), last=True)
            add, _ = update(UPD[I_FF2], N_SLABS - 1, r_ff2)
            dve.wait_ge(gain_loaded, 16 * (G_FINAL + 1))
            for tb in range(TB):
                for half in range(2):
                    add(tb, half, 2)
                for half in range(2 - tb):
                    c = slice(half * HALF, (half + 1) * HALF)
                    dve.wait_ge(h_updated, 6 * UPD[I_FF2] + 2 * tb + half + 1)
                    after(dve.tensor_tensor(xn[:, tb, c], h[:, tb, c], gain[:, c], ALU.mult))
                dve.wait_ge(last_sq, 2 * tb + 2)
                v, y, t = nv[:, tb:tb + 1], ny[:, tb:tb + 1], nt[:, tb:tb + 1]
                after(dve.tensor_tensor(v, sq_last[:, 2 * tb:2 * tb + 1], sq_last[:, 2 * tb + 1:2 * tb + 2], ALU.add))
                after(dve.tensor_scalar(v, v, 1.0 / D, EPS, ALU.mult, ALU.add))
                rsqrt(v, y, t)
                dve.sem_inc(y_ready, 1)
                dve.tensor_scalar(xn[:, tb, 0:HALF], xn[:, tb, 0:HALF], y, None, ALU.mult).then_inc(out_lead, 1)


def kernel(**inputs):
    import concourse.bacc as bacc
    from concourse.bass_utils import run_bass_kernel_spmd

    nc = bacc.Bacc("TRN2", target_bir_lowering=False, num_devices=1)
    arrays, aps = {}, {}
    for name in INPUTS:
        x = np.ascontiguousarray(inputs[name])
        arrays[f"in_{name}"] = x
        aps[name] = nc.dram_tensor(f"in_{name}", x.shape, mybir.dt.from_np(x.dtype), kind="ExternalInput").ap()
    out = nc.dram_tensor("out", (1, S, D), F32, kind="ExternalOutput").ap()
    build(nc, aps, out)
    r = run_bass_kernel_spmd(nc, [arrays], core_ids=[0])
    return r.results[0]["out"]
```
